# Optimizing a Trainium2 kernel written in Bass

```python
import math
import jax, jax.numpy as jnp
from jax import lax
import numpy as np

D_MODEL = 1024
BATCH = 1
SEQ = 128
DEPTH = 2
DEC_BATCH = 1
DEC_SEQ = 512
PAST_LEN = 128

GRID_W = 64
ATT_HEADS = 8
ATT_QK_DIM = 64
ATT_V_DIM = 2 * ATT_QK_DIM
ATT_QK_WIDTH = ATT_HEADS * 2 * ATT_QK_DIM
ATT_WIDTH = ATT_HEADS * ATT_V_DIM
ROPE_BASE = 10000.0
ROPE_AXIS_DIM = ATT_QK_DIM // 2
Q_BLOCK = 128
CONV_WIDTH = D_MODEL
CONV_K = 3
REC_HEADS = 8
REC_DK = 128
REC_DV = D_MODEL // REC_HEADS
REC_KW = REC_HEADS * REC_DK
REC_WIDTH = REC_HEADS * REC_DV
REC_CHUNK = 32
N_BRANCH = 3
PEER_HEADS = 8
PEER_N_KEYS = 128
PEER_N_EXPERTS = PEER_N_KEYS * PEER_N_KEYS
PEER_KEY_DIM = 256
PEER_HALF = PEER_KEY_DIM // 2
PEER_TOPK = 16
PEER_BLOCK = 128
LN_EPS = 1e-5
DEEPNORM_ALPHA = (2 * DEPTH) ** 0.25
DEEPNORM_BETA = (8 * DEPTH) ** -0.25

IN_SIZES = (ATT_QK_WIDTH, ATT_QK_WIDTH, ATT_WIDTH,
            CONV_WIDTH, CONV_WIDTH, CONV_WIDTH,
            REC_KW, REC_KW, REC_KW, REC_WIDTH, REC_WIDTH,
            N_BRANCH * D_MODEL)
W_IN_COLS = sum(IN_SIZES)

kernel_name = 'hybrid_diffusion_trunk_step'

def layer_norm(x, g, b):
    xf = x.astype(jnp.float32)
    mu = jnp.mean(xf, axis=-1, keepdims=True)
    var = jnp.mean(jnp.square(xf - mu), axis=-1, keepdims=True)
    return ((xf - mu) * lax.rsqrt(var + LN_EPS) * g.astype(jnp.float32) + b.astype(jnp.float32)).astype(x.dtype)

def rms_norm(x, g):
    xf = x.astype(jnp.float32)
    y = xf * lax.rsqrt(jnp.mean(jnp.square(xf), axis=-1, keepdims=True) + LN_EPS)
    return (y * g.astype(jnp.float32)).astype(x.dtype)

def split_cols(z):
    outs, start = [], 0
    for n in IN_SIZES:
        outs.append(z[..., start:start + n])
        start += n
    return outs

def rope_axial(x):
    T = x.shape[1]
    n_rows = T // GRID_W
    rows = jnp.repeat(jnp.arange(n_rows), GRID_W)
    cols = jnp.tile(jnp.arange(GRID_W), n_rows)
    freqs = ROPE_BASE ** (-jnp.arange(0, ROPE_AXIS_DIM, 2, dtype=jnp.float32) / ROPE_AXIS_DIM)

    def rot(xa, pos):
        ang = pos.astype(jnp.float32)[:, None] * freqs[None, :]
        cos, sin = jnp.cos(ang)[None, :, None, :], jnp.sin(ang)[None, :, None, :]
        xa = xa.astype(jnp.float32)
        x1, x2 = xa[..., :ROPE_AXIS_DIM // 2], xa[..., ROPE_AXIS_DIM // 2:]
        return jnp.concatenate([x1 * cos - x2 * sin, x1 * sin + x2 * cos], axis=-1)

    out = jnp.concatenate([rot(x[..., :ROPE_AXIS_DIM], rows), rot(x[..., ROPE_AXIS_DIM:], cols)], axis=-1)
    return out.astype(x.dtype)

def diff_attention(q1, q2, k1, k2, v, lam):
    B, T, H, dq = q1.shape
    nb = T // Q_BLOCK
    scale = dq ** -0.5

    def blocks(a):
        return a.reshape(B, nb, Q_BLOCK, H, dq).transpose(1, 0, 2, 3, 4)

    def one(qs):
        a1, a2 = qs
        s1 = jnp.einsum('bqhd,bkhd->bhqk', a1, k1).astype(jnp.float32) * scale
        s2 = jnp.einsum('bqhd,bkhd->bhqk', a2, k2).astype(jnp.float32) * scale
        pmap = jax.nn.softmax(s1, axis=-1) - lam * jax.nn.softmax(s2, axis=-1)
        return jnp.einsum('bhqk,bkhv->bqhv', pmap.astype(v.dtype), v)

    o = lax.map(one, (blocks(q1), blocks(q2)))
    return o.transpose(1, 0, 2, 3, 4).reshape(B, T, H, v.shape[-1])

def short_conv(u, w, b):
    up = jnp.pad(u, ((0, 0), (1, 1), (0, 0)))
    return up[:, :-2] * w[0] + up[:, 1:-1] * w[1] + up[:, 2:] * w[2] + b

def forget_log(fx, lb, shape):
    f = lb + (1.0 - lb) * jax.nn.sigmoid(fx.astype(jnp.float32))
    return jnp.log(f).reshape(shape)

def hgrn2_scan(q, logf, inp, s0):
    B, T, H, DK = q.shape
    DV = inp.shape[-1]
    n = T // REC_CHUNK

    def chunks(a):
        return a.astype(jnp.float32).reshape(B, n, REC_CHUNK, H, a.shape[-1]).transpose(1, 0, 3, 2, 4)

    k = -jnp.expm1(logf)
    mask = jnp.tril(jnp.ones((REC_CHUNK, REC_CHUNK), dtype=bool))

    def step(S, xs):
        qc, lc, kc, ic = xs
        b = jnp.cumsum(lc, axis=2)
        rel = jnp.where(mask[:, :, None], b[:, :, :, None, :] - b[:, :, None, :, :], -jnp.inf)
        A = jnp.einsum('bhtk,bhtsk,bhsk->bhts', qc, jnp.exp(rel), kc)
        o = jnp.einsum('bhts,bhsv->bhtv', A, ic) + jnp.einsum('bhtk,bhkv->bhtv', qc * jnp.exp(b), S)
        bl = b[:, :, -1:, :]
        S = jnp.exp(bl[:, :, 0, :])[..., None] * S + jnp.einsum('bhsk,bhsv->bhkv', kc * jnp.exp(bl - b), ic)
        return S, o

    S, o = lax.scan(step, s0.astype(jnp.float32), (chunks(q), chunks(logf), chunks(k), chunks(inp)))
    o = o.transpose(1, 0, 3, 2, 4).reshape(B, T, H, DV)
    return o, S

def token_mixer(h, l, p, ctx):
    B, T, _ = h.shape
    zq, zk, zv, zb, zc, zx, rq, rff, rfb, ri, rg, zg = split_cols(h @ p['w_in'])
    q = zq.reshape(B, T, ATT_HEADS, 2, ATT_QK_DIM)
    q1, q2 = q[..., 0, :], q[..., 1, :]
    k = zk.reshape(B, T, ATT_HEADS, 2 * ATT_QK_DIM)
    v = zv.reshape(B, T, ATT_HEADS, ATT_V_DIM)
    lam_init = 0.8 - 0.6 * math.exp(-0.3 * l)
    lp = p['attn_lambda'].astype(jnp.float32)
    lam = jnp.exp(jnp.sum(lp[0] * lp[1])) - jnp.exp(jnp.sum(lp[2] * lp[3])) + lam_init
    q_r = jax.nn.silu(rq).reshape(B, T, REC_HEADS, REC_DK)
    i_r = ri.reshape(B, T, REC_HEADS, REC_DV)
    logf_f = forget_log(rff, p['lb'][0], (B, T, REC_HEADS, REC_DK))
    logf_b = forget_log(rfb, p['lb'][1], (B, T, REC_HEADS, REC_DK))
    if ctx is None:
        k1, k2, vals = k[..., :ATT_QK_DIM], k[..., ATT_QK_DIM:], v
        s0 = jnp.zeros((B, 2, REC_HEADS, REC_DK, REC_DV), jnp.float32)
    else:
        k_ctx, v_ctx, s_ctx = ctx
        k_ctx = k_ctx.astype(k.dtype)
        q1, q2 = rope_axial(q1), rope_axial(q2)
        k1 = jnp.concatenate([rope_axial(k[..., :ATT_QK_DIM]), k_ctx[..., :ATT_QK_DIM]], axis=1)
        k2 = jnp.concatenate([rope_axial(k[..., ATT_QK_DIM:]), k_ctx[..., ATT_QK_DIM:]], axis=1)
        vals = jnp.concatenate([v, v_ctx.astype(v.dtype)], axis=1)
        s0 = s_ctx
    o_att = diff_attention(q1, q2, k1, k2, vals, lam)
    o_att = (rms_norm(o_att, p['attn_subln']) * (1.0 - lam_init)).reshape(B, T, ATT_WIDTH).astype(h.dtype)
    o_conv = zb * short_conv(zc * zx, p['conv_w'], p['conv_b'])
    o_f, s_f = hgrn2_scan(q_r, logf_f, i_r, s0[:, 0])
    o_b, s_b = hgrn2_scan(q_r[:, ::-1], logf_b[:, ::-1], i_r[:, ::-1], s0[:, 1])
    g_r = jax.nn.silu(rg.reshape(B, T, REC_HEADS, REC_DV).astype(jnp.float32))
    o_rec = (rms_norm(o_f + o_b[:, ::-1], p['rec_norm']) * g_r).reshape(B, T, REC_WIDTH).astype(h.dtype)
    gates = jax.nn.sigmoid(zg.reshape(B, T, N_BRANCH, D_MODEL))
    wb = p['w_branch']
    merged = (gates[..., 0, :] * (o_att @ wb[0]) + gates[..., 1, :] * (o_conv @ wb[1])
              + gates[..., 2, :] * (o_rec @ wb[2]))
    out = merged @ p['w_out']
    new_ctx = (k, v, jnp.stack([s_f, s_b], axis=1)) if ctx is None else None
    return out, new_ctx

def peer(h, wq, keys, u_tab, v_tab):
    B, T, D = h.shape
    nb = (B * T) // PEER_BLOCK

    def one(xb):
        q = (xb @ wq).reshape(PEER_BLOCK, PEER_HEADS, 2, PEER_HALF)
        s = jnp.einsum('thpd,hpnd->thpn', q, keys).astype(jnp.float32)
        s_top, i_top = lax.top_k(s, PEER_TOPK)
        cand = s_top[:, :, 0, :, None] + s_top[:, :, 1, None, :]
        cand_idx = i_top[:, :, 0, :, None] * PEER_N_KEYS + i_top[:, :, 1, None, :]
        best, pos = lax.top_k(cand.reshape(PEER_BLOCK, PEER_HEADS, PEER_TOPK * PEER_TOPK), PEER_TOPK)
        idx = jnp.take_along_axis(cand_idx.reshape(PEER_BLOCK, PEER_HEADS, PEER_TOPK * PEER_TOPK), pos, axis=-1)
        g = jax.nn.softmax(best, axis=-1)
        ue = jnp.take(u_tab, idx, axis=0)
        ve = jnp.take(v_tab, idx, axis=0)
        act = jax.nn.gelu(jnp.einsum('td,thkd->thk', xb, ue).astype(jnp.float32), approximate=False)
        return jnp.einsum('thk,thkd->td', (g * act).astype(ve.dtype), ve)

    y = lax.map(one, h.reshape(nb, PEER_BLOCK, D))
    return y.reshape(B, T, D)

def trunk_layer(x, mod, l, p, ctx):
    sh_a, sc_a, g_a, sh_f, sc_f, g_f = jnp.split(mod.astype(x.dtype), 6, axis=-1)
    h = x * (1.0 + sc_a) + sh_a
    mix, new_ctx = token_mixer(h, l, p, ctx)
    x = layer_norm(DEEPNORM_ALPHA * x + g_a * mix, p['ln_g'][0], p['ln_b'][0])
    h = x * (1.0 + sc_f) + sh_f
    ff = peer(h, p['peer_wq'], p['peer_keys'], p['peer_u'], p['peer_v'])
    x = layer_norm(DEEPNORM_ALPHA * x + g_f * ff, p['ln_g'][1], p['ln_b'][1])
    return x, new_ctx

def setup_inputs(seed: int = 0) -> dict:
    key = jax.random.key(seed)
    ks = jax.random.split(key, 24)

    def nrm(k, shape, s):
        return jax.random.normal(k, shape, jnp.float32) * s

    d_inv = D_MODEL ** -0.5
    return {
        'x_prompt': nrm(ks[0], (BATCH, SEQ, D_MODEL), 1.0),
        'x_sample': nrm(ks[1], (DEC_BATCH, DEC_SEQ, D_MODEL), 1.0),
        'c': nrm(ks[2], (DEC_BATCH, D_MODEL), 1.0),
        'cache_attn_k': nrm(ks[3], (DEC_BATCH, DEPTH, PAST_LEN, ATT_HEADS, 2 * ATT_QK_DIM), 1.0),
        'cache_attn_v': nrm(ks[4], (DEC_BATCH, DEPTH, PAST_LEN, ATT_HEADS, ATT_V_DIM), 1.0),
        'state_hgrn': nrm(ks[5], (DEC_BATCH, DEPTH, 2, REC_HEADS, REC_DK, REC_DV), 0.3),
        'c_ctx': nrm(ks[6], (D_MODEL,), 1.0),
        'mod_w': nrm(ks[7], (DEPTH, D_MODEL, 6 * D_MODEL), 0.5 * d_inv),
        'mod_b': nrm(ks[8], (DEPTH, 6 * D_MODEL), 0.01),
        'w_in': nrm(ks[9], (DEPTH, D_MODEL, W_IN_COLS), d_inv),
        'attn_lambda': nrm(ks[10], (DEPTH, 4, ATT_QK_DIM), 0.1),
        'attn_subln': 1.0 + nrm(ks[11], (DEPTH, ATT_V_DIM), 0.02),
        'conv_w': nrm(ks[12], (DEPTH, CONV_K, CONV_WIDTH), 0.5),
        'conv_b': nrm(ks[13], (DEPTH, CONV_WIDTH), 0.01),
        'rec_lb': nrm(ks[14], (DEPTH, 2, REC_KW), 1.0),
        'rec_norm': 1.0 + nrm(ks[15], (DEPTH, REC_DV), 0.02),
        'w_branch': nrm(ks[16], (DEPTH, N_BRANCH, D_MODEL, D_MODEL), d_inv),
        'w_out': nrm(ks[17], (DEPTH, D_MODEL, D_MODEL), DEEPNORM_BETA * d_inv),
        'ln_g': 1.0 + nrm(ks[18], (DEPTH, 2, D_MODEL), 0.02),
        'ln_b': nrm(ks[19], (DEPTH, 2, D_MODEL), 0.01),
        'peer_wq': nrm(ks[20], (DEPTH, D_MODEL, PEER_HEADS * PEER_KEY_DIM), d_inv),
        'peer_keys': nrm(ks[21], (DEPTH, PEER_HEADS, 2, PEER_N_KEYS, PEER_HALF), PEER_HALF ** -0.5),
        'peer_u': nrm(ks[22], (DEPTH, PEER_N_EXPERTS, D_MODEL), d_inv),
        'peer_v': nrm(ks[23], (DEPTH, PEER_N_EXPERTS, D_MODEL), DEEPNORM_BETA),
    }

def reference(x_prompt, x_sample, c, cache_attn_k, cache_attn_v, state_hgrn, c_ctx,
              mod_w, mod_b, w_in, attn_lambda, attn_subln, conv_w, conv_b, rec_lb, rec_norm,
              w_branch, w_out, ln_g, ln_b, peer_wq, peer_keys, peer_u, peer_v):
    lb_all = jnp.cumsum(jax.nn.softmax(rec_lb.astype(jnp.float32), axis=0), axis=0)
    lb_all = lb_all - lb_all[:1]
    y_p, y_s = x_prompt, x_sample
    ks, vs, ss = [], [], []
    for l in range(DEPTH):
        p = {'w_in': w_in[l], 'attn_lambda': attn_lambda[l], 'attn_subln': attn_subln[l],
             'conv_w': conv_w[l], 'conv_b': conv_b[l], 'lb': lb_all[l], 'rec_norm': rec_norm[l],
             'w_branch': w_branch[l], 'w_out': w_out[l], 'ln_g': ln_g[l], 'ln_b': ln_b[l],
             'peer_wq': peer_wq[l], 'peer_keys': peer_keys[l], 'peer_u': peer_u[l], 'peer_v': peer_v[l]}
        m_ctx = (jax.nn.silu(c_ctx) @ mod_w[l] + mod_b[l])[None, None, :]
        y_p, (k_l, v_l, s_l) = trunk_layer(y_p, m_ctx, l, p, None)
        ks.append(k_l)
        vs.append(v_l)
        ss.append(s_l)
        m_lat = (jax.nn.silu(c) @ mod_w[l] + mod_b[l])[:, None, :]
        y_s, _ = trunk_layer(y_s, m_lat, l, p, (cache_attn_k[:, l], cache_attn_v[:, l], state_hgrn[:, l]))
    new_cache_attn_k = jnp.stack(ks, axis=1)
    new_cache_attn_v = jnp.stack(vs, axis=1)
    new_state_hgrn = jnp.stack(ss, axis=1)
    return (y_p, y_s, new_cache_attn_k, new_cache_attn_v, new_state_hgrn)


_drawn_inputs = setup_inputs


def setup_inputs(seed=0):
    import zlib

    import numpy as np

    out = dict(_drawn_inputs(seed))
    spreads = {}
    factors = {'cache_attn_k': 4.561,
     'cache_attn_v': 4.187,
     'state_hgrn': 8.0,
     'mod_b': 3.001,
     'attn_lambda': 8.0,
     'attn_subln': 31.162,
     'conv_b': 39.366,
     'rec_norm': 36.265}
    for name, (base, spread) in spreads.items():
        noise = np.random.default_rng([zlib.crc32(name.encode()), seed]).standard_normal(out[name].shape)
        drawn = base * np.exp(spread * noise) if base else spread * noise
        out[name] = __import__('jax').numpy.asarray(drawn.astype(out[name].dtype))
    for name, factor in factors.items():
        out[name] = (out[name] * factor).astype(out[name].dtype)
    return out
```

```python
import math
from contextlib import ExitStack, contextmanager

import numpy as np
import concourse.bass as bass
from concourse import mybir

F32 = mybir.dt.float32
U32 = mybir.dt.uint32
ALU = mybir.AluOpType
ACT = mybir.ActivationFunctionType
AX = mybir.AxisListType

P = 128
D = 1024
KT = D // P
DEPTH = 2
LAT = 512
CTX = 128
TOK = LAT + CTX
NB = TOK // P
CHUNK = 512
HEADS = 8
QK = 64
SCALE = QK ** -0.5
LEVELS = 7
EXPERTS = 128 * 128
PH = 8
TOPK = 16
EPS = 1e-5
ALPHA = (2 * DEPTH) ** 0.25
LOWEST = -3.0e38
TINY = 2.0 ** -63
GRID_W = 64
LAM_INIT = [0.8 - 0.6 * math.exp(-0.3 * l) for l in range(DEPTH)]
ZQ, ZK, ZV, ZB, ZC, ZX, RQ, RFF, RFB, RI, RG, ZG = 0, 2, 4, 6, 8, 10, 12, 14, 16, 18, 20, 22


class Steps:

    def __init__(self, eng, sem, base=0):
        self.eng, self.sem, self.base, self.n = eng, sem, base, 0

    def mark(self, ins):
        self.n += 1
        ins.then_inc(self.sem, 1)
        return self.base + self.n

    def __call__(self, ins):
        self.eng.wait_ge(self.sem, self.mark(ins))


@contextmanager
def stage(nc, *names):
    with ExitStack() as ctx:
        sems = [ctx.enter_context(nc.semaphore(n)) for n in names]
        nums = sorted(s.num for s in sems)
        starts = [n for n in nums if n - 1 not in nums]
        ends = [n + 1 for n in nums if n + 1 not in nums]
        with nc.Block(no_gpsimd_drain=True) as block:
            yield block, sems
        for a, b in zip(starts, ends):
            nc.all_engine_barrier(sems_to_clear=range(a, b))


class Job:

    def __init__(self, weights, act_t, channel_major, engine, evac):
        self.weights, self.act_t, self.channel_major = weights, act_t, channel_major
        self.engine, self.evac = engine, evac
        self.tiles = CHUNK // P if channel_major else NB


def projections(nc, name, jobs, ring):
    tiles = [(c, m) for c, job in enumerate(jobs) for m in range(job.tiles)]
    done_through = [sum(j.tiles for j in jobs[:c + 1]) for c in range(len(jobs))]
    with ExitStack() as ctx:
        psum = [ctx.enter_context(nc.psum_tensor(f"{name}_ps{i}", [P, 1024], F32)) for i in range(4)]
        with stage(nc, f"{name}_w0", f"{name}_w1", f"{name}_tile", f"{name}_free0", f"{name}_free1",
                   f"{name}_free2", f"{name}_free3", f"{name}_dve", f"{name}_act") as (block, sems):
            w_loaded, tile_done, slot_free = sems[0:2], sems[2], sems[3:7]
            dve_steps, act_steps = sems[7], sems[8]

            @block.sync
            def _(sp):
                for c, job in enumerate(jobs):
                    if c >= 2:
                        sp.wait_ge(tile_done, done_through[c - 2])
                    sp.dma_start(ring[c % 2][:], job.weights).then_inc(w_loaded[c % 2], 16)

            @block.tensor
            def _(pe):
                for t, (c, m) in enumerate(tiles):
                    job, w, ps = jobs[c], ring[c % 2], psum[t % 4]
                    if m == 0:
                        pe.wait_ge(w_loaded[c % 2], 16 * (c // 2 + 1))
                    if t >= 4:
                        pe.wait_ge(slot_free[t % 4], t // 4)
                    if job.channel_major:
                        for t0, t1 in ((0, LAT), (LAT, TOK)):
                            for k in range(KT):
                                last = nc.tensor.matmul(ps[:, t0:t1], w[:, k, m * P:(m + 1) * P],
                                                        job.act_t[:, k, t0:t1], start=k == 0, stop=k == KT - 1)
                    else:
                        for k in range(KT):
                            last = nc.tensor.matmul(ps[:, 0:CHUNK], job.act_t[:, k, m * P:(m + 1) * P],
                                                    w[:, k, :], start=k == 0, stop=k == KT - 1)
                    last.then_inc(tile_done, 1)

            def evacuate(eng, which, steps):
                for t, (c, m) in enumerate(tiles):
                    if jobs[c].engine == which:
                        eng.wait_ge(tile_done, t + 1)
                        jobs[c].evac(eng, psum[t % 4], m, steps).then_inc(slot_free[t % 4], 1)

            @block.scalar
            def _(act):
                evacuate(act, "scalar", Steps(act, act_steps))

            @block.vector
            def _(dve):
                evacuate(dve, "vector", Steps(dve, dve_steps))


def modulation(nc, l, T, ring):
    with ExitStack() as ctx:
        cond = ctx.enter_context(nc.sbuf_tensor("cond", [P, KT, 2], F32))
        csilu = ctx.enter_context(nc.sbuf_tensor("csilu", [P, KT, 2], F32))
        bias = ctx.enter_context(nc.sbuf_tensor("mod_bias", [2, 6 * D], F32))
        rows = ctx.enter_context(nc.sbuf_tensor("mod_rows_sb", [2, 6 * D], F32))
        psum = [ctx.enter_context(nc.psum_tensor(f"mod_ps{i}", [P, 512], F32)) for i in range(2)]
        n = 6 * D // CHUNK
        with stage(nc, "mod_w0", "mod_w1", "mod_in", "mod_silu", "mod_tile", "mod_free", "mod_out") as (block, sems):
            w_loaded, cond_in, silu_done, tile_done, slot_free, rows_out = sems[0:2], *sems[2:]

            @block.sync
            def _(sp):
                sp.dma_start(cond[:], T["cond"]).then_inc(cond_in, 16)
                sp.dma_start(bias[:], T["mod_b"][bass.ds(l, 1), :].to_broadcast([2, 6 * D])).then_inc(cond_in, 16)
                for c in range(2):
                    sp.dma_start(ring[c][:], T["mod_w"][bass.ds(l, 1), c].rearrange("a p k n -> (a p) k n")).then_inc(w_loaded[c], 16)
                with sp.Fori(1, n // 2) as i:
                    for j in range(2):
                        sp.wait_ge(tile_done, 2 * i + j - 1)
                        sp.dma_start(ring[j][:], T["mod_w"][bass.ds(l, 1), bass.ds(2 * i + j, 1)].rearrange(
                            "a b p k n -> (a b p) k n")).then_inc(w_loaded[j], 16)
                sp.wait_ge(slot_free, 2 + n)
                sp.dma_start(T["mod_rows"], rows[:]).then_inc(rows_out, 16)
                sp.wait_ge(rows_out, 16)

            @block.scalar
            def _(act):
                act.wait_ge(cond_in, 32)
                act.activation(csilu[:], cond[:], ACT.Silu).then_inc(silu_done, 1)

            @block.tensor
            def _(pe):
                pe.wait_ge(silu_done, 1)
                with pe.Fori(0, n // 2) as i:
                    for j in range(2):
                        pe.wait_ge(w_loaded[j], 16 * i + 16)
                        pe.wait_ge(slot_free, 2 * i + j + 1)
                        for k in range(KT):
                            last = nc.tensor.matmul(psum[j][0:2, :], csilu[:, k, :], ring[j][:, k, :],
                                                    start=k == 0, stop=k == KT - 1)
                        last.then_inc(tile_done, 1)

            @block.vector
            def _(dve):
                dve.sem_inc(slot_free, 2)
                dve.wait_ge(cond_in, 32)
                with dve.Fori(0, n // 2) as i:
                    for j in range(2):
                        cols = bass.ds((2 * i + j) * CHUNK, CHUNK)
                        dve.wait_ge(tile_done, 2 * i + j + 1)
                        nc.vector.tensor_tensor(rows[:, cols], psum[j][0:2, :], bias[:, cols], ALU.add).then_inc(slot_free, 1)


def mod_row(T, cond, part):
    return T["mod_rows"][cond:cond + 1, part * D:(part + 1) * D].to_broadcast([P, D])


def modulate_and_transpose(nc, T, x_src, h_t, ident, first_part, h_keep=None):
    with ExitStack() as ctx:
        xb = [ctx.enter_context(nc.sbuf_tensor(f"mt_x{i}", [P, D], F32)) for i in range(NB)]
        vec = ctx.enter_context(nc.sbuf_tensor("mt_vec", [P, 2, 2, D], F32))
        psum = [ctx.enter_context(nc.psum_tensor(f"mt_ps{i}", [P, D], F32)) for i in range(2)]
        with stage(nc, "mt_x", "mt_vec_in", "mt_dve", "mt_tp", "mt_ev") as (block, (x_in, vec_in, dve_steps, transposed, copied)):

            @block.sync
            def _(sp):
                for cond in range(2):
                    for j in range(2):
                        sp.dma_start(vec[:, cond, j, :], mod_row(T, cond, first_part + j)).then_inc(vec_in, 16)
                for b in range(NB):
                    sp.dma_start(xb[b][:], x_src(b)).then_inc(x_in, 16)

            @block.vector
            def _(dve):
                step = Steps(dve, dve_steps)
                dve.wait_ge(vec_in, 64)
                dve.wait_ge(x_in, 16 * NB)
                step(nc.vector.tensor_scalar(vec[:, :, 1, :], vec[:, :, 1, :], 1.0, None, ALU.add))
                for b in range(NB):
                    cond = b // (NB - 1)
                    step(nc.vector.tensor_tensor(xb[b][:], xb[b][:], vec[:, cond, 1, :], ALU.mult))
                    step(nc.vector.tensor_tensor(xb[b][:], xb[b][:], vec[:, cond, 0, :], ALU.add))

            @block.tensor
            def _(pe):
                for b in range(NB):
                    pe.wait_ge(dve_steps, 3 + 2 * b)
                    if b >= 2:
                        pe.wait_ge(copied, b - 1)
                    for k in range(KT):
                        last = nc.tensor.transpose(psum[b % 2][:, k * P:(k + 1) * P], xb[b][:, k * P:(k + 1) * P], ident[:])
                    last.then_inc(transposed, 1)

            @block.scalar
            def _(act):
                for b in range(NB):
                    act.wait_ge(transposed, b + 1)
                    act.activation(h_t[:, :, b * P:(b + 1) * P],
                                   psum[b % 2][:].rearrange("p (k t) -> p k t", k=KT), ACT.Copy).then_inc(copied, 1)


def merge_branch(nc, l, T, name, branch, h_t, branch_t, merged_t, ring):
    with ExitStack() as ctx:
        sig = ctx.enter_context(nc.sbuf_tensor(f"{name}_sig", [P, D // P, TOK], F32))

        def gate(c):
            def evac(eng, ps, m, step):
                return nc.scalar.activation(sig[:, 4 * c + m, :], ps[:, 0:TOK], ACT.Sigmoid)
            return evac

        def product(c):
            def evac(eng, ps, m, step):
                t = 4 * c + m
                if branch == 1:
                    return nc.vector.tensor_tensor(merged_t[:, t, :], ps[:, 0:TOK], sig[:, t, :], ALU.mult)
                step(nc.vector.tensor_tensor(sig[:, t, :], ps[:, 0:TOK], sig[:, t, :], ALU.mult))
                return nc.vector.tensor_tensor(merged_t[:, t, :], merged_t[:, t, :], sig[:, t, :], ALU.add)
            return evac

        jobs = [Job(w_in(T, l, ZG + 2 * branch + c), h_t, True, "scalar", gate(c)) for c in range(2)]
        jobs += [Job(T["w_branch"][bass.ds(l, 1), branch, c].rearrange("a p k n -> (a p) k n"), branch_t, True,
                     "vector", product(c)) for c in range(2)]
        projections(nc, name, jobs, ring)


def w_in(T, l, c):
    return T["w_in"][bass.ds(l, 1), c].rearrange("a p k n -> (a p) k n")


def conv_branch(nc, l, T, h_t, out_t, ring):
    PAD = TOK + 4
    with ExitStack() as ctx:
        u = ctx.enter_context(nc.sbuf_tensor("conv_u", [P, KT, PAD], F32))
        y = ctx.enter_context(nc.sbuf_tensor("conv_y", [P, KT, PAD], F32))
        cw = ctx.enter_context(nc.sbuf_tensor("conv_w_sb", [P, KT, 4], F32))

        def parts(t):
            return ((t[:, 1:1 + LAT], 0, LAT), (t[:, LAT + 3:LAT + 3 + CTX], LAT, TOK))

        def keep_c(c):
            def evac(eng, ps, m, step):
                return nc.scalar.activation(out_t[:, 4 * c + m, :], ps[:, 0:TOK], ACT.Copy)
            return evac

        def times_c(c):
            def evac(eng, ps, m, step):
                for dst, t0, t1 in parts(u[:, 4 * c + m, :]):
                    last = nc.vector.tensor_tensor(dst, ps[:, t0:t1], out_t[:, 4 * c + m, t0:t1], ALU.mult)
                return last
            return evac

        def times_b(c):
            def evac(eng, ps, m, step):
                for src, t0, t1 in parts(y[:, 4 * c + m, :]):
                    last = nc.vector.tensor_tensor(out_t[:, 4 * c + m, t0:t1], ps[:, t0:t1], src, ALU.mult)
                return last
            return evac

        projections(nc, "convu", [Job(w_in(T, l, ZC + c), h_t, True, "scalar", keep_c(c)) for c in range(2)]
                    + [Job(w_in(T, l, ZX + c), h_t, True, "vector", times_c(c)) for c in range(2)], ring)
        with stage(nc, "conv_in", "conv_pad", "conv_dve") as (block, (w_loaded, pads, dve_steps)):
            @block.sync
            def _(sp):
                sp.dma_start(cw[:], T["conv"][bass.ds(l, 1)].rearrange("a p k n -> (a p) k n")).then_inc(w_loaded, 16)

            @block.gpsimd
            def _(pool):
                nc.gpsimd.memset(u[:, :, 0:1], 0.0).then_inc(pads, 1)
                nc.gpsimd.memset(u[:, :, LAT + 1:LAT + 3], 0.0).then_inc(pads, 1)
                nc.gpsimd.memset(u[:, :, PAD - 1:PAD], 0.0).then_inc(pads, 1)

            @block.vector
            def _(dve):
                step = Steps(dve, dve_steps)
                dve.wait_ge(w_loaded, 16)
                dve.wait_ge(pads, 3)
                n = PAD - 2
                for k in range(KT):
                    step(nc.vector.tensor_scalar(y[:, k, 1:1 + n], u[:, k, 0:n], cw[:, k, 0:1], cw[:, k, 3:4], ALU.mult, ALU.add))
                    step(nc.vector.scalar_tensor_tensor(y[:, k, 1:1 + n], u[:, k, 1:1 + n], cw[:, k, 1:2], y[:, k, 1:1 + n], ALU.mult, ALU.add))
                    step(nc.vector.scalar_tensor_tensor(y[:, k, 1:1 + n], u[:, k, 2:2 + n], cw[:, k, 2:3], y[:, k, 1:1 + n], ALU.mult, ALU.add))
        projections(nc, "convb", [Job(w_in(T, l, ZB + c), h_t, True, "vector", times_b(c)) for c in range(2)], ring)


def attention(nc, l, T, h_t, q_t, o_tok, ring, ident):
    with ExitStack() as ctx:
        def sb(name, shape):
            return ctx.enter_context(nc.sbuf_tensor(name, shape, F32))
        k_t = sb("att_k", [P, HEADS, TOK])
        v_tok = sb("att_v", [P, NB + 1, D])

        def channel(dst, c):
            def evac(eng, ps, m, step):
                return nc.scalar.activation(dst[:, 4 * c + m, :], ps[:, 0:TOK], ACT.Copy)
            return evac

        def token(dst, c):
            def evac(eng, ps, m, step):
                return nc.vector.tensor_copy(dst[:, m, c * CHUNK:(c + 1) * CHUNK], ps[:, 0:CHUNK])
            return evac

        projections(nc, "qkv",
                    [Job(w_in(T, l, ZQ + c), h_t, True, "scalar", channel(q_t, c)) for c in range(2)]
                    + [Job(w_in(T, l, ZK + c), h_t, True, "scalar", channel(k_t, c)) for c in range(2)]
                    + [Job(w_in(T, l, ZV + c), h_t, False, "vector", token(v_tok, c)) for c in range(2)], ring)
        attention_core(nc, l, T, q_t, k_t, v_tok, o_tok, ident)


def attention_core(nc, l, T, q_t, k_t, v_tok, o_tok, ident):
    UNITS = NB
    KEYS = LAT + CTX
    with ExitStack() as ctx:
        def sb(name, shape):
            return ctx.enter_context(nc.sbuf_tensor(name, shape, F32))
        kc = sb("att_kc", [P, HEADS, CTX])
        cos, sin, rot = sb("att_cos", [P, LAT]), sb("att_sin", [P, LAT]), sb("att_rot", [P, P])
        lam_in, lam_pr = sb("att_lam_in", [P, 4, QK]), sb("att_lam_pr", [P, 2, QK])
        lam = sb("att_lam", [P, 4])
        neg_lam, lam0 = sb("att_neg_lam", [P, 1]), sb("att_lam0", [P, DEPTH])
        qs, ks = sb("att_qs", [P, TOK]), sb("att_ks", [P, KEYS + CTX])
        rotated = sb("att_rotated", [P, LAT])
        prob = [sb(f"att_p{i}", [P, 2, KEYS]) for i in range(2)]
        prob_t = sb("att_pt", [P, KEYS])
        mx, rs, ri = sb("att_mx", [P, 2, 2]), sb("att_rs", [P, 2, 2]), sb("att_ri", [P, 2, 2])
        k_new = sb("att_knew", [P, D])
        ps_rot = ctx.enter_context(nc.psum_tensor("att_ps_rot", [P, LAT], F32))
        ps_s = ctx.enter_context(nc.psum_tensor("att_ps_s", [P, 2, 1024], F32))
        ps_t = ctx.enter_context(nc.psum_tensor("att_ps_t", [P, 1024], F32))
        ps_o = ctx.enter_context(nc.psum_tensor("att_ps_o", [P, 512], F32))
        with stage(nc, "ac_in", "ac_lam", "ac_lexp", "ac_rot", "ac_rotfree", "ac_staged", "ac_score", "ac_nmax",
                   "ac_exp", "ac_mixed", "ac_tp", "ac_ptc", "ac_pv", "ac_out", "ac_dve", "ac_knt", "ac_kout") as (block, sems):
            (loaded, lam_sum, lam_exp, rot_done, rot_used, staged, scored, maxed, exped, mixed, transposed,
             pt_ready, pv_done, o_out, dve_steps, kn_done, k_out) = sems

            @block.sync
            def _(sp):
                one = bass.ds(l, 1)
                for dst, src in ((kc[:], T["kc"][one].rearrange("a p h j -> (a p) h j")), (v_tok[:, NB, :], T["vc"][one].rearrange("a p n -> (a p) n")),
                                 (cos[:], T["cos"]), (sin[:], T["sin"]), (rot[:], T["rot"]), (lam0[:], T["lam0"]),
                                 (lam_in[:], T["lam"][one].rearrange("a x d -> a (x d)").to_broadcast([P, 4 * QK]).rearrange("p (x d) -> p x d", x=4))):
                    sp.dma_start(dst, src).then_inc(loaded, 16)
                sp.dma_start(T["new_v"][one].rearrange("a p n -> (a p) n"), v_tok[:, NB - 1, :]).then_inc(k_out, 16)
                sp.wait_ge(kn_done, HEADS)
                sp.dma_start(T["new_k"][one].rearrange("a p n -> (a p) n"), k_new[:]).then_inc(k_out, 16)
                sp.wait_ge(k_out, 32)

            def keys_of(u):
                return (0, KEYS) if u < UNITS - 1 else (KEYS, KEYS + CTX)

            @block.tensor
            def _(pe):
                def scores(h, u):
                    n = UNITS * h + u
                    k0, k1 = keys_of(u)
                    pe.wait_ge(exped, 2 * n + 1)
                    for j in range(2):
                        rows = slice(QK * j, QK * j + QK)
                        for c0 in range(k0, k1, LAT):
                            c1 = min(c0 + LAT, k1)
                            last = nc.tensor.matmul(ps_s[:, j, c0 - k0:c1 - k0], qs[rows, u * P:(u + 1) * P],
                                                    ks[rows, c0:c1], start=True, stop=True)
                    last.then_inc(scored, 1)

                pe.wait_ge(loaded, 16 * 7)
                with pe.Fori(0, HEADS) as h:
                    for n, src in enumerate((q_t, k_t)):
                        pe.wait_ge(rot_used, 3 * h + n + 1)
                        nc.tensor.matmul(ps_rot[:], rot[:], src[:, bass.ds(h, 1), 0:LAT].rearrange("p a t -> p (a t)"),
                                         start=True, stop=True).then_inc(rot_done, 1)
                    pe.wait_ge(staged, h + 1)
                    scores(h, 0)
                    for u in range(UNITS):
                        n = UNITS * h + u
                        k0, k1 = keys_of(u)
                        if u + 1 < UNITS:
                            scores(h, u + 1)
                        pe.wait_ge(mixed, n + 1)
                        pe.wait_ge(pt_ready, n + 1)
                        for kb in range((k1 - k0) // P):
                            last = nc.tensor.transpose(ps_t[:, kb * P:(kb + 1) * P], prob[u % 2][:, 0, kb * P:(kb + 1) * P], ident[:])
                        last.then_inc(transposed, 1)
                        pe.wait_ge(pt_ready, n + 2)
                        pe.wait_ge(o_out, n + 1)
                        blocks = [0, 1, 2, 3, NB] if u < UNITS - 1 else [NB - 1]
                        for i, vb in enumerate(blocks):
                            last = nc.tensor.matmul(ps_o[:, 0:P], prob_t[:, i * P:(i + 1) * P],
                                                    v_tok[:, vb, bass.ds(h * P, P)], start=i == 0, stop=i == len(blocks) - 1)
                        last.then_inc(pv_done, 1)
                    pe.wait_ge(rot_used, 3 * h + 3)
                    nc.tensor.transpose(ps_rot[:, 0:P], ks[:, KEYS:KEYS + CTX], ident[:]).then_inc(transposed, 1)

            @block.scalar
            def _(act):
                def exps(h, u):
                    n = UNITS * h + u
                    k0, k1 = keys_of(u)
                    act.wait_ge(maxed, n + 1)
                    for j in range(2):
                        act.activation(prob[u % 2][:, j, 0:k1 - k0], ps_s[:, j, 0:k1 - k0], ACT.Exp,
                                       bias=mx[:, u % 2, j:j + 1], scale=SCALE,
                                       accum_out=rs[:, u % 2, j:j + 1]).then_inc(exped, 1)

                act.sem_inc(exped, 1)
                act.sem_inc(pt_ready, 1)
                act.wait_ge(lam_sum, 1)
                act.activation(lam[:, 2:4], lam[:, 0:2], ACT.Exp).then_inc(lam_exp, 1)
                with act.Fori(0, HEADS) as h:
                    exps(h, 0)
                    for u in range(UNITS):
                        k0, k1 = keys_of(u)
                        act.wait_ge(transposed, (UNITS + 1) * h + u + 1)
                        act.activation(prob_t[:, 0:k1 - k0], ps_t[:, 0:k1 - k0], ACT.Copy).then_inc(pt_ready, 1)
                        if u + 1 < UNITS:
                            exps(h, u + 1)

            @block.vector
            def _(dve):
                dve.sem_inc(o_out, 1)
                dve.sem_inc(rot_used, 1)
                dve.wait_ge(loaded, 16 * 7)
                step = Steps(dve, dve_steps)
                step(nc.vector.tensor_tensor(lam_pr[:], lam_in[:, 0:4:2, :], lam_in[:, 1:4:2, :], ALU.mult))
                nc.vector.tensor_reduce(lam[:, 0:2], lam_pr[:], AX.X, ALU.add).then_inc(lam_sum, 1)
                dve.wait_ge(lam_exp, 1)
                step(nc.vector.tensor_tensor(neg_lam[:], lam[:, 3:4], lam[:, 2:3], ALU.subtract))
                step(nc.vector.tensor_tensor(neg_lam[:], neg_lam[:], lam0[:, bass.ds(l, 1)], ALU.subtract))
                first = step.n

                def flat(ap):
                    return ap.rearrange("p a t -> p (a t)")

                with dve.Fori(0, HEADS) as h:
                    per_head = 6 + 4 * UNITS
                    step = Steps(dve, dve_steps, per_head * h + first)
                    head = bass.ds(h, 1)

                    def maxima(u):
                        k0, k1 = keys_of(u)
                        m = mx[:, u % 2, :]
                        dve.wait_ge(scored, UNITS * h + u + 1)
                        step(nc.vector.tensor_reduce(m, ps_s[:, :, 0:k1 - k0], AX.X, ALU.max))
                        nc.vector.tensor_scalar(m, m, -SCALE, None, ALU.mult).then_inc(maxed, 1)

                    for n, (src, dst) in enumerate(((q_t, qs), (k_t, ks))):
                        dve.wait_ge(rot_done, 2 * h + n + 1)
                        nc.vector.tensor_tensor(rotated[:], ps_rot[:], sin[:], ALU.mult).then_inc(rot_used, 1)
                        step(nc.vector.tensor_tensor(dst[:, 0:LAT], flat(src[:, head, 0:LAT]), cos[:], ALU.mult))
                        dve.wait_ge(rot_used, 3 * h + n + 2)
                        step(nc.vector.tensor_tensor(dst[:, 0:LAT], dst[:, 0:LAT], rotated[:], ALU.add))
                    step(nc.vector.tensor_copy(qs[:, LAT:TOK], flat(q_t[:, head, LAT:TOK])))
                    step(nc.vector.tensor_copy(ks[:, KEYS:KEYS + CTX], flat(k_t[:, head, LAT:TOK])))
                    nc.vector.tensor_copy(ks[:, LAT:KEYS], flat(kc[:, head, :])).then_inc(staged, 1)
                    maxima(0)
                    for u in range(UNITS):
                        n = UNITS * h + u
                        k0, k1 = keys_of(u)
                        w = k1 - k0
                        pr, i = prob[u % 2], ri[:, u % 2, :]
                        dve.wait_ge(exped, 2 * n + 3)
                        step(nc.vector.reciprocal(i, rs[:, u % 2, :]))
                        step(nc.vector.tensor_scalar(i[:, 1:2], i[:, 1:2], neg_lam[:], None, ALU.mult))
                        step(nc.vector.tensor_scalar(pr[:, 1, 0:w], pr[:, 1, 0:w], i[:, 1:2], None, ALU.mult))
                        nc.vector.scalar_tensor_tensor(pr[:, 0, 0:w], pr[:, 0, 0:w], i[:, 0:1], pr[:, 1, 0:w], ALU.mult, ALU.add).then_inc(mixed, 1)
                        if u + 1 < UNITS:
                            maxima(u + 1)
                        dve.wait_ge(pv_done, n + 1)
                        nc.vector.tensor_copy(o_tok[:, u, bass.ds(h * P, P)], ps_o[:, 0:P]).then_inc(o_out, 1)
                    dve.wait_ge(transposed, (UNITS + 1) * h + UNITS + 1)
                    nc.vector.tensor_copy(k_new[:, bass.ds(h * P, P)], ps_rot[:, 0:P]).then_inc(kn_done, 1)
                    dve.wait_ge(kn_done, h + 1)
                    dve.sem_inc(rot_used, 1)
                    assert step.n == per_head, step.n


def normalise(nc, name, o_tok, weight, factor):
    with ExitStack() as ctx:
        def sb(n, shape):
            return ctx.enter_context(nc.sbuf_tensor(f"{name}_{n}", shape, F32))
        sq, w, fac = sb("sq", [P, D]), sb("w", [P, P]), sb("fac", [P, 1])
        ms, rstd = sb("ms", [P, NB * HEADS]), sb("rstd", [P, NB * HEADS])
        with stage(nc, f"{name}_in", f"{name}_dve", f"{name}_ms", f"{name}_rt") as (block, (loaded, dve_steps, ms_done, root_done)):
            @block.sync
            def _(sp):
                sp.dma_start(w[:], weight.to_broadcast([P, P])).then_inc(loaded, 16)
                if factor is not None:
                    sp.dma_start(fac[:], factor).then_inc(loaded, 16)

            @block.scalar
            def _(act):
                act.wait_ge(ms_done, 1)
                act.activation(rstd[:], ms[:], ACT.Sqrt).then_inc(root_done, 1)

            @block.vector
            def _(dve):
                step = Steps(dve, dve_steps)
                for b in range(NB):
                    step(nc.vector.tensor_tensor(sq[:], o_tok[:, b, :], o_tok[:, b, :], ALU.mult))
                    step(nc.vector.tensor_reduce(ms[:, b * HEADS:(b + 1) * HEADS], sq[:].rearrange("p (h v) -> p h v", h=HEADS), AX.X, ALU.add))
                nc.vector.tensor_scalar(ms[:], ms[:], 1.0 / P, EPS, ALU.mult, ALU.add).then_inc(ms_done, 1)
                dve.wait_ge(root_done, 1)
                step(nc.vector.reciprocal(rstd[:], rstd[:]))
                dve.wait_ge(loaded, 16 if factor is None else 32)
                if factor is not None:
                    step(nc.vector.tensor_scalar(w[:], w[:], fac[:], None, ALU.mult))
                for b in range(NB):
                    o = o_tok[:, b, :].rearrange("p (h v) -> p h v", h=HEADS)
                    step(nc.vector.tensor_tensor(o, o, rstd[:, b * HEADS:(b + 1) * HEADS].unsqueeze(2).to_broadcast([P, HEADS, P]), ALU.mult))
                    step(nc.vector.tensor_tensor(o, o, w[:].unsqueeze(1).to_broadcast([P, HEADS, P]), ALU.mult))


def to_channel_major(nc, name, src_tok, dst_t, ident):
    with ExitStack() as ctx:
        psum = [ctx.enter_context(nc.psum_tensor(f"{name}_ps{i}", [P, D], F32)) for i in range(2)]
        with stage(nc, f"{name}_tp", f"{name}_cp") as (block, (transposed, copied)):
            @block.tensor
            def _(pe):
                for b in range(NB):
                    if b >= 2:
                        pe.wait_ge(copied, b - 1)
                    for k in range(KT):
                        last = nc.tensor.transpose(psum[b % 2][:, k * P:(k + 1) * P], src_tok[:, b, k * P:(k + 1) * P], ident[:])
                    last.then_inc(transposed, 1)

            @block.scalar
            def _(act):
                for b in range(NB):
                    act.wait_ge(transposed, b + 1)
                    act.activation(dst_t[:, :, b * P:(b + 1) * P], psum[b % 2][:].rearrange("p (k t) -> p k t", k=KT),
                                   ACT.Copy).then_inc(copied, 1)


def recurrent_branch(nc, l, T, h_t, q_t, o_tok, ring, ident):
    with ExitStack() as ctx:
        i_tok = ctx.enter_context(nc.sbuf_tensor("rec_i", [P, NB, D], F32))

        def channel(c):
            def evac(eng, ps, m, step):
                return nc.scalar.activation(q_t[:, 4 * c + m, :], ps[:, 0:TOK], ACT.Silu)
            return evac

        def token(c):
            def evac(eng, ps, m, step):
                return nc.vector.tensor_copy(i_tok[:, m, c * CHUNK:(c + 1) * CHUNK], ps[:, 0:CHUNK])
            return evac

        projections(nc, "rqi", [Job(w_in(T, l, RQ + c), h_t, True, "scalar", channel(c)) for c in range(2)]
                    + [Job(w_in(T, l, RI + c), h_t, False, "vector", token(c)) for c in range(2)], ring)
        with ExitStack() as inner:
            lf = inner.enter_context(nc.sbuf_tensor("rec_lf", [P, NB, D], F32))
            kk = inner.enter_context(nc.sbuf_tensor("rec_k", [P, NB, D], F32))
            for d, first in enumerate((RFF, RFB)):
                def sig(c):
                    def evac(eng, ps, m, step):
                        return nc.scalar.activation(kk[:, m, c * CHUNK:(c + 1) * CHUNK], ps[:, 0:CHUNK], ACT.Sigmoid)
                    return evac
                projections(nc, f"rf{d}", [Job(w_in(T, l, first + c), h_t, False, "scalar", sig(c)) for c in range(2)], ring)
                forget_gates(nc, l, T, d, kk, lf, ring)
                scan(nc, l, T, d, q_t, i_tok, kk, lf, o_tok, ring, ident)
        normalise(nc, f"recn", o_tok, T["rec_norm"][bass.ds(l, 1), :], None)
        gate = i_tok

        def gated(c):
            def evac(eng, ps, m, step):
                cols = slice(c * CHUNK, (c + 1) * CHUNK)
                step(nc.scalar.activation(gate[:, m, cols], ps[:, 0:CHUNK], ACT.Silu))
                return nc.scalar.activation(gate[:, m, cols], gate[:, m, cols], ACT.Copy)
            return evac
        projections(nc, "rg", [Job(w_in(T, l, RG + c), h_t, False, "scalar", gated(c)) for c in range(2)], ring)
        with stage(nc, "rg_mul") as (block, (multiplied,)):
            @block.vector
            def _(dve):
                for b in range(NB):
                    nc.vector.tensor_tensor(o_tok[:, b, :], o_tok[:, b, :], gate[:, b, :], ALU.mult).then_inc(multiplied, 1)


def forget_gates(nc, l, T, d, kk, lf, ring):
    r = ring[0][:].rearrange("p k n -> p (k n)").rearrange("p (a n) -> p a n", a=4)
    with ExitStack() as ctx:
        sel = ctx.enter_context(nc.sbuf_tensor(f"fg{d}_sel", [P, DEPTH], F32))
        with stage(nc, "fg_in", "fg_dve", "fg_cent", "fg_exp", "fg_f", "fg_ln") as (block, (loaded, dve_steps, centred, exped, f_ready, ln_done)):
            @block.sync
            def _(sp):
                sp.dma_start(sel[:], T["sel"]).then_inc(loaded, 16)
                for j in range(DEPTH):
                    sp.dma_start(r[:, j, :], T["rec_lb"][j, d:d + 1, :].to_broadcast([P, D])).then_inc(loaded, 16)

            @block.scalar
            def _(act):
                act.wait_ge(centred, 1)
                act.activation(r[:, 0:2, :], r[:, 0:2, :], ACT.Exp).then_inc(exped, 1)
                for b in range(NB):
                    act.wait_ge(f_ready, b + 1)
                    act.activation(lf[:, b, :], lf[:, b, :], ACT.Ln).then_inc(ln_done, 1)

            @block.vector
            def _(dve):
                step = Steps(dve, dve_steps)
                dve.wait_ge(loaded, 16 * 3)
                step(nc.vector.tensor_tensor(r[:, 2, :], r[:, 0, :], r[:, 1, :], ALU.max))
                nc.vector.tensor_tensor(r[:, 0:2, :], r[:, 0:2, :], r[:, 2:3, :].to_broadcast([P, 2, D]), ALU.subtract).then_inc(centred, 1)
                dve.wait_ge(exped, 1)
                step(nc.vector.tensor_tensor(r[:, 2, :], r[:, 0, :], r[:, 1, :], ALU.add))
                step(nc.vector.reciprocal(r[:, 2, :], r[:, 2, :]))
                step(nc.vector.tensor_tensor(r[:, 1, :], r[:, 1, :], r[:, 2, :], ALU.mult))
                step(nc.vector.tensor_scalar(r[:, 1, :], r[:, 1, :], sel[:, bass.ds(l, 1)], None, ALU.mult))
                step(nc.vector.tensor_scalar(r[:, 0, :], r[:, 1, :], -1.0, 1.0, ALU.mult, ALU.add))
                for b in range(NB):
                    step(nc.vector.tensor_tensor(lf[:, b, :], kk[:, b, :], r[:, 0, :], ALU.mult))
                    step(nc.vector.tensor_tensor(lf[:, b, :], lf[:, b, :], r[:, 1, :], ALU.add))
                    step(nc.vector.tensor_scalar(kk[:, b, :], lf[:, b, :], -1.0, 1.0, ALU.mult, ALU.add))
                    nc.vector.tensor_scalar(lf[:, b, :], lf[:, b, :], TINY, None, ALU.max).then_inc(f_ready, 1)


def scan(nc, l, T, d, q_t, i_tok, kk, lf, o_tok, ring, ident):
    units = NB * HEADS
    edge = P - 1 if d == 0 else 0
    with ExitStack() as ctx:
        def sb(name, shape):
            return ctx.enter_context(nc.sbuf_tensor(f"scan{d}_{name}", shape, F32))
        levels, suffix, mask = sb("levels", [P, LEVELS + 1, P]), sb("suffix", [P, P]), sb("mask", [P, LEVELS + 1, P])
        state = sb("state", [P, 2, D])
        room = [r[:].rearrange("p k n -> p (k n)") for r in ring]

        def carve(j, at, n):
            return room[j][:, at * P:(at + n) * P]
        expd = [carve(j, 0, 8) for j in range(2)]
        xq = [carve(j, 8, 8) for j in range(2)]
        xk = [carve(j, 16, 7) for j in range(2)]
        k_tr = [carve(j, 23, 1) for j in range(2)]
        masked_w = [carve(j, 24, 8) for j in range(2)]
        lfs = [sb(f"lfs{j}", [P, P]) for j in range(2)]
        ks = [sb(f"ks{j}", [P, P]) for j in range(2)]
        rest = [sb(f"rest{j}", [P, P]) for j in range(2)]
        k_dec = [sb(f"kdec{j}", [P, P]) for j in range(2)]
        weights = [sb(f"w{j}", [P, P]) for j in range(2)]
        ps_d = ctx.enter_context(nc.psum_tensor(f"scan{d}_ps_d", [P, 1024], F32))
        ps_r = ctx.enter_context(nc.psum_tensor(f"scan{d}_ps_r", [P, 512], F32))
        ps_a = ctx.enter_context(nc.psum_tensor(f"scan{d}_ps_a", [P, 1024], F32))
        ps_o = ctx.enter_context(nc.psum_tensor(f"scan{d}_ps_o", [P, 512], F32))
        ps_s = ctx.enter_context(nc.psum_tensor(f"scan{d}_ps_s", [P, 512], F32))

        def where(i, j):
            b = i // 4 if d == 0 else NB - 1 - i // 4
            return b, b // (NB - 1), (i % 4) * 2 + j

        def blk(t, b, h):
            return t[:, bass.ds(b, 1), bass.ds(h * P, P)].rearrange("p a n -> p (a n)")

        def over_units(eng, body, last=None):
            with eng.Fori(0, units // 2 - 1) as i:
                body(i, 0, True)
                body(i, 1, True)
            body(units // 2 - 1, 0, True)
            body(units // 2 - 1, 1, False)

        with stage(nc, "sc_in", "sc_copied", "sc_s1", "sc_exped", "sc_xk", "sc_xq", "sc_a", "sc_masked",
                   "sc_as", "sc_o", "sc_unit", "sc_out") as (block, sems):
            loaded, staged, spans, exped, xk_done, xq_done, a_done, masked, w_done, o_done, unit_done, s_out = sems

            @block.sync
            def _(sp):
                one = bass.ds(l, 1)
                sp.dma_start(levels[:], T["levels"][d]).then_inc(loaded, 16)
                sp.dma_start(suffix[:], T["suffix"][d]).then_inc(loaded, 16)
                sp.dma_start(mask[:], T["mask"][d]).then_inc(loaded, 16)
                sp.dma_start(state[:, 0, :], T["state"][one, d].rearrange("a p n -> (a p) n")).then_inc(loaded, 16)
                sp.wait_ge(unit_done, 2 + units)
                sp.dma_start(T["new_state"][one, d].rearrange("a p n -> (a p) n"), state[:, 1, :]).then_inc(s_out, 16)
                sp.wait_ge(s_out, 16)

            @block.gpsimd
            def _(pool):
                nc.gpsimd.memset(state[:, 1, :], 0.0).then_inc(staged, 1)

                def stage_in(i, j):
                    b, _, h = where(i, j)
                    pool.wait_ge(spans, 2 * i + j + 1)
                    nc.gpsimd.tensor_copy(lfs[j][:], blk(lf, b, h)).then_inc(staged, 1)
                    nc.gpsimd.tensor_copy(ks[j][:], blk(kk, b, h)).then_inc(staged, 1)

                def body(i, j, more):
                    b, _, h = where(i, j)
                    if more:
                        stage_in(i + j, 1 - j)
                    pool.wait_ge(exped, 6 * i + 3 * j + 4)
                    pool.wait_ge(unit_done, 2 * i + j + 1)
                    q = q_t[:, bass.ds(h, 1), bass.ds(b * P, P)].to_broadcast([P, LEVELS + 1, P])
                    nc.gpsimd.tensor_tensor(xq[j].rearrange("p (a t) -> p a t", t=P), expd[j].rearrange("p (a t) -> p a t", t=P),
                                            q, ALU.mult).then_inc(xq_done, 1)
                stage_in(0, 0)
                over_units(pool, body)

            @block.tensor
            def _(pe):
                def span_sums(i, j):
                    pe.wait_ge(staged, 4 * i + 2 * j + 3)
                    pe.wait_ge(exped, 6 * i + 3 * j + 1)
                    for c in range(2):
                        nc.tensor.matmul(ps_d[:, c * 512:(c + 1) * 512], lfs[j][:],
                                         levels[:, 4 * c:4 * c + 4, :].rearrange("p a t -> p (a t)"), start=True, stop=True)
                    nc.tensor.matmul(ps_r[:, 0:P], suffix[:], lfs[j][:], start=True, stop=True)
                    nc.tensor.transpose(ps_r[:, P:2 * P], ks[j][:], ident[:]).then_inc(spans, 1)

                def body(i, j, more):
                    b, req, h = where(i, j)
                    if more:
                        span_sums(i + j, 1 - j)
                    pe.wait_ge(xk_done, 4 * i + 2 * j + 1)
                    pe.wait_ge(xq_done, 2 * i + j + 1)
                    pe.wait_ge(w_done, 2 * i + j + 1)
                    for a in range(LEVELS):
                        nc.tensor.matmul(ps_a[:, a * P:(a + 1) * P], xk[j][:, a * P:(a + 1) * P], xq[j][:, a * P:(a + 1) * P],
                                         start=True, stop=True)
                    nc.tensor.matmul(ps_a[:, LEVELS * P:], k_tr[j],
                                     q_t[:, bass.ds(h, 1), bass.ds(b * P, P)].rearrange("p a t -> p (a t)"),
                                     start=True, stop=True).then_inc(a_done, 1)
                    pe.wait_ge(w_done, 2 * i + j + 2)
                    pe.wait_ge(xk_done, 4 * i + 2 * j + 2)
                    pe.wait_ge(unit_done, 2 * i + j + 2)
                    nc.tensor.matmul(ps_o[:, 0:P], weights[j][:], blk(i_tok, b, h), start=True, stop=False)
                    nc.tensor.matmul(ps_o[:, 0:P], xq[j][:, LEVELS * P:], blk(state, req, h), start=False, stop=True)
                    nc.tensor.matmul(ps_s[:, 0:P], k_dec[j][:], blk(i_tok, b, h), start=True, stop=True).then_inc(o_done, 1)

                pe.sem_inc(spans, 2)
                pe.wait_ge(loaded, 64)
                span_sums(0, 0)
                over_units(pe, body)

            @block.scalar
            def _(act):
                act.sem_inc(exped, 1)

                def body(i, j, more):
                    act.wait_ge(spans, 2 * i + j + 3)
                    act.wait_ge(unit_done, 2 * i + j + 1)
                    act.activation(expd[j], ps_d[:], ACT.Exp).then_inc(exped, 1)
                    act.activation(rest[j][:], ps_r[:, 0:P], ACT.Exp).then_inc(exped, 1)
                    act.activation(k_tr[j], ps_r[:, P:2 * P], ACT.Copy).then_inc(exped, 1)
                over_units(act, body)

            @block.vector
            def _(dve):
                def keys(i, j):
                    b, _, h = where(i, j)
                    dve.wait_ge(exped, 6 * i + 3 * j + 4)
                    nc.vector.tensor_tensor(xk[j].rearrange("p (a t) -> p a t", t=P), expd[j][:, 0:LEVELS * P].rearrange("p (a t) -> p a t", t=P),
                                            k_tr[j].unsqueeze(1).to_broadcast([P, LEVELS, P]), ALU.mult).then_inc(xk_done, 1)
                    nc.vector.tensor_tensor(k_dec[j][:], blk(kk, b, h), rest[j][:], ALU.mult).then_inc(xk_done, 1)

                def body(i, j, more):
                    b, req, h = where(i, j)
                    dve.wait_ge(a_done, 2 * i + j + 1)
                    nc.vector.tensor_tensor(masked_w[j], ps_a[:], mask[:].rearrange("p a t -> p (a t)"), ALU.mult).then_inc(masked, 1)
                    dve.wait_ge(masked, 2 * i + j + 1)
                    nc.vector.tensor_reduce(weights[j][:], masked_w[j].rearrange("p (a t) -> p t a", t=P), AX.X, ALU.add).then_inc(w_done, 1)
                    if more:
                        keys(i + j, 1 - j)
                    dve.wait_ge(o_done, 2 * i + j + 1)
                    if d == 0:
                        nc.vector.tensor_copy(blk(o_tok, b, h), ps_o[:, 0:P])
                    else:
                        nc.vector.tensor_tensor(blk(o_tok, b, h), blk(o_tok, b, h), ps_o[:, 0:P], ALU.add)
                    nc.vector.scalar_tensor_tensor(blk(state, req, h), blk(state, req, h), expd[j][:, LEVELS * P + edge:LEVELS * P + edge + 1],
                                                   ps_s[:, 0:P], ALU.mult, ALU.add).then_inc(unit_done, 1)

                dve.sem_inc(unit_done, 2)
                dve.sem_inc(w_done, 1)
                dve.wait_ge(loaded, 64)
                dve.wait_ge(staged, 1)
                keys(0, 0)
                over_units(dve, body)


def output_projection(nc, l, T, merged_t, y_tok, ring):
    with ExitStack() as ctx:
        gate = ctx.enter_context(nc.sbuf_tensor("op_gate", [P, 2, D], F32))
        with stage(nc, "op_in") as (block, (loaded,)):
            @block.sync
            def _(sp):
                for cond in range(2):
                    sp.dma_start(gate[:, cond, :], mod_row(T, cond, 2)).then_inc(loaded, 16)
                sp.wait_ge(loaded, 32)

        def evac(c):
            def f(eng, ps, m, step):
                cols = slice(c * CHUNK, (c + 1) * CHUNK)
                return nc.vector.tensor_tensor(y_tok[:, m, cols], ps[:, 0:CHUNK], gate[:, m // (NB - 1), cols], ALU.mult)
            return f
        projections(nc, "op", [Job(T["w_out"][bass.ds(l, 1), c].rearrange("a p k n -> (a p) k n"), merged_t, False, "vector", evac(c))
                               for c in range(2)], ring)


def residual_norm(nc, l, T, name, which, y_tok, x_tok, x_from, h_tok, gate_part, x_to):
    with ExitStack() as ctx:
        def sb(n, shape):
            return ctx.enter_context(nc.sbuf_tensor(f"{name}_{n}", shape, F32))
        gb = sb("gb", [P, 2, D])
        vec = sb("vec", [P, 2, 2, D]) if h_tok is not None else None
        scale = sb("ysc", [P, 2, D]) if gate_part is not None else None
        stats, mv, root, nbias = sb("stats", [P, NB, 12]), sb("mv", [P, NB, 2]), sb("root", [P, NB]), sb("nb", [P, NB])
        with stage(nc, f"{name}_in", f"{name}_dve", f"{name}_var", f"{name}_root", f"{name}_xd", f"{name}_out") as (
                block, (loaded, dve_steps, var_done, root_done, x_done, stored)):
            n_in = 2 + (NB if x_from is not None else 0) + (4 if h_tok is not None else 0) + (2 if gate_part is not None else 0)

            @block.sync
            def _(sp):
                one = bass.ds(l, 1)
                sp.dma_start(gb[:, 0, :], T["ln_g"][one, which, :].to_broadcast([P, D])).then_inc(loaded, 16)
                sp.dma_start(gb[:, 1, :], T["ln_b"][one, which, :].to_broadcast([P, D])).then_inc(loaded, 16)
                if x_from is not None:
                    for b in range(NB):
                        sp.dma_start(x_tok[:, b, :], x_from(b)).then_inc(loaded, 16)
                if h_tok is not None:
                    for cond in range(2):
                        for j in range(2):
                            sp.dma_start(vec[:, cond, j, :], mod_row(T, cond, 3 + j)).then_inc(loaded, 16)
                if scale is not None:
                    for cond in range(2):
                        sp.dma_start(scale[:, cond, :], mod_row(T, cond, gate_part)).then_inc(loaded, 16)
                if x_to is not None:
                    for b in range(NB):
                        sp.wait_ge(x_done, b + 1)
                        sp.dma_start(x_to(b), x_tok[:, b, :]).then_inc(stored, 16)
                    sp.wait_ge(stored, 16 * NB)

            @block.scalar
            def _(act):
                act.wait_ge(var_done, 1)
                act.activation(root[:], mv[:, :, 1], ACT.Sqrt).then_inc(root_done, 1)

            @block.vector
            def _(dve):
                step = Steps(dve, dve_steps)
                dve.wait_ge(loaded, 16 * n_in)
                if vec is not None:
                    step(nc.vector.tensor_scalar(vec[:, :, 1, :], vec[:, :, 1, :], 1.0, None, ALU.add))
                for b in range(NB):
                    if scale is not None:
                        step(nc.vector.tensor_tensor(y_tok[:, b, :], y_tok[:, b, :], scale[:, b // (NB - 1), :], ALU.mult))
                    step(nc.vector.scalar_tensor_tensor(x_tok[:, b, :], x_tok[:, b, :], ALPHA, y_tok[:, b, :], ALU.mult, ALU.add))
                    for half in range(2):
                        step(nc.vector.bn_stats(stats[:, b, 6 * half:6 * half + 6], x_tok[:, b, half * 512:(half + 1) * 512]))
                    step(nc.vector.bn_aggr(mv[:, b, :], stats[:, b, :]))
                nc.vector.tensor_scalar(mv[:, :, 1], mv[:, :, 1], EPS, None, ALU.add).then_inc(var_done, 1)
                dve.wait_ge(root_done, 1)
                step(nc.vector.reciprocal(root[:], root[:]))
                for b in range(NB):
                    x = x_tok[:, b, :]
                    step(nc.vector.tensor_scalar(x, x, mv[:, b, 0:1], root[:, b:b + 1], ALU.subtract, ALU.mult))
                    step(nc.vector.tensor_tensor(x, x, gb[:, 0, :], ALU.mult))
                    nc.vector.tensor_tensor(x, x, gb[:, 1, :], ALU.add).then_inc(x_done, 1)
                    if h_tok is not None:
                        cond = b // (NB - 1)
                        dve.wait_ge(x_done, b + 1)
                        step(nc.vector.tensor_tensor(h_tok[:, b, :], x, vec[:, cond, 1, :], ALU.mult))
                        step(nc.vector.tensor_tensor(h_tok[:, b, :], h_tok[:, b, :], vec[:, cond, 0, :], ALU.add))


def peer_queries(nc, l, T, h_t, q_t, ring):
    def evac(c):
        def f(eng, ps, m, step):
            return nc.scalar.activation(q_t[:, 4 * c + m, :], ps[:, 0:TOK], ACT.Copy)
        return f
    projections(nc, "pq", [Job(T["peer_wq"][bass.ds(l, 1), c].rearrange("a p k n -> (a p) k n"), h_t, True, "scalar", evac(c))
                           for c in range(4)], ring)


def routing(nc, l, T, q_t, index, gate):
    S = 2 * PH
    with ExitStack() as ctx:
        def sb(name, shape, dt=F32):
            return ctx.enter_context(nc.sbuf_tensor(name, shape, dt))
        keys = sb("ro_keys", [P, S, P])
        sc = [sb(f"ro_sc{i}", [P, S, P]) for i in range(2)]
        cut = sb("ro_cut", [P, S, P])
        top, top_i = sb("ro_top", [P, S, TOPK]), sb("ro_topi", [P, S, TOPK], U32)
        top_f = sb("ro_topf", [P, S, TOPK])
        cand, cand2 = sb("ro_cand", [P, PH, TOPK * TOPK]), sb("ro_cand2", [P, PH, TOPK * TOPK])
        best, pos = sb("ro_best", [P, PH, TOPK]), sb("ro_pos", [P, PH, TOPK], U32)
        part_u = sb("ro_part_u", [P, 2, PH, TOPK], U32)
        part_f = sb("ro_part_f", [P, 2, PH, TOPK])
        iota, base = sb("ro_iota", [P, TOPK]), sb("ro_base", [P, DEPTH])
        hit = sb("ro_hit", [P, PH, TOPK, TOPK])
        num = sb("ro_num", [P, 2, PH, TOPK])
        total = sb("ro_total", [P, PH])
        psum = [ctx.enter_context(nc.psum_tensor(f"ro_ps{i}", [P, S * P], F32)) for i in range(2)]
        with stage(nc, "ro_in", "ro_dve", "ro_mm", "ro_sc", "ro_used", "ro_cent", "ro_exp") as (
                block, (loaded, dve_steps, scored, copied, used, centred, exped)):
            @block.sync
            def _(sp):
                sp.dma_start(keys[:], T["peer_keys"][bass.ds(l, 1)].rearrange("a p s n -> (a p) s n")).then_inc(loaded, 16)
                sp.dma_start(iota[:], T["iota"]).then_inc(loaded, 16)
                sp.dma_start(base[:], T["base"]).then_inc(loaded, 16)

            @block.tensor
            def _(pe):
                pe.wait_ge(loaded, 48)
                for b in range(NB):
                    if b >= 2:
                        pe.wait_ge(copied, b - 1)
                    for s in range(S):
                        last = nc.tensor.matmul(psum[b % 2][:, s * P:(s + 1) * P], q_t[:, s, b * P:(b + 1) * P], keys[:, s, :],
                                                start=True, stop=True)
                    last.then_inc(scored, 1)

            @block.scalar
            def _(act):
                for b in range(NB):
                    act.wait_ge(scored, b + 1)
                    if b >= 2:
                        act.wait_ge(used, b - 1)
                    act.activation(sc[b % 2][:].rearrange("p s n -> p (s n)"), psum[b % 2][:], ACT.Copy).then_inc(copied, 1)
                    act.wait_ge(centred, b + 1)
                    act.activation(gate[:, b, :], gate[:, b, :], ACT.Exp).then_inc(exped, 1)

            @block.vector
            def _(dve):
                step = Steps(dve, dve_steps)
                V = nc.vector

                def top16(lists, values, positions, scratch):
                    for v, i, x, y in zip(values, positions, lists, scratch):
                        last = V.max(v[:, 0:8], x)
                    step(last)
                    for v, i, x, y in zip(values, positions, lists, scratch):
                        V.max_index(i[:, 0:8], v[:, 0:8], x)
                        last = V.match_replace(y, v[:, 0:8], x, LOWEST)
                    step(last)
                    for v, i, x, y in zip(values, positions, lists, scratch):
                        last = V.max(v[:, 8:16], y)
                    step(last)
                    for v, i, x, y in zip(values, positions, lists, scratch):
                        last = V.max_index(i[:, 8:16], v[:, 8:16], y)
                    step(last)

                dve.wait_ge(loaded, 48)
                for b in range(NB):
                    x = sc[b % 2]
                    dve.wait_ge(copied, b + 1)
                    top16([x[:, s, :] for s in range(S)], [top[:, s, :] for s in range(S)], [top_i[:, s, :] for s in range(S)],
                          [cut[:, s, :] for s in range(S)])
                    dve.sem_inc(used, 1)
                    step(V.tensor_copy(top_f[:], top_i[:]))
                    pair = top[:].rearrange("p (h a) k -> p a h k", a=2)
                    pair_f = top_f[:].rearrange("p (h a) k -> p a h k", a=2)
                    for h in range(PH):
                        last = V.tensor_tensor(cand[:, h, :].rearrange("p (i j) -> p i j", i=TOPK),
                                               top[:, 2 * h, :].unsqueeze(2).to_broadcast([P, TOPK, TOPK]),
                                               top[:, 2 * h + 1, :].unsqueeze(1).to_broadcast([P, TOPK, TOPK]), ALU.add)
                    step(last)
                    top16([cand[:, h, :] for h in range(PH)], [best[:, h, :] for h in range(PH)], [pos[:, h, :] for h in range(PH)],
                          [cand2[:, h, :] for h in range(PH)])
                    V.tensor_tensor(gate[:, b, :].rearrange("p (h k) -> p h k", h=PH), best[:],
                                    best[:, :, 0:1].to_broadcast([P, PH, TOPK]), ALU.subtract).then_inc(centred, 1)
                    V.tensor_scalar(part_u[:, 0], pos[:], 4, None, ALU.logical_shift_right)
                    step(V.tensor_scalar(part_u[:, 1], pos[:], 15, None, ALU.bitwise_and))
                    step(V.tensor_copy(part_f[:], part_u[:]))
                    for a in range(2):
                        for h in range(PH):
                            last = V.tensor_tensor(hit[:, h], part_f[:, a, h, :].unsqueeze(2).to_broadcast([P, TOPK, TOPK]),
                                                   iota[:].unsqueeze(1).to_broadcast([P, TOPK, TOPK]), ALU.is_equal)
                        step(last)
                        for h in range(PH):
                            last = V.tensor_tensor(hit[:, h], hit[:, h], top_f[:, 2 * h + a, :].unsqueeze(1).to_broadcast([P, TOPK, TOPK]), ALU.mult)
                        step(last)
                        step(V.tensor_reduce(num[:, a], hit[:], AX.X, ALU.add))
                    step(V.scalar_tensor_tensor(num[:, 0], num[:, 0], float(P), num[:, 1], ALU.mult, ALU.add))
                    step(V.tensor_scalar(index[:, b, :], num[:, 0].rearrange("p h k -> p (h k)"), base[:, bass.ds(l, 1)], None, ALU.add))
                    dve.wait_ge(exped, b + 1)
                    g = gate[:, b, :].rearrange("p (h k) -> p h k", h=PH)
                    step(V.tensor_reduce(total[:], g, AX.X, ALU.add))
                    step(V.reciprocal(total[:], total[:]))
                    step(V.tensor_tensor(g, g, total[:].unsqueeze(2).to_broadcast([P, PH, TOPK]), ALU.mult))


def experts(nc, l, T, h_tok, y_tok, index, gate, ident, u_in, v_in, ring):
    pairs = PH // 2
    with ExitStack() as ctx:
        def sb(name, shape):
            return ctx.enter_context(nc.sbuf_tensor(name, shape, F32))
        rooms = [r[:].rearrange("p k n -> p (k n)") for r in ring]
        u_row = [rooms[s // 4][:, (s % 4) * D:(s % 4 + 1) * D] for s in range(8)]
        u_row += [sb(f"ex_u{s}", [P, D])[:] for s in range(8, TOPK)]
        v_row = [sb(f"ex_v{s}", [P, D])[:] for s in range(TOPK)]
        h_now = sb("ex_h", [P, D])
        idx_now = [ctx.enter_context(nc.sbuf_tensor(f"ex_i{j}", [P, TOPK], U32)) for j in range(2)]
        dot = [sb(f"ex_dot{j}", [P, TOPK]) for j in range(2)]
        act_v = [sb(f"ex_act{j}", [P, TOPK]) for j in range(2)]
        wgt = [sb(f"ex_w{j}", [P, TOPK]) for j in range(2)]
        DIAGS = 4
        diag = [sb(f"ex_diag{i}", [P, P]) for i in range(DIAGS)]
        zero = sb("ex_zero", [P, 512])
        ps_y = ctx.enter_context(nc.psum_tensor("ex_ps_y", [P, D], F32))
        index_all = index[:].rearrange("p b s -> p (b s)")
        gate_all = gate[:].rearrange("p b s -> p (b s)")
        with stage(nc, "ex_hnow", "ex_idx", "ex_udone", "ex_vdone", "ex_gelu", "ex_wgt", "ex_diagd", "ex_ydone", "ex_yout", "ex_zeroed", "ex_going") as (
                block, (h_ready, idx_ready, u_used, v_used, gelu_done, w_ready, diag_ready, y_done, y_out, zeroed, going)):

            def layer_units(n):
                return (l * (NB * PH) + n) * 16 + 16

            @block.gpsimd
            def _(pool):
                pool.wait_ge(zeroed, 1)
                with pool.Fori(0, NB * pairs) as i:
                    for j in range(2):
                        n = 2 * i + j
                        nc.gpsimd.tensor_copy(idx_now[j][:], index_all[:, bass.ds(TOPK * n, TOPK)]).then_inc(idx_ready, 1)
                        for rows, arrived, used, table in ((u_row, u_in, u_used, T["peer_u"]), (v_row, v_in, v_used, T["peer_v"])):
                            for s in range(TOPK):
                                if s % 4 == 0:
                                    pool.wait_ge(used, TOPK * n + s + 4)
                                    if s == 0 and rows is u_row:
                                        pool.wait_ge(idx_ready, n + 1)
                                    pool.sem_inc(going, 1)
                                nc.gpsimd.indirect_dma_start(rows[s], None, table, bass.IndirectOffsetOnAxis(ap=idx_now[j][:, s:s + 1], axis=0)).then_inc(arrived[s], 16)

            @block.vector
            def _(dve):
                nc.vector.memset(zero[:], 0.0).then_inc(zeroed, 1)
                dve.sem_inc(u_used, TOPK)
                with dve.Fori(0, NB) as b:
                    nc.vector.tensor_copy(h_now[:], h_tok[:, bass.ds(b, 1), :].rearrange("p a n -> p (a n)")).then_inc(h_ready, 1)
                    with dve.Fori(0, pairs) as i:
                        for j in range(2):
                            n = PH * b + 2 * i + j
                            dve.wait_ge(h_ready, b + 1)
                            for s in range(TOPK):
                                dve.wait_ge(u_in[s], layer_units(n))
                                nc.vector.tensor_tensor_reduce(out=u_row[s], in0=u_row[s], in1=h_now[:], scale=1.0, scalar=0.0,
                                                               op0=ALU.mult, op1=ALU.add, accum_out=dot[j][:, s:s + 1]).then_inc(u_used, 1)
                            dve.wait_ge(gelu_done, n + 1)
                            nc.vector.tensor_tensor(wgt[j][:], act_v[j][:], gate_all[:, bass.ds(TOPK * n, TOPK)], ALU.mult).then_inc(w_ready, 1)

            @block.scalar
            def _(act):
                with act.Fori(0, NB) as b:
                    with act.Fori(0, pairs) as i:
                        for j in range(2):
                            n = PH * b + 2 * i + j
                            act.wait_ge(u_used, TOPK * n + 2 * TOPK)
                            act.activation(act_v[j][:], dot[j][:], ACT.Gelu).then_inc(gelu_done, 1)
                            act.wait_ge(w_ready, n + 1)
                            for s in range(TOPK):
                                act.wait_ge(v_used, TOPK * n + s + 1 + TOPK - DIAGS)
                                act.activation(diag[s % DIAGS][:], ident[:], ACT.Copy, scale=wgt[j][:, s:s + 1]).then_inc(diag_ready, 1)
                    act.wait_ge(y_done, b + 1)
                    act.activation(y_tok[:, bass.ds(b, 1), :].rearrange("p a n -> p (a n)"), ps_y[:], ACT.Copy).then_inc(y_out, 1)

            @block.tensor
            def _(pe):
                pe.sem_inc(v_used, TOPK)
                pe.sem_inc(y_out, 1)
                pe.wait_ge(zeroed, 1)
                with pe.Fori(0, NB) as b:
                    pe.wait_ge(y_out, b + 1)
                    for c in (0, 512):
                        nc.tensor.matmul(ps_y[:, c:c + 512], zero[:, 0:P], zero[:], start=True, stop=False)
                    with pe.Fori(0, pairs) as i:
                        for j in range(2):
                            n = PH * b + 2 * i + j
                            for s in range(TOPK):
                                pe.wait_ge(v_in[s], layer_units(n))
                                pe.wait_ge(diag_ready, TOPK * n + s + 1)
                                for c in (0, 512):
                                    last = nc.tensor.matmul(ps_y[:, c:c + 512], diag[s % DIAGS][:], v_row[s][:, c:c + 512], start=False, stop=False)
                                last.then_inc(v_used, 1)
                    for c in (0, 512):
                        last = nc.tensor.matmul(ps_y[:, c:c + 512], zero[:, 0:P], zero[:], start=False, stop=True)
                    last.then_inc(y_done, 1)


def token_rows(x_rows):
    return lambda b: x_rows[b * P:(b + 1) * P, :]


def copy_rows(nc, name, pairs):
    with stage(nc, f"{name}_done") as (block, (done,)):
        @block.sync
        def _(sp):
            for dst, src in pairs:
                sp.dma_start(dst, src).then_inc(done, 16)
            sp.wait_ge(done, 16 * len(pairs))


def trunk(nc, T, depth=DEPTH, stop=None):
    with ExitStack() as ctx:
        def sb(name, shape):
            return ctx.enter_context(nc.sbuf_tensor(name, shape, F32))
        ident = sb("ident", [P, P])
        h_t = sb("h_t", [P, KT, TOK])
        ring = [sb(f"ring{i}", [P, KT, CHUNK]) for i in range(2)]
        u_in = [ctx.enter_context(nc.semaphore(f"u_in{s}")) for s in range(TOPK)]
        v_in = [ctx.enter_context(nc.semaphore(f"v_in{s}")) for s in range(TOPK)]
        copy_rows(nc, "start", [(T["x_rows"][0:LAT, :], T["x_sample"]), (T["x_rows"][LAT:TOK, :], T["x_prompt"]), (ident[:], T["ident"])])
        with nc.Fori(0, depth) as l:
            modulation(nc, l, T, ring)
            modulate_and_transpose(nc, T, token_rows(T["x_rows"]), h_t, ident, 0)
            if stop == "mod": return
            with ExitStack() as mixer:
                merged_t = mixer.enter_context(nc.sbuf_tensor("merged_t", [P, KT, TOK], F32))
                branch_t = mixer.enter_context(nc.sbuf_tensor("branch_t", [P, KT, TOK], F32))
                conv_branch(nc, l, T, h_t, branch_t, ring)
                if stop == "conv": return
                merge_branch(nc, l, T, "mg1", 1, h_t, branch_t, merged_t, ring)
                with ExitStack() as inner:
                    o_tok = inner.enter_context(nc.sbuf_tensor("o_tok", [P, NB, D], F32))
                    attention(nc, l, T, h_t, branch_t, o_tok, ring, ident)
                    if stop == "attcore": return
                    normalise(nc, "attn", o_tok, T["subln"][bass.ds(l, 1), :], T["lam_keep"][bass.ds(l, 1)].rearrange("a p n -> (a p) n"))
                    to_channel_major(nc, "attt", o_tok, branch_t, ident)
                    if stop == "att": return
                    merge_branch(nc, l, T, "mg0", 0, h_t, branch_t, merged_t, ring)
                    recurrent_branch(nc, l, T, h_t, branch_t, o_tok, ring, ident)
                    to_channel_major(nc, "rect", o_tok, branch_t, ident)
                    if stop == "rec": return
                    merge_branch(nc, l, T, "mg2", 2, h_t, branch_t, merged_t, ring)
                y_tok = branch_t[:].rearrange("p k t -> p (k t)").rearrange("p (b n) -> p b n", b=NB)
                output_projection(nc, l, T, merged_t, y_tok, ring)
                if stop == "mix": return
                with ExitStack() as norm:
                    x_tok = norm.enter_context(nc.sbuf_tensor("x_tok1", [P, NB, D], F32))
                    h_tok = norm.enter_context(nc.sbuf_tensor("h_tok1", [P, NB, D], F32))
                    rows = token_rows(T["x_rows"])
                    residual_norm(nc, l, T, "ln1", 0, y_tok, x_tok, rows, h_tok, None, rows)
                    to_channel_major(nc, "ht", h_tok, h_t, ident)
                    copy_rows(nc, "h_out", [(T["h_rows"].rearrange("(b p) n -> p b n", p=P), h_tok[:])])
            with ExitStack() as peer:
                index = peer.enter_context(nc.sbuf_tensor("index", [P, NB, PH * TOPK], U32))
                gate = peer.enter_context(nc.sbuf_tensor("gate", [P, NB, PH * TOPK], F32))
                with ExitStack() as inner:
                    q_t = inner.enter_context(nc.sbuf_tensor("peer_q", [P, 2 * PH, TOK], F32))
                    peer_queries(nc, l, T, h_t, q_t, ring)
                    routing(nc, l, T, q_t, index, gate)
                if stop == "route": return
                y_tok = h_t[:].rearrange("p k t -> p (k t)").rearrange("p (b n) -> p b n", b=NB)
                with ExitStack() as inner:
                    h_tok = inner.enter_context(nc.sbuf_tensor("h_tok2", [P, NB, D], F32))
                    copy_rows(nc, "h_in", [(h_tok[:], T["h_rows"].rearrange("(b p) n -> p b n", p=P))])
                    experts(nc, l, T, h_tok, y_tok, index, gate, ident, u_in, v_in, ring)
            if stop == "experts": return
            with ExitStack() as norm:
                x_tok = norm.enter_context(nc.sbuf_tensor("x_tok2", [P, NB, D], F32))
                rows = token_rows(T["x_rows"])
                residual_norm(nc, l, T, "ln2", 1, y_tok, x_tok, rows, None, 5, rows)
        copy_rows(nc, "end", [(T["y_sample"], T["x_rows"][0:LAT, :]), (T["y_prompt"], T["x_rows"][LAT:TOK, :])])


def constants():
    eye = np.eye(P, dtype=np.float32)
    levels = np.zeros((2, P, LEVELS + 1, P), np.float32)
    mask = np.zeros((2, P, LEVELS + 1, P), np.float32)
    s, t = np.meshgrid(np.arange(P), np.arange(P), indexing="ij")
    for a in range(LEVELS):
        half = 1 << a
        mid = (t // (2 * half)) * (2 * half) + half
        levels[0, :, a, :] = np.where(t >= mid, (s >= mid) & (s <= t), (s > t) & (s < mid))
        mask[0, :, a, :] = (s // (2 * half) == t // (2 * half)) & (s < mid) & (t >= mid)
    levels[0, :, LEVELS, :] = s <= t
    mask[0, :, LEVELS, :] = s == t
    suffix = np.stack([s > t, s < t]).astype(np.float32)
    levels[1], mask[1] = levels[0, ::-1, :, ::-1], mask[0, ::-1, :, ::-1]
    half, quarter = QK // 2, QK // 4
    freqs = (10000.0 ** (-np.arange(0, half, 2, dtype=np.float32) / np.float32(half))).astype(np.float32)
    tok = np.arange(LAT)
    cos, sin = np.zeros((P, LAT), np.float32), np.zeros((P, LAT), np.float32)
    rot = np.zeros((P, P), np.float32)
    for c in range(P):
        axis, place = (c % QK) // half, c % half
        ang = (tok // GRID_W if axis == 0 else tok % GRID_W).astype(np.float32) * freqs[place % quarter]
        cos[c], sin[c] = np.cos(ang), np.sin(ang)
        if place < quarter:
            rot[c + quarter, c] = -1.0
        else:
            rot[c - quarter, c] = 1.0
    ones = np.ones((P, 1), np.float32)
    return {
        "ident": eye, "levels": levels, "suffix": suffix, "mask": mask, "cos": cos, "sin": sin, "rot": rot,
        "lam0": ones * np.array(LAM_INIT, np.float32), "sel": ones * np.arange(DEPTH, dtype=np.float32),
        "lam_keep": np.stack([ones * np.float32(1.0 - x) for x in LAM_INIT]),
        "iota": ones * np.arange(TOPK, dtype=np.float32), "base": ones * (EXPERTS * np.arange(DEPTH, dtype=np.float32)),
    }


def layouts(a):
    def chunks(w):
        *lead, d, n = w.shape
        w = w.reshape(*lead, KT, P, n // CHUNK, CHUNK)
        r = len(lead)
        return w.transpose(*range(r), r + 2, r + 1, r, r + 3)

    conv = np.concatenate([a["conv_w"], a["conv_b"][:, None, :]], axis=1)
    return {
        "x_sample": a["x_sample"].reshape(LAT, D), "x_prompt": a["x_prompt"].reshape(CTX, D),
        "cond": np.stack([a["c"].reshape(KT, P), a["c_ctx"].reshape(KT, P)]).transpose(2, 1, 0),
        "kc": a["cache_attn_k"][0].transpose(0, 3, 2, 1), "vc": a["cache_attn_v"][0].reshape(DEPTH, CTX, D),
        "state": a["state_hgrn"][0].transpose(0, 1, 3, 2, 4).reshape(DEPTH, 2, P, D),
        "mod_w": chunks(a["mod_w"]), "mod_b": a["mod_b"], "w_in": chunks(a["w_in"]), "lam": a["attn_lambda"],
        "subln": a["attn_subln"], "conv": conv.reshape(DEPTH, 4, KT, P).transpose(0, 3, 2, 1), "rec_lb": a["rec_lb"],
        "rec_norm": a["rec_norm"], "w_branch": chunks(a["w_branch"]), "w_out": chunks(a["w_out"]), "ln_g": a["ln_g"],
        "ln_b": a["ln_b"], "peer_wq": chunks(a["peer_wq"]),
        "peer_keys": a["peer_keys"].reshape(DEPTH, 2 * PH, P, P).transpose(0, 3, 1, 2),
        "peer_u": a["peer_u"].reshape(DEPTH * EXPERTS, D), "peer_v": a["peer_v"].reshape(DEPTH * EXPERTS, D),
    }


OUTPUTS = {"y_prompt": (CTX, D), "y_sample": (LAT, D), "new_k": (DEPTH, CTX, D), "new_v": (DEPTH, CTX, D),
           "new_state": (DEPTH, 2, P, D)}
SCRATCH = {"x_rows": (TOK, D), "h_rows": (TOK, D), "mod_rows": (2, 6 * D)}


def build(nc, arrays, depth=DEPTH, stop=None):
    tensors = {n: nc.dram_tensor(f"in_{n}", a.shape, F32, kind="ExternalInput").ap() for n, a in arrays.items()}
    tensors.update({n: nc.dram_tensor(f"out_{n}", s, F32, kind="ExternalOutput").ap() for n, s in OUTPUTS.items()})
    tensors.update({n: nc.dram_tensor(n, s, F32, kind="Internal").ap() for n, s in SCRATCH.items()})
    trunk(nc, tensors, depth, stop)


def kernel(**inputs):
    import concourse.bacc as bacc
    from concourse.bass_utils import run_bass_kernel_spmd

    arrays = layouts({k: np.asarray(v) for k, v in inputs.items()})
    arrays.update(constants())
    arrays = {k: np.ascontiguousarray(v) for k, v in arrays.items()}
    nc = bacc.Bacc("TRN2", target_bir_lowering=False, num_devices=1)
    build(nc, arrays)
    got = run_bass_kernel_spmd(nc, [{f"in_{k}": a for k, a in arrays.items()}], core_ids=[0]).results[0]
    out = {n: got[f"out_{n}"] for n in OUTPUTS}
    state = out["new_state"].reshape(DEPTH, 2, P, HEADS, P).transpose(0, 1, 3, 2, 4)
    return (out["y_prompt"].reshape(1, CTX, D), out["y_sample"].reshape(1, LAT, D),
            out["new_k"].reshape(1, DEPTH, CTX, HEADS, P), out["new_v"].reshape(1, DEPTH, CTX, HEADS, P),
            np.ascontiguousarray(state)[None])
```

```python
import math
from contextlib import ExitStack, contextmanager

import numpy as np
import concourse.bass as bass
from concourse import mybir

F32 = mybir.dt.float32
U32 = mybir.dt.uint32
ALU = mybir.AluOpType
ACT = mybir.ActivationFunctionType
AX = mybir.AxisListType

P = 128
D = 1024
KT = D // P
DEPTH = 2
LAT = 512
CTX = 128
TOK = LAT + CTX
NB = TOK // P
CHUNK = 512
HEADS = 8
QK = 64
SCALE = QK ** -0.5
LEVELS = 7
EXPERTS = 128 * 128
PH = 8
TOPK = 16
EPS = 1e-5
ALPHA = (2 * DEPTH) ** 0.25
LOWEST = -3.0e38
TINY = 2.0 ** -63
GRID_W = 64
LAM_INIT = [0.8 - 0.6 * math.exp(-0.3 * l) for l in range(DEPTH)]
ZQ, ZK, ZV, ZB, ZC, ZX, RQ, RFF, RFB, RI, RG, ZG = 0, 2, 4, 6, 8, 10, 12, 14, 16, 18, 20, 22


class Steps:

    def __init__(self, eng, sem, base=0):
        self.eng, self.sem, self.base, self.n = eng, sem, base, 0

    def mark(self, ins):
        self.n += 1
        ins.then_inc(self.sem, 1)
        return self.base + self.n

    def __call__(self, ins):
        self.eng.wait_ge(self.sem, self.mark(ins))


@contextmanager
def stage(nc, *names):
    with ExitStack() as ctx:
        sems = [ctx.enter_context(nc.semaphore(n)) for n in names]
        nums = sorted(s.num for s in sems)
        starts = [n for n in nums if n - 1 not in nums]
        ends = [n + 1 for n in nums if n + 1 not in nums]
        with nc.Block(no_gpsimd_drain=True) as block:
            yield block, sems
        for a, b in zip(starts, ends):
            nc.all_engine_barrier(sems_to_clear=range(a, b))


class Job:

    def __init__(self, weights, act_t, channel_major, engine, evac):
        self.weights, self.act_t, self.channel_major = weights, act_t, channel_major
        self.engine, self.evac = engine, evac
        self.tiles = CHUNK // P if channel_major else NB


def projections(nc, name, jobs, ring):
    tiles = [(c, m) for c, job in enumerate(jobs) for m in range(job.tiles)]
    done_through = [sum(j.tiles for j in jobs[:c + 1]) for c in range(len(jobs))]
    with ExitStack() as ctx:
        psum = [ctx.enter_context(nc.psum_tensor(f"{name}_ps{i}", [P, 1024], F32)) for i in range(4)]
        PIECES = 4
        with stage(nc, f"{name}_w0", f"{name}_w1", f"{name}_tile", f"{name}_free0", f"{name}_free1",
                   f"{name}_free2", f"{name}_free3", f"{name}_dve", f"{name}_act",
                   *[f"{name}_first{i}" for i in range(PIECES)]) as (block, sems):
            w_loaded, tile_done, slot_free = sems[0:2], sems[2], sems[3:7]
            dve_steps, act_steps, first_loaded = sems[7], sems[8], sems[9:]

            @block.sync
            def _(sp):
                n = KT // PIECES
                for i in range(PIECES):
                    sp.dma_start(ring[0][:, n * i:n * i + n, :], jobs[0].weights[:, n * i:n * i + n, :]).then_inc(first_loaded[i], 16)
                for c, job in enumerate(jobs[1:], 1):
                    if c >= 2:
                        sp.wait_ge(tile_done, done_through[c - 2])
                    sp.dma_start(ring[c % 2][:], job.weights).then_inc(w_loaded[c % 2], 16)

            @block.tensor
            def _(pe):
                n_piece = KT // PIECES
                for t, (c, m) in enumerate(tiles):
                    job, w, ps = jobs[c], ring[c % 2], psum[t % 4]
                    if m == 0 and c > 0:
                        pe.wait_ge(w_loaded[c % 2], 16 * ((c + 1) // 2 if c % 2 else c // 2))
                    if t >= 4:
                        pe.wait_ge(slot_free[t % 4], t // 4)
                    if job.channel_major:
                        for t0, t1 in ((0, LAT), (LAT, TOK)):
                            for k in range(KT):
                                if t == 0 and t0 == 0 and k % n_piece == 0:
                                    pe.wait_ge(first_loaded[k // n_piece], 16)
                                last = nc.tensor.matmul(ps[:, t0:t1], w[:, k, m * P:(m + 1) * P],
                                                        job.act_t[:, k, t0:t1], start=k == 0, stop=k == KT - 1)
                    else:
                        for k in range(KT):
                            if t == 0 and k % n_piece == 0:
                                pe.wait_ge(first_loaded[k // n_piece], 16)
                            last = nc.tensor.matmul(ps[:, 0:CHUNK], job.act_t[:, k, m * P:(m + 1) * P],
                                                    w[:, k, :], start=k == 0, stop=k == KT - 1)
                    last.then_inc(tile_done, 1)

            def evacuate(eng, which, steps):
                for t, (c, m) in enumerate(tiles):
                    if jobs[c].engine == which:
                        eng.wait_ge(tile_done, t + 1)
                        jobs[c].evac(eng, psum[t % 4], m, steps).then_inc(slot_free[t % 4], 1)

            @block.scalar
            def _(act):
                evacuate(act, "scalar", Steps(act, act_steps))

            @block.vector
            def _(dve):
                evacuate(dve, "vector", Steps(dve, dve_steps))


def modulation(nc, l, T, ring):
    with ExitStack() as ctx:
        cond = ctx.enter_context(nc.sbuf_tensor("cond", [P, KT, 2], F32))
        csilu = ctx.enter_context(nc.sbuf_tensor("csilu", [P, KT, 2], F32))
        bias = ctx.enter_context(nc.sbuf_tensor("mod_bias", [2, 6 * D], F32))
        rows = ctx.enter_context(nc.sbuf_tensor("mod_rows_sb", [2, 6 * D], F32))
        psum = [ctx.enter_context(nc.psum_tensor(f"mod_ps{i}", [P, 512], F32)) for i in range(2)]
        n = 6 * D // CHUNK
        with stage(nc, "mod_w0", "mod_w1", "mod_in", "mod_silu", "mod_tile", "mod_free", "mod_out") as (block, sems):
            w_loaded, cond_in, silu_done, tile_done, slot_free, rows_out = sems[0:2], *sems[2:]

            @block.sync
            def _(sp):
                sp.dma_start(cond[:], T["cond"]).then_inc(cond_in, 16)
                sp.dma_start(bias[:], T["mod_b"][bass.ds(l, 1), :].to_broadcast([2, 6 * D])).then_inc(cond_in, 16)
                for c in range(2):
                    sp.dma_start(ring[c][:], T["mod_w"][bass.ds(l, 1), c].rearrange("a p k n -> (a p) k n")).then_inc(w_loaded[c], 16)
                with sp.Fori(1, n // 2) as i:
                    for j in range(2):
                        sp.wait_ge(tile_done, 2 * i + j - 1)
                        sp.dma_start(ring[j][:], T["mod_w"][bass.ds(l, 1), bass.ds(2 * i + j, 1)].rearrange(
                            "a b p k n -> (a b p) k n")).then_inc(w_loaded[j], 16)
                sp.wait_ge(slot_free, 2 + n)
                sp.dma_start(T["mod_rows"], rows[:]).then_inc(rows_out, 16)
                sp.wait_ge(rows_out, 16)

            @block.scalar
            def _(act):
                act.wait_ge(cond_in, 32)
                act.activation(csilu[:], cond[:], ACT.Silu).then_inc(silu_done, 1)

            @block.tensor
            def _(pe):
                pe.wait_ge(silu_done, 1)
                with pe.Fori(0, n // 2) as i:
                    for j in range(2):
                        pe.wait_ge(w_loaded[j], 16 * i + 16)
                        pe.wait_ge(slot_free, 2 * i + j + 1)
                        for k in range(KT):
                            last = nc.tensor.matmul(psum[j][0:2, :], csilu[:, k, :], ring[j][:, k, :],
                                                    start=k == 0, stop=k == KT - 1)
                        last.then_inc(tile_done, 1)

            @block.vector
            def _(dve):
                dve.sem_inc(slot_free, 2)
                dve.wait_ge(cond_in, 32)
                with dve.Fori(0, n // 2) as i:
                    for j in range(2):
                        cols = bass.ds((2 * i + j) * CHUNK, CHUNK)
                        dve.wait_ge(tile_done, 2 * i + j + 1)
                        nc.vector.tensor_tensor(rows[:, cols], psum[j][0:2, :], bias[:, cols], ALU.add).then_inc(slot_free, 1)


def mod_row(T, cond, part):
    return T["mod_rows"][cond:cond + 1, part * D:(part + 1) * D].to_broadcast([P, D])


def modulate_and_transpose(nc, T, x_src, h_t, ident, first_part, h_keep=None):
    with ExitStack() as ctx:
        xb = [ctx.enter_context(nc.sbuf_tensor(f"mt_x{i}", [P, D], F32)) for i in range(NB)]
        vec = ctx.enter_context(nc.sbuf_tensor("mt_vec", [P, 2, 2, D], F32))
        psum = [ctx.enter_context(nc.psum_tensor(f"mt_ps{i}", [P, D], F32)) for i in range(2)]
        with stage(nc, "mt_x", "mt_vec_in", "mt_dve", "mt_tp", "mt_ev") as (block, (x_in, vec_in, dve_steps, transposed, copied)):

            @block.sync
            def _(sp):
                for cond in range(2):
                    for j in range(2):
                        sp.dma_start(vec[:, cond, j, :], mod_row(T, cond, first_part + j)).then_inc(vec_in, 16)
                for b in range(NB):
                    sp.dma_start(xb[b][:], x_src(b)).then_inc(x_in, 16)

            @block.vector
            def _(dve):
                step = Steps(dve, dve_steps)
                dve.wait_ge(vec_in, 64)
                dve.wait_ge(x_in, 16 * NB)
                step(nc.vector.tensor_scalar(vec[:, :, 1, :], vec[:, :, 1, :], 1.0, None, ALU.add))
                for b in range(NB):
                    cond = b // (NB - 1)
                    step(nc.vector.tensor_tensor(xb[b][:], xb[b][:], vec[:, cond, 1, :], ALU.mult))
                    step(nc.vector.tensor_tensor(xb[b][:], xb[b][:], vec[:, cond, 0, :], ALU.add))

            @block.tensor
            def _(pe):
                for b in range(NB):
                    pe.wait_ge(dve_steps, 3 + 2 * b)
                    if b >= 2:
                        pe.wait_ge(copied, b - 1)
                    for k in range(KT):
                        last = nc.tensor.transpose(psum[b % 2][:, k * P:(k + 1) * P], xb[b][:, k * P:(k + 1) * P], ident[:])
                    last.then_inc(transposed, 1)

            @block.scalar
            def _(act):
                for b in range(NB):
                    act.wait_ge(transposed, b + 1)
                    act.activation(h_t[:, :, b * P:(b + 1) * P],
                                   psum[b % 2][:].rearrange("p (k t) -> p k t", k=KT), ACT.Copy).then_inc(copied, 1)


def merge_branch(nc, l, T, name, branch, h_t, branch_t, merged_t, ring):
    with ExitStack() as ctx:
        sig = ctx.enter_context(nc.sbuf_tensor(f"{name}_sig", [P, D // P, TOK], F32))

        def gate(c):
            def evac(eng, ps, m, step):
                return nc.scalar.activation(sig[:, 4 * c + m, :], ps[:, 0:TOK], ACT.Sigmoid)
            return evac

        def product(c):
            def evac(eng, ps, m, step):
                t = 4 * c + m
                if branch == 1:
                    return nc.vector.tensor_tensor(merged_t[:, t, :], ps[:, 0:TOK], sig[:, t, :], ALU.mult)
                step(nc.vector.tensor_tensor(sig[:, t, :], ps[:, 0:TOK], sig[:, t, :], ALU.mult))
                return nc.vector.tensor_tensor(merged_t[:, t, :], merged_t[:, t, :], sig[:, t, :], ALU.add)
            return evac

        jobs = [Job(w_in(T, l, ZG + 2 * branch + c), h_t, True, "scalar", gate(c)) for c in range(2)]
        jobs += [Job(T["w_branch"][bass.ds(l, 1), branch, c].rearrange("a p k n -> (a p) k n"), branch_t, True,
                     "vector", product(c)) for c in range(2)]
        projections(nc, name, jobs, ring)


def w_in(T, l, c):
    return T["w_in"][bass.ds(l, 1), c].rearrange("a p k n -> (a p) k n")


def conv_branch(nc, l, T, h_t, out_t, ring):
    PAD = TOK + 4
    with ExitStack() as ctx:
        u = ctx.enter_context(nc.sbuf_tensor("conv_u", [P, KT, PAD], F32))
        y = ctx.enter_context(nc.sbuf_tensor("conv_y", [P, KT, PAD], F32))
        cw = ctx.enter_context(nc.sbuf_tensor("conv_w_sb", [P, KT, 4], F32))

        def parts(t):
            return ((t[:, 1:1 + LAT], 0, LAT), (t[:, LAT + 3:LAT + 3 + CTX], LAT, TOK))

        def keep_c(c):
            def evac(eng, ps, m, step):
                return nc.scalar.activation(out_t[:, 4 * c + m, :], ps[:, 0:TOK], ACT.Copy)
            return evac

        def times_c(c):
            def evac(eng, ps, m, step):
                for dst, t0, t1 in parts(u[:, 4 * c + m, :]):
                    last = nc.vector.tensor_tensor(dst, ps[:, t0:t1], out_t[:, 4 * c + m, t0:t1], ALU.mult)
                return last
            return evac

        def times_b(c):
            def evac(eng, ps, m, step):
                for src, t0, t1 in parts(y[:, 4 * c + m, :]):
                    last = nc.vector.tensor_tensor(out_t[:, 4 * c + m, t0:t1], ps[:, t0:t1], src, ALU.mult)
                return last
            return evac

        projections(nc, "convu", [Job(w_in(T, l, ZC + c), h_t, True, "scalar", keep_c(c)) for c in range(2)]
                    + [Job(w_in(T, l, ZX + c), h_t, True, "vector", times_c(c)) for c in range(2)], ring)
        with stage(nc, "conv_in", "conv_pad", "conv_dve") as (block, (w_loaded, pads, dve_steps)):
            @block.sync
            def _(sp):
                sp.dma_start(cw[:], T["conv"][bass.ds(l, 1)].rearrange("a p k n -> (a p) k n")).then_inc(w_loaded, 16)

            @block.gpsimd
            def _(pool):
                nc.gpsimd.memset(u[:, :, 0:1], 0.0).then_inc(pads, 1)
                nc.gpsimd.memset(u[:, :, LAT + 1:LAT + 3], 0.0).then_inc(pads, 1)
                nc.gpsimd.memset(u[:, :, PAD - 1:PAD], 0.0).then_inc(pads, 1)

            @block.vector
            def _(dve):
                step = Steps(dve, dve_steps)
                dve.wait_ge(w_loaded, 16)
                dve.wait_ge(pads, 3)
                n = PAD - 2
                for k in range(KT):
                    step(nc.vector.tensor_scalar(y[:, k, 1:1 + n], u[:, k, 0:n], cw[:, k, 0:1], cw[:, k, 3:4], ALU.mult, ALU.add))
                    step(nc.vector.scalar_tensor_tensor(y[:, k, 1:1 + n], u[:, k, 1:1 + n], cw[:, k, 1:2], y[:, k, 1:1 + n], ALU.mult, ALU.add))
                    step(nc.vector.scalar_tensor_tensor(y[:, k, 1:1 + n], u[:, k, 2:2 + n], cw[:, k, 2:3], y[:, k, 1:1 + n], ALU.mult, ALU.add))
        projections(nc, "convb", [Job(w_in(T, l, ZB + c), h_t, True, "vector", times_b(c)) for c in range(2)], ring)


def attention(nc, l, T, h_t, q_t, o_tok, ring, ident):
    with ExitStack() as ctx:
        def sb(name, shape):
            return ctx.enter_context(nc.sbuf_tensor(name, shape, F32))
        k_t = sb("att_k", [P, HEADS, TOK])
        v_tok = sb("att_v", [P, NB + 1, D])

        def channel(dst, c):
            def evac(eng, ps, m, step):
                return nc.scalar.activation(dst[:, 4 * c + m, :], ps[:, 0:TOK], ACT.Copy)
            return evac

        def token(dst, c):
            def evac(eng, ps, m, step):
                return nc.vector.tensor_copy(dst[:, m, c * CHUNK:(c + 1) * CHUNK], ps[:, 0:CHUNK])
            return evac

        projections(nc, "qkv",
                    [Job(w_in(T, l, ZQ + c), h_t, True, "scalar", channel(q_t, c)) for c in range(2)]
                    + [Job(w_in(T, l, ZK + c), h_t, True, "scalar", channel(k_t, c)) for c in range(2)]
                    + [Job(w_in(T, l, ZV + c), h_t, False, "vector", token(v_tok, c)) for c in range(2)], ring)
        attention_core(nc, l, T, q_t, k_t, v_tok, o_tok, ident)


def attention_core(nc, l, T, q_t, k_t, v_tok, o_tok, ident):
    UNITS = NB
    KEYS = LAT + CTX
    with ExitStack() as ctx:
        def sb(name, shape):
            return ctx.enter_context(nc.sbuf_tensor(name, shape, F32))
        kc = sb("att_kc", [P, HEADS, CTX])
        cos, sin, rot = sb("att_cos", [P, LAT]), sb("att_sin", [P, LAT]), sb("att_rot", [P, P])
        lam_in, lam_pr = sb("att_lam_in", [P, 4, QK]), sb("att_lam_pr", [P, 2, QK])
        lam = sb("att_lam", [P, 4])
        neg_lam, lam0 = sb("att_neg_lam", [P, 1]), sb("att_lam0", [P, DEPTH])
        qs, ks = sb("att_qs", [P, TOK]), sb("att_ks", [P, KEYS + CTX])
        rotated = sb("att_rotated", [P, LAT])
        prob = [sb(f"att_p{i}", [P, 2, KEYS]) for i in range(2)]
        prob_t = sb("att_pt", [P, KEYS])
        mx, rs, ri = sb("att_mx", [P, 2, 2]), sb("att_rs", [P, 2, 2]), sb("att_ri", [P, 2, 2])
        k_new = sb("att_knew", [P, D])
        ps_rot = ctx.enter_context(nc.psum_tensor("att_ps_rot", [P, LAT], F32))
        ps_s = ctx.enter_context(nc.psum_tensor("att_ps_s", [P, 2, 1024], F32))
        ps_t = ctx.enter_context(nc.psum_tensor("att_ps_t", [P, 1024], F32))
        ps_o = ctx.enter_context(nc.psum_tensor("att_ps_o", [P, 512], F32))
        with stage(nc, "ac_in", "ac_lam", "ac_lexp", "ac_rot", "ac_rotfree", "ac_staged", "ac_score", "ac_nmax",
                   "ac_exp", "ac_mixed", "ac_tp", "ac_ptc", "ac_pv", "ac_out", "ac_dve", "ac_knt", "ac_kout") as (block, sems):
            (loaded, lam_sum, lam_exp, rot_done, rot_used, staged, scored, maxed, exped, mixed, transposed,
             pt_ready, pv_done, o_out, dve_steps, kn_done, k_out) = sems

            @block.sync
            def _(sp):
                one = bass.ds(l, 1)
                for dst, src in ((kc[:], T["kc"][one].rearrange("a p h j -> (a p) h j")), (v_tok[:, NB, :], T["vc"][one].rearrange("a p n -> (a p) n")),
                                 (cos[:], T["cos"]), (sin[:], T["sin"]), (rot[:], T["rot"]), (lam0[:], T["lam0"]),
                                 (lam_in[:], T["lam"][one].rearrange("a x d -> a (x d)").to_broadcast([P, 4 * QK]).rearrange("p (x d) -> p x d", x=4))):
                    sp.dma_start(dst, src).then_inc(loaded, 16)
                sp.dma_start(T["new_v"][one].rearrange("a p n -> (a p) n"), v_tok[:, NB - 1, :]).then_inc(k_out, 16)
                sp.wait_ge(kn_done, HEADS)
                sp.dma_start(T["new_k"][one].rearrange("a p n -> (a p) n"), k_new[:]).then_inc(k_out, 16)
                sp.wait_ge(k_out, 32)

            def keys_of(u):
                return (0, KEYS) if u < UNITS - 1 else (KEYS, KEYS + CTX)

            @block.tensor
            def _(pe):
                def scores(h, u):
                    n = UNITS * h + u
                    k0, k1 = keys_of(u)
                    pe.wait_ge(exped, 2 * n + 1)
                    for j in range(2):
                        rows = slice(QK * j, QK * j + QK)
                        for c0 in range(k0, k1, LAT):
                            c1 = min(c0 + LAT, k1)
                            last = nc.tensor.matmul(ps_s[:, j, c0 - k0:c1 - k0], qs[rows, u * P:(u + 1) * P],
                                                    ks[rows, c0:c1], start=True, stop=True)
                    last.then_inc(scored, 1)

                pe.wait_ge(loaded, 16 * 7)
                with pe.Fori(0, HEADS) as h:
                    for n, src in enumerate((q_t, k_t)):
                        pe.wait_ge(rot_used, 3 * h + n + 1)
                        nc.tensor.matmul(ps_rot[:], rot[:], src[:, bass.ds(h, 1), 0:LAT].rearrange("p a t -> p (a t)"),
                                         start=True, stop=True).then_inc(rot_done, 1)
                    pe.wait_ge(staged, h + 1)
                    scores(h, 0)
                    for u in range(UNITS):
                        n = UNITS * h + u
                        k0, k1 = keys_of(u)
                        if u + 1 < UNITS:
                            scores(h, u + 1)
                        pe.wait_ge(mixed, n + 1)
                        pe.wait_ge(pt_ready, n + 1)
                        for kb in range((k1 - k0) // P):
                            last = nc.tensor.transpose(ps_t[:, kb * P:(kb + 1) * P], prob[u % 2][:, 0, kb * P:(kb + 1) * P], ident[:])
                        last.then_inc(transposed, 1)
                        pe.wait_ge(pt_ready, n + 2)
                        pe.wait_ge(o_out, n + 1)
                        blocks = [0, 1, 2, 3, NB] if u < UNITS - 1 else [NB - 1]
                        for i, vb in enumerate(blocks):
                            last = nc.tensor.matmul(ps_o[:, 0:P], prob_t[:, i * P:(i + 1) * P],
                                                    v_tok[:, vb, bass.ds(h * P, P)], start=i == 0, stop=i == len(blocks) - 1)
                        last.then_inc(pv_done, 1)
                    pe.wait_ge(rot_used, 3 * h + 3)
                    nc.tensor.transpose(ps_rot[:, 0:P], ks[:, KEYS:KEYS + CTX], ident[:]).then_inc(transposed, 1)

            @block.scalar
            def _(act):
                def exps(h, u):
                    n = UNITS * h + u
                    k0, k1 = keys_of(u)
                    act.wait_ge(maxed, n + 1)
                    for j in range(2):
                        act.activation(prob[u % 2][:, j, 0:k1 - k0], ps_s[:, j, 0:k1 - k0], ACT.Exp,
                                       bias=mx[:, u % 2, j:j + 1], scale=SCALE,
                                       accum_out=rs[:, u % 2, j:j + 1]).then_inc(exped, 1)

                act.sem_inc(exped, 1)
                act.sem_inc(pt_ready, 1)
                act.wait_ge(lam_sum, 1)
                act.activation(lam[:, 2:4], lam[:, 0:2], ACT.Exp).then_inc(lam_exp, 1)
                with act.Fori(0, HEADS) as h:
                    exps(h, 0)
                    for u in range(UNITS):
                        k0, k1 = keys_of(u)
                        act.wait_ge(transposed, (UNITS + 1) * h + u + 1)
                        act.activation(prob_t[:, 0:k1 - k0], ps_t[:, 0:k1 - k0], ACT.Copy).then_inc(pt_ready, 1)
                        if u + 1 < UNITS:
                            exps(h, u + 1)

            @block.vector
            def _(dve):
                dve.sem_inc(o_out, 1)
                dve.sem_inc(rot_used, 1)
                dve.wait_ge(loaded, 16 * 7)
                step = Steps(dve, dve_steps)
                step(nc.vector.tensor_tensor(lam_pr[:], lam_in[:, 0:4:2, :], lam_in[:, 1:4:2, :], ALU.mult))
                nc.vector.tensor_reduce(lam[:, 0:2], lam_pr[:], AX.X, ALU.add).then_inc(lam_sum, 1)
                dve.wait_ge(lam_exp, 1)
                step(nc.vector.tensor_tensor(neg_lam[:], lam[:, 3:4], lam[:, 2:3], ALU.subtract))
                step(nc.vector.tensor_tensor(neg_lam[:], neg_lam[:], lam0[:, bass.ds(l, 1)], ALU.subtract))
                first = step.n

                def flat(ap):
                    return ap.rearrange("p a t -> p (a t)")

                with dve.Fori(0, HEADS) as h:
                    per_head = 6 + 4 * UNITS
                    step = Steps(dve, dve_steps, per_head * h + first)
                    head = bass.ds(h, 1)

                    def maxima(u):
                        k0, k1 = keys_of(u)
                        m = mx[:, u % 2, :]
                        dve.wait_ge(scored, UNITS * h + u + 1)
                        step(nc.vector.tensor_reduce(m, ps_s[:, :, 0:k1 - k0], AX.X, ALU.max))
                        nc.vector.tensor_scalar(m, m, -SCALE, None, ALU.mult).then_inc(maxed, 1)

                    for n, (src, dst) in enumerate(((q_t, qs), (k_t, ks))):
                        dve.wait_ge(rot_done, 2 * h + n + 1)
                        nc.vector.tensor_tensor(rotated[:], ps_rot[:], sin[:], ALU.mult).then_inc(rot_used, 1)
                        step(nc.vector.tensor_tensor(dst[:, 0:LAT], flat(src[:, head, 0:LAT]), cos[:], ALU.mult))
                        dve.wait_ge(rot_used, 3 * h + n + 2)
                        step(nc.vector.tensor_tensor(dst[:, 0:LAT], dst[:, 0:LAT], rotated[:], ALU.add))
                    step(nc.vector.tensor_copy(qs[:, LAT:TOK], flat(q_t[:, head, LAT:TOK])))
                    step(nc.vector.tensor_copy(ks[:, KEYS:KEYS + CTX], flat(k_t[:, head, LAT:TOK])))
                    nc.vector.tensor_copy(ks[:, LAT:KEYS], flat(kc[:, head, :])).then_inc(staged, 1)
                    maxima(0)
                    for u in range(UNITS):
                        n = UNITS * h + u
                        k0, k1 = keys_of(u)
                        w = k1 - k0
                        pr, i = prob[u % 2], ri[:, u % 2, :]
                        dve.wait_ge(exped, 2 * n + 3)
                        step(nc.vector.reciprocal(i, rs[:, u % 2, :]))
                        step(nc.vector.tensor_scalar(i[:, 1:2], i[:, 1:2], neg_lam[:], None, ALU.mult))
                        step(nc.vector.tensor_scalar(pr[:, 1, 0:w], pr[:, 1, 0:w], i[:, 1:2], None, ALU.mult))
                        nc.vector.scalar_tensor_tensor(pr[:, 0, 0:w], pr[:, 0, 0:w], i[:, 0:1], pr[:, 1, 0:w], ALU.mult, ALU.add).then_inc(mixed, 1)
                        if u + 1 < UNITS:
                            maxima(u + 1)
                        dve.wait_ge(pv_done, n + 1)
                        nc.vector.tensor_copy(o_tok[:, u, bass.ds(h * P, P)], ps_o[:, 0:P]).then_inc(o_out, 1)
                    dve.wait_ge(transposed, (UNITS + 1) * h + UNITS + 1)
                    nc.vector.tensor_copy(k_new[:, bass.ds(h * P, P)], ps_rot[:, 0:P]).then_inc(kn_done, 1)
                    dve.wait_ge(kn_done, h + 1)
                    dve.sem_inc(rot_used, 1)
                    assert step.n == per_head, step.n


def normalise(nc, name, o_tok, weight, factor):
    with ExitStack() as ctx:
        def sb(n, shape):
            return ctx.enter_context(nc.sbuf_tensor(f"{name}_{n}", shape, F32))
        sq, w, fac = sb("sq", [P, D]), sb("w", [P, P]), sb("fac", [P, 1])
        ms, rstd = sb("ms", [P, NB * HEADS]), sb("rstd", [P, NB * HEADS])
        with stage(nc, f"{name}_in", f"{name}_dve", f"{name}_ms", f"{name}_rt") as (block, (loaded, dve_steps, ms_done, root_done)):
            @block.sync
            def _(sp):
                sp.dma_start(w[:], weight.to_broadcast([P, P])).then_inc(loaded, 16)
                if factor is not None:
                    sp.dma_start(fac[:], factor).then_inc(loaded, 16)

            @block.scalar
            def _(act):
                act.wait_ge(ms_done, 1)
                act.activation(rstd[:], ms[:], ACT.Sqrt).then_inc(root_done, 1)

            @block.vector
            def _(dve):
                step = Steps(dve, dve_steps)
                for b in range(NB):
                    step(nc.vector.tensor_tensor(sq[:], o_tok[:, b, :], o_tok[:, b, :], ALU.mult))
                    step(nc.vector.tensor_reduce(ms[:, b * HEADS:(b + 1) * HEADS], sq[:].rearrange("p (h v) -> p h v", h=HEADS), AX.X, ALU.add))
                nc.vector.tensor_scalar(ms[:], ms[:], 1.0 / P, EPS, ALU.mult, ALU.add).then_inc(ms_done, 1)
                dve.wait_ge(root_done, 1)
                step(nc.vector.reciprocal(rstd[:], rstd[:]))
                dve.wait_ge(loaded, 16 if factor is None else 32)
                if factor is not None:
                    step(nc.vector.tensor_scalar(w[:], w[:], fac[:], None, ALU.mult))
                for b in range(NB):
                    o = o_tok[:, b, :].rearrange("p (h v) -> p h v", h=HEADS)
                    step(nc.vector.tensor_tensor(o, o, rstd[:, b * HEADS:(b + 1) * HEADS].unsqueeze(2).to_broadcast([P, HEADS, P]), ALU.mult))
                    step(nc.vector.tensor_tensor(o, o, w[:].unsqueeze(1).to_broadcast([P, HEADS, P]), ALU.mult))


def to_channel_major(nc, name, src_tok, dst_t, ident):
    with ExitStack() as ctx:
        psum = [ctx.enter_context(nc.psum_tensor(f"{name}_ps{i}", [P, D], F32)) for i in range(2)]
        with stage(nc, f"{name}_tp", f"{name}_cp") as (block, (transposed, copied)):
            @block.tensor
            def _(pe):
                for b in range(NB):
                    if b >= 2:
                        pe.wait_ge(copied, b - 1)
                    for k in range(KT):
                        last = nc.tensor.transpose(psum[b % 2][:, k * P:(k + 1) * P], src_tok[:, b, k * P:(k + 1) * P], ident[:])
                    last.then_inc(transposed, 1)

            @block.scalar
            def _(act):
                for b in range(NB):
                    act.wait_ge(transposed, b + 1)
                    act.activation(dst_t[:, :, b * P:(b + 1) * P], psum[b % 2][:].rearrange("p (k t) -> p k t", k=KT),
                                   ACT.Copy).then_inc(copied, 1)


def recurrent_branch(nc, l, T, h_t, q_t, o_tok, ring, ident):
    with ExitStack() as ctx:
        i_tok = ctx.enter_context(nc.sbuf_tensor("rec_i", [P, NB, D], F32))

        def channel(c):
            def evac(eng, ps, m, step):
                return nc.scalar.activation(q_t[:, 4 * c + m, :], ps[:, 0:TOK], ACT.Silu)
            return evac

        def token(c):
            def evac(eng, ps, m, step):
                return nc.vector.tensor_copy(i_tok[:, m, c * CHUNK:(c + 1) * CHUNK], ps[:, 0:CHUNK])
            return evac

        projections(nc, "rqi", [Job(w_in(T, l, RQ + c), h_t, True, "scalar", channel(c)) for c in range(2)]
                    + [Job(w_in(T, l, RI + c), h_t, False, "vector", token(c)) for c in range(2)], ring)
        with ExitStack() as inner:
            lf = inner.enter_context(nc.sbuf_tensor("rec_lf", [P, NB, D], F32))
            kk = inner.enter_context(nc.sbuf_tensor("rec_k", [P, NB, D], F32))
            for d, first in enumerate((RFF, RFB)):
                def sig(c):
                    def evac(eng, ps, m, step):
                        return nc.scalar.activation(kk[:, m, c * CHUNK:(c + 1) * CHUNK], ps[:, 0:CHUNK], ACT.Sigmoid)
                    return evac
                projections(nc, f"rf{d}", [Job(w_in(T, l, first + c), h_t, False, "scalar", sig(c)) for c in range(2)], ring)
                forget_gates(nc, l, T, d, kk, lf, ring)
                scan(nc, l, T, d, q_t, i_tok, kk, lf, o_tok, ring, ident)
        normalise(nc, f"recn", o_tok, T["rec_norm"][bass.ds(l, 1), :], None)
        gate = i_tok

        def gated(c):
            def evac(eng, ps, m, step):
                cols = slice(c * CHUNK, (c + 1) * CHUNK)
                step(nc.scalar.activation(gate[:, m, cols], ps[:, 0:CHUNK], ACT.Silu))
                return nc.scalar.activation(gate[:, m, cols], gate[:, m, cols], ACT.Copy)
            return evac
        projections(nc, "rg", [Job(w_in(T, l, RG + c), h_t, False, "scalar", gated(c)) for c in range(2)], ring)
        with stage(nc, "rg_mul") as (block, (multiplied,)):
            @block.vector
            def _(dve):
                for b in range(NB):
                    nc.vector.tensor_tensor(o_tok[:, b, :], o_tok[:, b, :], gate[:, b, :], ALU.mult).then_inc(multiplied, 1)


def forget_gates(nc, l, T, d, kk, lf, ring):
    r = ring[0][:].rearrange("p k n -> p (k n)").rearrange("p (a n) -> p a n", a=4)
    with ExitStack() as ctx:
        sel = ctx.enter_context(nc.sbuf_tensor(f"fg{d}_sel", [P, DEPTH], F32))
        with stage(nc, "fg_in", "fg_dve", "fg_cent", "fg_exp", "fg_f", "fg_ln") as (block, (loaded, dve_steps, centred, exped, f_ready, ln_done)):
            @block.sync
            def _(sp):
                sp.dma_start(sel[:], T["sel"]).then_inc(loaded, 16)
                for j in range(DEPTH):
                    sp.dma_start(r[:, j, :], T["rec_lb"][j, d:d + 1, :].to_broadcast([P, D])).then_inc(loaded, 16)

            @block.scalar
            def _(act):
                act.wait_ge(centred, 1)
                act.activation(r[:, 0:2, :], r[:, 0:2, :], ACT.Exp).then_inc(exped, 1)
                for b in range(NB):
                    act.wait_ge(f_ready, b + 1)
                    act.activation(lf[:, b, :], lf[:, b, :], ACT.Ln).then_inc(ln_done, 1)

            @block.vector
            def _(dve):
                step = Steps(dve, dve_steps)
                dve.wait_ge(loaded, 16 * 3)
                step(nc.vector.tensor_tensor(r[:, 2, :], r[:, 0, :], r[:, 1, :], ALU.max))
                nc.vector.tensor_tensor(r[:, 0:2, :], r[:, 0:2, :], r[:, 2:3, :].to_broadcast([P, 2, D]), ALU.subtract).then_inc(centred, 1)
                dve.wait_ge(exped, 1)
                step(nc.vector.tensor_tensor(r[:, 2, :], r[:, 0, :], r[:, 1, :], ALU.add))
                step(nc.vector.reciprocal(r[:, 2, :], r[:, 2, :]))
                step(nc.vector.tensor_tensor(r[:, 1, :], r[:, 1, :], r[:, 2, :], ALU.mult))
                step(nc.vector.tensor_scalar(r[:, 1, :], r[:, 1, :], sel[:, bass.ds(l, 1)], None, ALU.mult))
                step(nc.vector.tensor_scalar(r[:, 0, :], r[:, 1, :], -1.0, 1.0, ALU.mult, ALU.add))
                for b in range(NB):
                    step(nc.vector.tensor_tensor(lf[:, b, :], kk[:, b, :], r[:, 0, :], ALU.mult))
                    step(nc.vector.tensor_tensor(lf[:, b, :], lf[:, b, :], r[:, 1, :], ALU.add))
                    step(nc.vector.tensor_scalar(kk[:, b, :], lf[:, b, :], -1.0, 1.0, ALU.mult, ALU.add))
                    nc.vector.tensor_scalar(lf[:, b, :], lf[:, b, :], TINY, None, ALU.max).then_inc(f_ready, 1)


def scan(nc, l, T, d, q_t, i_tok, kk, lf, o_tok, ring, ident):
    units = NB * HEADS
    edge = P - 1 if d == 0 else 0
    with ExitStack() as ctx:
        def sb(name, shape):
            return ctx.enter_context(nc.sbuf_tensor(f"scan{d}_{name}", shape, F32))
        levels, suffix, mask = sb("levels", [P, LEVELS + 1, P]), sb("suffix", [P, P]), sb("mask", [P, LEVELS + 1, P])
        state = sb("state", [P, 2, D])
        room = [r[:].rearrange("p k n -> p (k n)") for r in ring]

        def carve(j, at, n):
            return room[j][:, at * P:(at + n) * P]
        expd = [carve(j, 0, 8) for j in range(2)]
        xq = [carve(j, 8, 8) for j in range(2)]
        xk = [carve(j, 16, 7) for j in range(2)]
        k_tr = [carve(j, 23, 1) for j in range(2)]
        masked_w = [carve(j, 24, 8) for j in range(2)]
        lfs = [sb(f"lfs{j}", [P, P]) for j in range(2)]
        ks = [sb(f"ks{j}", [P, P]) for j in range(2)]
        rest = [sb(f"rest{j}", [P, P]) for j in range(2)]
        k_dec = [sb(f"kdec{j}", [P, P]) for j in range(2)]
        weights = [sb(f"w{j}", [P, P]) for j in range(2)]
        ps_d = ctx.enter_context(nc.psum_tensor(f"scan{d}_ps_d", [P, 1024], F32))
        ps_r = ctx.enter_context(nc.psum_tensor(f"scan{d}_ps_r", [P, 512], F32))
        ps_a = ctx.enter_context(nc.psum_tensor(f"scan{d}_ps_a", [P, 1024], F32))
        ps_o = ctx.enter_context(nc.psum_tensor(f"scan{d}_ps_o", [P, 512], F32))
        ps_s = ctx.enter_context(nc.psum_tensor(f"scan{d}_ps_s", [P, 512], F32))

        def where(i, j):
            b = i // 4 if d == 0 else NB - 1 - i // 4
            return b, b // (NB - 1), (i % 4) * 2 + j

        def blk(t, b, h):
            return t[:, bass.ds(b, 1), bass.ds(h * P, P)].rearrange("p a n -> p (a n)")

        def over_units(eng, body):
            with eng.Fori(0, units // 2 - 1) as i:
                body(i, 0, True)
                body(i, 1, True)
            body(units // 2 - 1, 0, False)
            body(units // 2 - 1, 1, False)

        with stage(nc, "sc_in", "sc_copied", "sc_s1", "sc_exped", "sc_xk", "sc_xq", "sc_a", "sc_masked",
                   "sc_as", "sc_o", "sc_unit", "sc_out") as (block, sems):
            loaded, staged, spans, exped, xk_done, xq_done, a_done, masked, w_done, o_done, unit_done, s_out = sems

            @block.sync
            def _(sp):
                one = bass.ds(l, 1)
                sp.dma_start(levels[:], T["levels"][d]).then_inc(loaded, 16)
                sp.dma_start(suffix[:], T["suffix"][d]).then_inc(loaded, 16)
                sp.dma_start(mask[:], T["mask"][d]).then_inc(loaded, 16)
                sp.dma_start(state[:, 0, :], T["state"][one, d].rearrange("a p n -> (a p) n")).then_inc(loaded, 16)
                sp.wait_ge(unit_done, 2 + units)
                sp.dma_start(T["new_state"][one, d].rearrange("a p n -> (a p) n"), state[:, 1, :]).then_inc(s_out, 16)
                sp.wait_ge(s_out, 16)

            @block.gpsimd
            def _(pool):
                nc.gpsimd.memset(state[:, 1, :], 0.0).then_inc(staged, 1)

                def stage_in(i, j):
                    b, _, h = where(i, j)
                    pool.wait_ge(spans, 2 * i + j + 1)
                    nc.gpsimd.tensor_copy(lfs[j][:], blk(lf, b, h)).then_inc(staged, 1)
                    nc.gpsimd.tensor_copy(ks[j][:], blk(kk, b, h)).then_inc(staged, 1)

                def body(i, j, more):
                    b, _, h = where(i, j)
                    pool.wait_ge(exped, 6 * i + 3 * j + 4)
                    pool.wait_ge(unit_done, 2 * i + j + 1)
                    q = q_t[:, bass.ds(h, 1), bass.ds(b * P, P)].to_broadcast([P, LEVELS + 1, P])
                    nc.gpsimd.tensor_tensor(xq[j].rearrange("p (a t) -> p a t", t=P), expd[j].rearrange("p (a t) -> p a t", t=P),
                                            q, ALU.mult).then_inc(xq_done, 1)
                    if more:
                        stage_in(i + 1, j)
                stage_in(0, 0)
                stage_in(0, 1)
                over_units(pool, body)

            @block.tensor
            def _(pe):
                def span_sums(i, j):
                    pe.wait_ge(staged, 4 * i + 2 * j + 3)
                    pe.wait_ge(exped, 6 * i + 3 * j + 1)
                    for c in range(2):
                        nc.tensor.matmul(ps_d[:, c * 512:(c + 1) * 512], lfs[j][:],
                                         levels[:, 4 * c:4 * c + 4, :].rearrange("p a t -> p (a t)"), start=True, stop=True)
                    nc.tensor.matmul(ps_r[:, 0:P], suffix[:], lfs[j][:], start=True, stop=True)
                    nc.tensor.transpose(ps_r[:, P:2 * P], ks[j][:], ident[:]).then_inc(spans, 1)

                def body(i, j, more):
                    b, req, h = where(i, j)
                    pe.wait_ge(xk_done, 4 * i + 2 * j + 1)
                    pe.wait_ge(xq_done, 2 * i + j + 1)
                    pe.wait_ge(w_done, 2 * i + j + 1)
                    for a in range(LEVELS):
                        nc.tensor.matmul(ps_a[:, a * P:(a + 1) * P], xk[j][:, a * P:(a + 1) * P], xq[j][:, a * P:(a + 1) * P],
                                         start=True, stop=True)
                    nc.tensor.matmul(ps_a[:, LEVELS * P:], k_tr[j],
                                     q_t[:, bass.ds(h, 1), bass.ds(b * P, P)].rearrange("p a t -> p (a t)"),
                                     start=True, stop=True).then_inc(a_done, 1)
                    if more:
                        span_sums(i + 1, j)
                    pe.wait_ge(w_done, 2 * i + j + 2)
                    pe.wait_ge(xk_done, 4 * i + 2 * j + 2)
                    pe.wait_ge(unit_done, 2 * i + j + 2)
                    nc.tensor.matmul(ps_o[:, 0:P], weights[j][:], blk(i_tok, b, h), start=True, stop=False)
                    nc.tensor.matmul(ps_o[:, 0:P], xq[j][:, LEVELS * P:], blk(state, req, h), start=False, stop=True)
                    nc.tensor.matmul(ps_s[:, 0:P], k_dec[j][:], blk(i_tok, b, h), start=True, stop=True).then_inc(o_done, 1)

                pe.sem_inc(spans, 2)
                pe.wait_ge(loaded, 64)
                span_sums(0, 0)
                span_sums(0, 1)
                over_units(pe, body)

            @block.scalar
            def _(act):
                act.sem_inc(exped, 1)

                def body(i, j, more):
                    act.wait_ge(spans, 2 * i + j + 3)
                    act.wait_ge(unit_done, 2 * i + j + 1)
                    act.activation(expd[j], ps_d[:], ACT.Exp).then_inc(exped, 1)
                    act.activation(rest[j][:], ps_r[:, 0:P], ACT.Exp).then_inc(exped, 1)
                    act.activation(k_tr[j], ps_r[:, P:2 * P], ACT.Copy).then_inc(exped, 1)
                over_units(act, body)

            @block.vector
            def _(dve):
                def keys(i, j):
                    b, _, h = where(i, j)
                    dve.wait_ge(exped, 6 * i + 3 * j + 4)
                    nc.vector.tensor_tensor(xk[j].rearrange("p (a t) -> p a t", t=P), expd[j][:, 0:LEVELS * P].rearrange("p (a t) -> p a t", t=P),
                                            k_tr[j].unsqueeze(1).to_broadcast([P, LEVELS, P]), ALU.mult).then_inc(xk_done, 1)
                    nc.vector.tensor_tensor(k_dec[j][:], blk(kk, b, h), rest[j][:], ALU.mult).then_inc(xk_done, 1)

                def body(i, j, more):
                    b, req, h = where(i, j)
                    dve.wait_ge(a_done, 2 * i + j + 1)
                    nc.vector.tensor_tensor(masked_w[j], ps_a[:], mask[:].rearrange("p a t -> p (a t)"), ALU.mult).then_inc(masked, 1)
                    dve.wait_ge(masked, 2 * i + j + 1)
                    nc.vector.tensor_reduce(weights[j][:], masked_w[j].rearrange("p (a t) -> p t a", t=P), AX.X, ALU.add).then_inc(w_done, 1)
                    if more or j == 0:
                        keys(i + j, 1 - j)
                    dve.wait_ge(o_done, 2 * i + j + 1)
                    if d == 0:
                        nc.vector.tensor_copy(blk(o_tok, b, h), ps_o[:, 0:P])
                    else:
                        nc.vector.tensor_tensor(blk(o_tok, b, h), blk(o_tok, b, h), ps_o[:, 0:P], ALU.add)
                    nc.vector.scalar_tensor_tensor(blk(state, req, h), blk(state, req, h), expd[j][:, LEVELS * P + edge:LEVELS * P + edge + 1],
                                                   ps_s[:, 0:P], ALU.mult, ALU.add).then_inc(unit_done, 1)

                dve.sem_inc(unit_done, 2)
                dve.sem_inc(w_done, 1)
                dve.wait_ge(loaded, 64)
                dve.wait_ge(staged, 1)
                keys(0, 0)
                over_units(dve, body)


def output_projection(nc, l, T, merged_t, y_tok, ring):
    with ExitStack() as ctx:
        gate = ctx.enter_context(nc.sbuf_tensor("op_gate", [P, 2, D], F32))
        with stage(nc, "op_in") as (block, (loaded,)):
            @block.sync
            def _(sp):
                for cond in range(2):
                    sp.dma_start(gate[:, cond, :], mod_row(T, cond, 2)).then_inc(loaded, 16)
                sp.wait_ge(loaded, 32)

        def evac(c):
            def f(eng, ps, m, step):
                cols = slice(c * CHUNK, (c + 1) * CHUNK)
                return nc.vector.tensor_tensor(y_tok[:, m, cols], ps[:, 0:CHUNK], gate[:, m // (NB - 1), cols], ALU.mult)
            return f
        projections(nc, "op", [Job(T["w_out"][bass.ds(l, 1), c].rearrange("a p k n -> (a p) k n"), merged_t, False, "vector", evac(c))
                               for c in range(2)], ring)


def residual_norm(nc, l, T, name, which, y_tok, x_tok, x_from, h_tok, gate_part, x_to):
    with ExitStack() as ctx:
        def sb(n, shape):
            return ctx.enter_context(nc.sbuf_tensor(f"{name}_{n}", shape, F32))
        gb = sb("gb", [P, 2, D])
        vec = sb("vec", [P, 2, 2, D]) if h_tok is not None else None
        scale = sb("ysc", [P, 2, D]) if gate_part is not None else None
        stats, mv, root, nbias = sb("stats", [P, NB, 12]), sb("mv", [P, NB, 2]), sb("root", [P, NB]), sb("nb", [P, NB])
        with stage(nc, f"{name}_in", f"{name}_dve", f"{name}_var", f"{name}_root", f"{name}_xd", f"{name}_out") as (
                block, (loaded, dve_steps, var_done, root_done, x_done, stored)):
            n_in = 2 + (NB if x_from is not None else 0) + (4 if h_tok is not None else 0) + (2 if gate_part is not None else 0)

            @block.sync
            def _(sp):
                one = bass.ds(l, 1)
                sp.dma_start(gb[:, 0, :], T["ln_g"][one, which, :].to_broadcast([P, D])).then_inc(loaded, 16)
                sp.dma_start(gb[:, 1, :], T["ln_b"][one, which, :].to_broadcast([P, D])).then_inc(loaded, 16)
                if x_from is not None:
                    for b in range(NB):
                        sp.dma_start(x_tok[:, b, :], x_from(b)).then_inc(loaded, 16)
                if h_tok is not None:
                    for cond in range(2):
                        for j in range(2):
                            sp.dma_start(vec[:, cond, j, :], mod_row(T, cond, 3 + j)).then_inc(loaded, 16)
                if scale is not None:
                    for cond in range(2):
                        sp.dma_start(scale[:, cond, :], mod_row(T, cond, gate_part)).then_inc(loaded, 16)
                if x_to is not None:
                    for b in range(NB):
                        sp.wait_ge(x_done, b + 1)
                        sp.dma_start(x_to(b), x_tok[:, b, :]).then_inc(stored, 16)
                    sp.wait_ge(stored, 16 * NB)

            @block.scalar
            def _(act):
                act.wait_ge(var_done, 1)
                act.activation(root[:], mv[:, :, 1], ACT.Sqrt).then_inc(root_done, 1)

            @block.vector
            def _(dve):
                step = Steps(dve, dve_steps)
                dve.wait_ge(loaded, 16 * n_in)
                if vec is not None:
                    step(nc.vector.tensor_scalar(vec[:, :, 1, :], vec[:, :, 1, :], 1.0, None, ALU.add))
                for b in range(NB):
                    if scale is not None:
                        step(nc.vector.tensor_tensor(y_tok[:, b, :], y_tok[:, b, :], scale[:, b // (NB - 1), :], ALU.mult))
                    step(nc.vector.scalar_tensor_tensor(x_tok[:, b, :], x_tok[:, b, :], ALPHA, y_tok[:, b, :], ALU.mult, ALU.add))
                    for half in range(2):
                        step(nc.vector.bn_stats(stats[:, b, 6 * half:6 * half + 6], x_tok[:, b, half * 512:(half + 1) * 512]))
                    step(nc.vector.bn_aggr(mv[:, b, :], stats[:, b, :]))
                nc.vector.tensor_scalar(mv[:, :, 1], mv[:, :, 1], EPS, None, ALU.add).then_inc(var_done, 1)
                dve.wait_ge(root_done, 1)
                step(nc.vector.reciprocal(root[:], root[:]))
                for b in range(NB):
                    x = x_tok[:, b, :]
                    step(nc.vector.tensor_scalar(x, x, mv[:, b, 0:1], root[:, b:b + 1], ALU.subtract, ALU.mult))
                    step(nc.vector.tensor_tensor(x, x, gb[:, 0, :], ALU.mult))
                    nc.vector.tensor_tensor(x, x, gb[:, 1, :], ALU.add).then_inc(x_done, 1)
                    if h_tok is not None:
                        cond = b // (NB - 1)
                        dve.wait_ge(x_done, b + 1)
                        step(nc.vector.tensor_tensor(h_tok[:, b, :], x, vec[:, cond, 1, :], ALU.mult))
                        step(nc.vector.tensor_tensor(h_tok[:, b, :], h_tok[:, b, :], vec[:, cond, 0, :], ALU.add))


def peer_queries(nc, l, T, h_t, q_t, ring):
    def evac(c):
        def f(eng, ps, m, step):
            return nc.scalar.activation(q_t[:, 4 * c + m, :], ps[:, 0:TOK], ACT.Copy)
        return f
    projections(nc, "pq", [Job(T["peer_wq"][bass.ds(l, 1), c].rearrange("a p k n -> (a p) k n"), h_t, True, "scalar", evac(c))
                           for c in range(4)], ring)


def expert_scores(nc, l, T, q_t, scores):
    S = 2 * PH
    with ExitStack() as ctx:
        keys = ctx.enter_context(nc.sbuf_tensor("es_keys", [P, S, P], F32))
        psum = [ctx.enter_context(nc.psum_tensor(f"es_ps{i}", [P, S * P], F32)) for i in range(2)]
        with stage(nc, "es_in", "es_mm", "es_cp") as (block, (loaded, scored, copied)):
            @block.sync
            def _(sp):
                sp.dma_start(keys[:], T["peer_keys"][bass.ds(l, 1)].rearrange("a p s n -> (a p) s n")).then_inc(loaded, 16)

            @block.tensor
            def _(pe):
                pe.wait_ge(loaded, 16)
                for b in range(NB):
                    if b >= 2:
                        pe.wait_ge(copied, b - 1)
                    for s in range(S):
                        last = nc.tensor.matmul(psum[b % 2][:, s * P:(s + 1) * P], q_t[:, s, b * P:(b + 1) * P], keys[:, s, :],
                                                start=True, stop=True)
                    last.then_inc(scored, 1)

            @block.scalar
            def _(act):
                for b in range(NB):
                    act.wait_ge(scored, b + 1)
                    act.activation(scores[:, b, :], psum[b % 2][:], ACT.Copy).then_inc(copied, 1)


def experts(nc, l, T, h_tok, y_tok, scores, ident, u_in, v_in, ring):
    units, pairs = NB * PH, PH // 2
    with ExitStack() as ctx:
        def sb(name, shape, dt=F32):
            return ctx.enter_context(nc.sbuf_tensor(name, shape, dt))
        U_SLOTS, V_SLOTS, DIAGS = 8, TOPK, 4
        rooms = [r[:].rearrange("p k n -> p (k n)") for r in ring]
        u_row = [rooms[s // 4][:, (s % 4) * D:(s % 4 + 1) * D] for s in range(U_SLOTS)]
        v_row = [sb(f"ex_v{s}", [P, D])[:] for s in range(V_SLOTS)]
        h_now, zero = sb("ex_h", [P, D]), sb("ex_zero", [P, 512])
        idx_now = [sb(f"ex_i{j}", [P, TOPK], U32) for j in range(2)]
        dot = [sb(f"ex_dot{j}", [P, TOPK]) for j in range(2)]
        act_v = [sb(f"ex_act{j}", [P, TOPK]) for j in range(2)]
        soft = [sb(f"ex_soft{j}", [P, TOPK]) for j in range(2)]
        total = [sb(f"ex_total{j}", [P, 1]) for j in range(2)]
        wgt = [sb(f"ex_w{j}", [P, TOPK]) for j in range(2)]
        diag = [sb(f"ex_diag{i}", [P, P]) for i in range(DIAGS)]
        index, centred = sb("ex_index", [P, units * TOPK], U32), sb("ex_centred", [P, units * TOPK])
        lists, top, top_i = sb("ex_lists", [P, 2, P]), sb("ex_top", [P, 2, TOPK]), sb("ex_topi", [P, 2, TOPK], U32)
        top_f, cand = sb("ex_topf", [P, 2, TOPK]), sb("ex_cand", [P, TOPK * TOPK])
        best, pos = sb("ex_best", [P, TOPK]), sb("ex_pos", [P, TOPK], U32)
        part_u, part_f = sb("ex_partu", [P, 2, TOPK], U32), sb("ex_partf", [P, 2, TOPK])
        hit, num = sb("ex_hit", [P, 2, TOPK, TOPK]), sb("ex_num", [P, 2, TOPK])
        iota, base = sb("ex_iota", [P, TOPK]), sb("ex_base", [P, DEPTH])
        ps_y = ctx.enter_context(nc.psum_tensor("ex_ps_y", [P, D], F32))
        by_list = scores[:].rearrange("p b (s n) -> p (b s) n", n=P)
        with stage(nc, "ex_in", "ex_hnow", "ex_idx", "ex_udone", "ex_vdone", "ex_gelu", "ex_wgt", "ex_diagd", "ex_ydone", "ex_yout",
                   "ex_zeroed", "ex_going", "ex_dve", "ex_routed", "ex_recip", "ex_picking") as (block, sems):
            (loaded, h_ready, idx_ready, u_used, v_used, gelu_done, w_ready, diag_ready, y_done, y_out, zeroed, going,
             dve_steps, routed, recip_done, picking) = sems

            @block.sync
            def _(sp):
                sp.dma_start(iota[:], T["iota"]).then_inc(loaded, 16)
                sp.dma_start(base[:], T["base"]).then_inc(loaded, 16)

            @block.gpsimd
            def _(pool):
                with pool.Fori(0, NB * pairs) as i:
                    for j in range(2):
                        n = 2 * i + j
                        pool.wait_ge(routed, n + 1)
                        nc.gpsimd.tensor_copy(idx_now[j][:], index[:, bass.ds(TOPK * n, TOPK)]).then_inc(idx_ready, 1)
                        for rows, arrived, used, table, go in ((u_row, u_in, u_used, T["peer_u"], 2), (v_row, v_in, v_used, T["peer_v"], 4)):
                            for s in range(TOPK):
                                slot = s % len(rows)
                                if s % go == 0:
                                    pool.wait_ge(used, TOPK * n + s + go)
                                    if s == 0 and rows is u_row:
                                        pool.wait_ge(idx_ready, n + 1)
                                    pool.sem_inc(going, 1)
                                nc.gpsimd.indirect_dma_start(rows[slot], None, table, bass.IndirectOffsetOnAxis(
                                    ap=idx_now[j][:, s:s + 1], axis=0)).then_inc(arrived[slot], 16)

            @block.vector
            def _(dve):
                V = nc.vector

                def choose(count, unit):
                    step = Steps(dve, dve_steps, count * CHOICE_STEPS)
                    cols = bass.ds(unit * TOPK, TOPK)
                    step(V.tensor_copy(lists[:], by_list[:, bass.ds(2 * unit, 2), :]))
                    for lo in (0, 8):
                        dve.sem_inc(picking, 1)
                        for a in range(2):
                            last = V.max(top[:, a, lo:lo + 8], lists[:, a, :])
                        step(last)
                        dve.sem_inc(picking, 1)
                        for a in range(2):
                            last = V.max_index(top_i[:, a, lo:lo + 8], top[:, a, lo:lo + 8], lists[:, a, :])
                            if lo == 0:
                                last = V.match_replace(lists[:, a, :], top[:, a, 0:8], lists[:, a, :], LOWEST)
                        step(last)
                    V.tensor_copy(top_f[:], top_i[:])
                    step(V.tensor_tensor(cand[:].rearrange("p (i j) -> p i j", i=TOPK), top[:, 0, :].unsqueeze(2).to_broadcast([P, TOPK, TOPK]),
                                         top[:, 1, :].unsqueeze(1).to_broadcast([P, TOPK, TOPK]), ALU.add))
                    dve.sem_inc(picking, 1)
                    step(V.max(best[:, 0:8], cand[:]))
                    dve.sem_inc(picking, 1)
                    V.max_index(pos[:, 0:8], best[:, 0:8], cand[:])
                    step(V.match_replace(cand[:], best[:, 0:8], cand[:], LOWEST))
                    dve.sem_inc(picking, 1)
                    step(V.max(best[:, 8:16], cand[:]))
                    dve.sem_inc(picking, 1)
                    step(V.max_index(pos[:, 8:16], best[:, 8:16], cand[:]))
                    V.tensor_scalar(centred[:, cols], best[:], best[:, 0:1], None, ALU.subtract)
                    V.tensor_scalar(part_u[:, 0], pos[:], 4, None, ALU.logical_shift_right)
                    step(V.tensor_scalar(part_u[:, 1], pos[:], 15, None, ALU.bitwise_and))
                    step(V.tensor_copy(part_f[:], part_u[:]))
                    full = [P, 2, TOPK, TOPK]
                    step(V.tensor_tensor(hit[:], part_f[:].unsqueeze(3).to_broadcast(full),
                                         iota[:].unsqueeze(1).unsqueeze(1).to_broadcast(full), ALU.is_equal))
                    step(V.tensor_tensor(hit[:], hit[:], top_f[:].unsqueeze(2).to_broadcast(full), ALU.mult))
                    step(V.tensor_reduce(num[:], hit[:], AX.X, ALU.add))
                    step(V.scalar_tensor_tensor(num[:, 0], num[:, 0], float(P), num[:, 1], ALU.mult, ALU.add))
                    V.tensor_scalar(index[:, cols], num[:, 0], base[:, bass.ds(l, 1)], None, ALU.add).then_inc(routed, 1)
                    assert step.n == CHOICE_STEPS, step.n

                V.memset(zero[:], 0.0).then_inc(zeroed, 1)
                dve.sem_inc(u_used, U_SLOTS)
                dve.wait_ge(loaded, 32)
                choose(0, 0)
                choose(1, 1)
                with dve.Fori(0, NB) as b:
                    V.tensor_copy(h_now[:], h_tok[:, bass.ds(b, 1), :].rearrange("p a n -> p (a n)")).then_inc(h_ready, 1)
                    with dve.Fori(0, pairs) as i:
                        for j in range(2):
                            n = PH * b + 2 * i + j
                            dve.wait_ge(h_ready, b + 1)
                            for s in range(TOPK):
                                dve.wait_ge(u_in[s % U_SLOTS], (l * units + n) * 32 + 16 * (s // U_SLOTS + 1))
                                row = u_row[s % U_SLOTS]
                                V.tensor_tensor_reduce(out=row, in0=row, in1=h_now[:], scale=1.0, scalar=0.0, op0=ALU.mult,
                                                       op1=ALU.add, accum_out=dot[j][:, s:s + 1]).then_inc(u_used, 1)
                            dve.wait_ge(gelu_done, n + 1)
                            V.reciprocal(total[j][:], total[j][:]).then_inc(recip_done, 1)
                            dve.wait_ge(recip_done, n + 1)
                            V.scalar_tensor_tensor(wgt[j][:], act_v[j][:], total[j][:], soft[j][:], ALU.mult, ALU.mult).then_inc(w_ready, 1)
                            choose(n + 2, (n + 2) % units)

            @block.scalar
            def _(act):
                with act.Fori(0, NB) as b:
                    with act.Fori(0, pairs) as i:
                        for j in range(2):
                            n = PH * b + 2 * i + j
                            act.wait_ge(routed, n + 1)
                            act.activation(soft[j][:], centred[:, bass.ds(TOPK * n, TOPK)], ACT.Exp, accum_out=total[j][:])
                            act.wait_ge(u_used, TOPK * n + TOPK + U_SLOTS)
                            act.activation(act_v[j][:], dot[j][:], ACT.Gelu).then_inc(gelu_done, 1)
                            act.wait_ge(w_ready, n + 1)
                            for s in range(TOPK):
                                act.wait_ge(v_used, TOPK * n + s + 1 + V_SLOTS - DIAGS)
                                act.activation(diag[s % DIAGS][:], ident[:], ACT.Copy, scale=wgt[j][:, s:s + 1]).then_inc(diag_ready, 1)
                    act.wait_ge(y_done, b + 1)
                    act.activation(y_tok[:, bass.ds(b, 1), :].rearrange("p a n -> p (a n)"), ps_y[:], ACT.Copy).then_inc(y_out, 1)

            @block.tensor
            def _(pe):
                pe.sem_inc(v_used, V_SLOTS)
                pe.sem_inc(y_out, 1)
                pe.wait_ge(zeroed, 1)
                with pe.Fori(0, NB) as b:
                    pe.wait_ge(y_out, b + 1)
                    for c in (0, 512):
                        nc.tensor.matmul(ps_y[:, c:c + 512], zero[:, 0:P], zero[:], start=True, stop=False)
                    with pe.Fori(0, pairs) as i:
                        for j in range(2):
                            n = PH * b + 2 * i + j
                            for s in range(TOPK):
                                pe.wait_ge(v_in[s], (l * units + n) * 16 + 16)
                                pe.wait_ge(diag_ready, TOPK * n + s + 1)
                                for c in (0, 512):
                                    last = nc.tensor.matmul(ps_y[:, c:c + 512], diag[s % DIAGS][:], v_row[s][:, c:c + 512], start=False, stop=False)
                                last.then_inc(v_used, 1)
                    for c in (0, 512):
                        last = nc.tensor.matmul(ps_y[:, c:c + 512], zero[:, 0:P], zero[:], start=False, stop=True)
                    last.then_inc(y_done, 1)


CHOICE_STEPS = 16


def token_rows(x_rows):
    return lambda b: x_rows[b * P:(b + 1) * P, :]


def copy_rows(nc, name, pairs):
    with stage(nc, f"{name}_done") as (block, (done,)):
        @block.sync
        def _(sp):
            for dst, src in pairs:
                sp.dma_start(dst, src).then_inc(done, 16)
            sp.wait_ge(done, 16 * len(pairs))


def trunk(nc, T, depth=DEPTH, stop=None):
    with ExitStack() as ctx:
        def sb(name, shape):
            return ctx.enter_context(nc.sbuf_tensor(name, shape, F32))
        ident = sb("ident", [P, P])
        h_t = sb("h_t", [P, KT, TOK])
        ring = [sb(f"ring{i}", [P, KT, CHUNK]) for i in range(2)]
        u_in = [ctx.enter_context(nc.semaphore(f"u_in{s}")) for s in range(TOPK // 2)]
        v_in = [ctx.enter_context(nc.semaphore(f"v_in{s}")) for s in range(TOPK)]
        copy_rows(nc, "start", [(T["x_rows"][0:LAT, :], T["x_sample"]), (T["x_rows"][LAT:TOK, :], T["x_prompt"]), (ident[:], T["ident"])])
        with nc.Fori(0, depth) as l:
            modulation(nc, l, T, ring)
            modulate_and_transpose(nc, T, token_rows(T["x_rows"]), h_t, ident, 0)
            if stop == "mod": return
            with ExitStack() as mixer:
                merged_t = mixer.enter_context(nc.sbuf_tensor("merged_t", [P, KT, TOK], F32))
                branch_t = mixer.enter_context(nc.sbuf_tensor("branch_t", [P, KT, TOK], F32))
                conv_branch(nc, l, T, h_t, branch_t, ring)
                if stop == "conv": return
                merge_branch(nc, l, T, "mg1", 1, h_t, branch_t, merged_t, ring)
                with ExitStack() as inner:
                    o_tok = inner.enter_context(nc.sbuf_tensor("o_tok", [P, NB, D], F32))
                    attention(nc, l, T, h_t, branch_t, o_tok, ring, ident)
                    if stop == "attcore": return
                    normalise(nc, "attn", o_tok, T["subln"][bass.ds(l, 1), :], T["lam_keep"][bass.ds(l, 1)].rearrange("a p n -> (a p) n"))
                    to_channel_major(nc, "attt", o_tok, branch_t, ident)
                    if stop == "att": return
                    merge_branch(nc, l, T, "mg0", 0, h_t, branch_t, merged_t, ring)
                    recurrent_branch(nc, l, T, h_t, branch_t, o_tok, ring, ident)
                    to_channel_major(nc, "rect", o_tok, branch_t, ident)
                    if stop == "rec": return
                    merge_branch(nc, l, T, "mg2", 2, h_t, branch_t, merged_t, ring)
                y_tok = branch_t[:].rearrange("p k t -> p (k t)").rearrange("p (b n) -> p b n", b=NB)
                output_projection(nc, l, T, merged_t, y_tok, ring)
                if stop == "mix": return
                with ExitStack() as norm:
                    x_tok = norm.enter_context(nc.sbuf_tensor("x_tok1", [P, NB, D], F32))
                    h_tok = norm.enter_context(nc.sbuf_tensor("h_tok1", [P, NB, D], F32))
                    rows = token_rows(T["x_rows"])
                    residual_norm(nc, l, T, "ln1", 0, y_tok, x_tok, rows, h_tok, None, rows)
                    to_channel_major(nc, "ht", h_tok, h_t, ident)
                    copy_rows(nc, "h_out", [(T["h_rows"].rearrange("(b p) n -> p b n", p=P), h_tok[:])])
            with ExitStack() as peer:
                scores = peer.enter_context(nc.sbuf_tensor("scores", [P, NB, 2 * PH * P], F32))
                with ExitStack() as inner:
                    q_t = inner.enter_context(nc.sbuf_tensor("peer_q", [P, 2 * PH, TOK], F32))
                    peer_queries(nc, l, T, h_t, q_t, ring)
                    expert_scores(nc, l, T, q_t, scores)
                y_tok = h_t[:].rearrange("p k t -> p (k t)").rearrange("p (b n) -> p b n", b=NB)
                with ExitStack() as inner:
                    h_tok = inner.enter_context(nc.sbuf_tensor("h_tok2", [P, NB, D], F32))
                    copy_rows(nc, "h_in", [(h_tok[:], T["h_rows"].rearrange("(b p) n -> p b n", p=P))])
                    experts(nc, l, T, h_tok, y_tok, scores, ident, u_in, v_in, ring)
            if stop == "experts": return
            with ExitStack() as norm:
                x_tok = norm.enter_context(nc.sbuf_tensor("x_tok2", [P, NB, D], F32))
                rows = token_rows(T["x_rows"])
                residual_norm(nc, l, T, "ln2", 1, y_tok, x_tok, rows, None, 5, rows)
        copy_rows(nc, "end", [(T["y_sample"], T["x_rows"][0:LAT, :]), (T["y_prompt"], T["x_rows"][LAT:TOK, :])])


def constants():
    eye = np.eye(P, dtype=np.float32)
    levels = np.zeros((2, P, LEVELS + 1, P), np.float32)
    mask = np.zeros((2, P, LEVELS + 1, P), np.float32)
    s, t = np.meshgrid(np.arange(P), np.arange(P), indexing="ij")
    for a in range(LEVELS):
        half = 1 << a
        mid = (t // (2 * half)) * (2 * half) + half
        levels[0, :, a, :] = np.where(t >= mid, (s >= mid) & (s <= t), (s > t) & (s < mid))
        mask[0, :, a, :] = (s // (2 * half) == t // (2 * half)) & (s < mid) & (t >= mid)
    levels[0, :, LEVELS, :] = s <= t
    mask[0, :, LEVELS, :] = s == t
    suffix = np.stack([s > t, s < t]).astype(np.float32)
    levels[1], mask[1] = levels[0, ::-1, :, ::-1], mask[0, ::-1, :, ::-1]
    half, quarter = QK // 2, QK // 4
    freqs = (10000.0 ** (-np.arange(0, half, 2, dtype=np.float32) / np.float32(half))).astype(np.float32)
    tok = np.arange(LAT)
    cos, sin = np.zeros((P, LAT), np.float32), np.zeros((P, LAT), np.float32)
    rot = np.zeros((P, P), np.float32)
    for c in range(P):
        axis, place = (c % QK) // half, c % half
        ang = (tok // GRID_W if axis == 0 else tok % GRID_W).astype(np.float32) * freqs[place % quarter]
        cos[c], sin[c] = np.cos(ang), np.sin(ang)
        if place < quarter:
            rot[c + quarter, c] = -1.0
        else:
            rot[c - quarter, c] = 1.0
    ones = np.ones((P, 1), np.float32)
    return {
        "ident": eye, "levels": levels, "suffix": suffix, "mask": mask, "cos": cos, "sin": sin, "rot": rot,
        "lam0": ones * np.array(LAM_INIT, np.float32), "sel": ones * np.arange(DEPTH, dtype=np.float32),
        "lam_keep": np.stack([ones * np.float32(1.0 - x) for x in LAM_INIT]),
        "iota": ones * np.arange(TOPK, dtype=np.float32), "base": ones * (EXPERTS * np.arange(DEPTH, dtype=np.float32)),
    }


def layouts(a):
    def chunks(w):
        *lead, d, n = w.shape
        w = w.reshape(*lead, KT, P, n // CHUNK, CHUNK)
        r = len(lead)
        return w.transpose(*range(r), r + 2, r + 1, r, r + 3)

    conv = np.concatenate([a["conv_w"], a["conv_b"][:, None, :]], axis=1)
    return {
        "x_sample": a["x_sample"].reshape(LAT, D), "x_prompt": a["x_prompt"].reshape(CTX, D),
        "cond": np.stack([a["c"].reshape(KT, P), a["c_ctx"].reshape(KT, P)]).transpose(2, 1, 0),
        "kc": a["cache_attn_k"][0].transpose(0, 3, 2, 1), "vc": a["cache_attn_v"][0].reshape(DEPTH, CTX, D),
        "state": a["state_hgrn"][0].transpose(0, 1, 3, 2, 4).reshape(DEPTH, 2, P, D),
        "mod_w": chunks(a["mod_w"]), "mod_b": a["mod_b"], "w_in": chunks(a["w_in"]), "lam": a["attn_lambda"],
        "subln": a["attn_subln"], "conv": conv.reshape(DEPTH, 4, KT, P).transpose(0, 3, 2, 1), "rec_lb": a["rec_lb"],
        "rec_norm": a["rec_norm"], "w_branch": chunks(a["w_branch"]), "w_out": chunks(a["w_out"]), "ln_g": a["ln_g"],
        "ln_b": a["ln_b"], "peer_wq": chunks(a["peer_wq"]),
        "peer_keys": a["peer_keys"].reshape(DEPTH, 2 * PH, P, P).transpose(0, 3, 1, 2),
        "peer_u": a["peer_u"].reshape(DEPTH * EXPERTS, D), "peer_v": a["peer_v"].reshape(DEPTH * EXPERTS, D),
    }


OUTPUTS = {"y_prompt": (CTX, D), "y_sample": (LAT, D), "new_k": (DEPTH, CTX, D), "new_v": (DEPTH, CTX, D),
           "new_state": (DEPTH, 2, P, D)}
SCRATCH = {"x_rows": (TOK, D), "h_rows": (TOK, D), "mod_rows": (2, 6 * D)}


def build(nc, arrays, depth=DEPTH, stop=None):
    tensors = {n: nc.dram_tensor(f"in_{n}", a.shape, F32, kind="ExternalInput").ap() for n, a in arrays.items()}
    tensors.update({n: nc.dram_tensor(f"out_{n}", s, F32, kind="ExternalOutput").ap() for n, s in OUTPUTS.items()})
    tensors.update({n: nc.dram_tensor(n, s, F32, kind="Internal").ap() for n, s in SCRATCH.items()})
    trunk(nc, tensors, depth, stop)


def kernel(**inputs):
    import concourse.bacc as bacc
    from concourse.bass_utils import run_bass_kernel_spmd

    arrays = layouts({k: np.asarray(v) for k, v in inputs.items()})
    arrays.update(constants())
    arrays = {k: np.ascontiguousarray(v) for k, v in arrays.items()}
    nc = bacc.Bacc("TRN2", target_bir_lowering=False, num_devices=1)
    build(nc, arrays)
    got = run_bass_kernel_spmd(nc, [{f"in_{k}": a for k, a in arrays.items()}], core_ids=[0]).results[0]
    out = {n: got[f"out_{n}"] for n in OUTPUTS}
    state = out["new_state"].reshape(DEPTH, 2, P, HEADS, P).transpose(0, 1, 3, 2, 4)
    return (out["y_prompt"].reshape(1, CTX, D), out["y_sample"].reshape(1, LAT, D),
            out["new_k"].reshape(1, DEPTH, CTX, HEADS, P), out["new_v"].reshape(1, DEPTH, CTX, HEADS, P),
            np.ascontiguousarray(state)[None])
```

```python
import math
from contextlib import ExitStack, contextmanager

import numpy as np
import concourse.bass as bass
from concourse import mybir

F32 = mybir.dt.float32
F32R = mybir.dt.float32r
U32 = mybir.dt.uint32
ALU = mybir.AluOpType
ACT = mybir.ActivationFunctionType
AX = mybir.AxisListType

P = 128
D = 1024
KT = D // P
DEPTH = 2
LAT = 512
CTX = 128
TOK = LAT + CTX
NB = TOK // P
CHUNK = 512
HALF = CHUNK // 2
HEADS = 8
QK = 64
SCALE = QK ** -0.5
LEVELS = 7
EXPERTS = 128 * 128
PH = 8
TOPK = 16
EPS = 1e-5
ALPHA = (2 * DEPTH) ** 0.25
LOWEST = -3.0e38
TINY = 2.0 ** -63
GRID_W = 64
LAM_INIT = [0.8 - 0.6 * math.exp(-0.3 * l) for l in range(DEPTH)]
ZQ, ZK, ZV, ZB, ZC, ZX, RQ, RFF, RFB, RI, RG, ZG = 0, 2, 4, 6, 8, 10, 12, 14, 16, 18, 20, 22


class Steps:

    def __init__(self, eng, sem, base=0):
        self.eng, self.sem, self.base, self.n = eng, sem, base, 0

    def mark(self, ins):
        self.n += 1
        ins.then_inc(self.sem, 1)
        return self.base + self.n

    def __call__(self, ins):
        self.eng.wait_ge(self.sem, self.mark(ins))


@contextmanager
def stage(nc, *names):
    with ExitStack() as ctx:
        sems = [ctx.enter_context(nc.semaphore(n)) for n in names]
        nums = sorted(s.num for s in sems)
        starts = [n for n in nums if n - 1 not in nums]
        ends = [n + 1 for n in nums if n + 1 not in nums]
        with nc.Block(no_gpsimd_drain=True) as block:
            yield block, sems
        for a, b in zip(starts, ends):
            nc.all_engine_barrier(sems_to_clear=range(a, b))


class Job:

    def __init__(self, weights, act_split, channel_major, engine, evac):
        self.weights, self.act_split, self.channel_major = weights, act_split, channel_major
        self.engine, self.evac = engine, evac
        self.tiles = HALF // P if channel_major else NB


def bank_pair(ps):
    return ps[:].rearrange("p (b n) -> p b n", b=2)[:, :, 0:TOK // 2]


def token_pair(row):
    return row.rearrange("p (b n) -> p b n", b=2)


def low_part(nc, low, full, high):
    return nc.vector.tensor_tensor(low, full, high.bitcast(F32), ALU.subtract)


def projections(nc, name, jobs, ring):
    halves = [(c, e) for c in range(len(jobs)) for e in range(2)]
    tiles = [(i, m) for i, (c, e) in enumerate(halves) for m in range(jobs[c].tiles)]
    done_through = [sum(jobs[c].tiles for c, e in halves[:i + 1]) for i in range(len(halves))]
    PIECES = 2
    with ExitStack() as ctx:
        psum = [ctx.enter_context(nc.psum_tensor(f"{name}_ps{i}", [P, 1024], F32)) for i in range(4)]
        w_high = [ctx.enter_context(nc.sbuf_tensor(f"{name}_wh{i}", [P, KT, HALF], F32R)) for i in range(2)]
        w_low = [ctx.enter_context(nc.sbuf_tensor(f"{name}_wl{i}", [P, KT, HALF], F32R)) for i in range(2)]
        with stage(nc, f"{name}_w0", f"{name}_w1", f"{name}_tile", f"{name}_free0", f"{name}_free1",
                   f"{name}_free2", f"{name}_free3", f"{name}_dve", f"{name}_act", f"{name}_high", f"{name}_low",
                   *[f"{name}_first{i}" for i in range(PIECES)]) as (block, sems):
            w_loaded, tile_done, slot_free = sems[0:2], sems[2], sems[3:7]
            dve_steps, act_steps, high_done, low_done, first_loaded = *sems[7:11], sems[11:]

            def pieces(i):
                n = KT // PIECES if i == 0 else KT
                return [(k, k + n) for k in range(0, KT, n)]

            def splits(i):
                return PIECES + i

            @block.sync
            def _(sp):
                for p, (k0, k1) in enumerate(pieces(0)):
                    sp.dma_start(ring[0][:, k0:k1, 0:HALF], jobs[0].weights[:, k0:k1, 0:HALF]).then_inc(first_loaded[p], 16)
                sp.dma_start(ring[0][:, :, HALF:], jobs[0].weights[:, :, HALF:]).then_inc(w_loaded[0], 16)
                for c, job in enumerate(jobs[1:], 1):
                    if c >= 2:
                        sp.wait_ge(low_done, splits(2 * (c - 2) + 1))
                    sp.dma_start(ring[c % 2][:], job.weights).then_inc(w_loaded[c % 2], 16)

            @block.tensor
            def _(pe):
                for t, (i, m) in enumerate(tiles):
                    job, ps = jobs[halves[i][0]], psum[t % 4]
                    wh, wl = w_high[i % 2], w_low[i % 2]
                    xh, xl = job.act_split
                    if m == 0 and i > 0:
                        pe.wait_ge(low_done, splits(i))
                    if t >= 4:
                        pe.wait_ge(slot_free[t % 4], t // 4)
                    if job.channel_major:
                        w_cols = slice(m * P, (m + 1) * P)
                        spans = [(512 * b, slice(TOK // 2 * b, TOK // 2 * (b + 1))) for b in range(2)]
                    else:
                        w_cols = slice(0, HALF)
                        spans = [(0, slice(m * P, (m + 1) * P))]
                    for at, toks in spans:
                        for k in range(KT):
                            if t == 0 and at == 0:
                                for p, (k0, k1) in enumerate(pieces(0)):
                                    if k == k0:
                                        pe.wait_ge(low_done, p + 1)
                            for n, (w, x) in enumerate(((wh, xh), (wh, xl), (wl, xh))):
                                w_ap, x_ap = w[:, k, w_cols], x[:, k, toks]
                                lhs, rhs = (w_ap, x_ap) if job.channel_major else (x_ap, w_ap)
                                cols = TOK // 2 if job.channel_major else HALF
                                last = nc.tensor.matmul(ps[:, at:at + cols], lhs, rhs, start=k == 0 and n == 0,
                                                        stop=k == KT - 1 and n == 2)
                    last.then_inc(tile_done, 1)

            def evacuate(eng, which, steps, split):
                split(0)
                split(1)
                for i, (c, e) in enumerate(halves):
                    for t, (j, m) in enumerate(tiles):
                        if j == i and jobs[c].engine == which:
                            eng.wait_ge(tile_done, t + 1)
                            if jobs[c].channel_major:
                                last = jobs[c].evac(eng, psum[t % 4], e * jobs[c].tiles + m, steps)
                            else:
                                last = jobs[c].evac(eng, psum[t % 4], m, steps, e)
                            last.then_inc(slot_free[t % 4], 1)
                    if i + 2 < len(halves):
                        eng.wait_ge(tile_done, done_through[i])
                        split(i + 2)

            @block.scalar
            def _(act):
                def split(i):
                    c, e = halves[i]
                    cols = slice(e * HALF, (e + 1) * HALF)
                    for p, (k0, k1) in enumerate(pieces(i)):
                        if i == 0:
                            act.wait_ge(first_loaded[p], 16)
                        else:
                            act.wait_ge(w_loaded[c % 2], 16 * (c // 2 + 1))
                        act.activation(w_high[i % 2][:, k0:k1, :], ring[c % 2][:, k0:k1, cols], ACT.Copy).then_inc(high_done, 1)
                evacuate(act, "scalar", Steps(act, act_steps), split)

            @block.vector
            def _(dve):
                def split(i):
                    c, e = halves[i]
                    cols = slice(e * HALF, (e + 1) * HALF)
                    for p, (k0, k1) in enumerate(pieces(i)):
                        dve.wait_ge(high_done, splits(i) if i else p + 1)
                        low_part(nc, w_low[i % 2][:, k0:k1, :], ring[c % 2][:, k0:k1, cols],
                                 w_high[i % 2][:, k0:k1, :]).then_inc(low_done, 1)
                evacuate(dve, "vector", Steps(dve, dve_steps), split)


def modulation(nc, l, T, ring):
    with ExitStack() as ctx:
        cond = ctx.enter_context(nc.sbuf_tensor("cond", [P, KT, 2], F32))
        csilu = ctx.enter_context(nc.sbuf_tensor("csilu", [P, KT, 2], F32))
        bias = ctx.enter_context(nc.sbuf_tensor("mod_bias", [2, 6 * D], F32))
        rows = ctx.enter_context(nc.sbuf_tensor("mod_rows_sb", [2, 6 * D], F32))
        psum = [ctx.enter_context(nc.psum_tensor(f"mod_ps{i}", [P, 512], F32)) for i in range(2)]
        n = 6 * D // CHUNK
        with stage(nc, "mod_w0", "mod_w1", "mod_in", "mod_silu", "mod_tile", "mod_free", "mod_out") as (block, sems):
            w_loaded, cond_in, silu_done, tile_done, slot_free, rows_out = sems[0:2], *sems[2:]

            @block.sync
            def _(sp):
                sp.dma_start(cond[:], T["cond"]).then_inc(cond_in, 16)
                sp.dma_start(bias[:], T["mod_b"][bass.ds(l, 1), :].to_broadcast([2, 6 * D])).then_inc(cond_in, 16)
                for c in range(2):
                    sp.dma_start(ring[c][:], T["mod_w"][bass.ds(l, 1), c].rearrange("a p k n -> (a p) k n")).then_inc(w_loaded[c], 16)
                with sp.Fori(1, n // 2) as i:
                    for j in range(2):
                        sp.wait_ge(tile_done, 2 * i + j - 1)
                        sp.dma_start(ring[j][:], T["mod_w"][bass.ds(l, 1), bass.ds(2 * i + j, 1)].rearrange(
                            "a b p k n -> (a b p) k n")).then_inc(w_loaded[j], 16)
                sp.wait_ge(slot_free, 2 + n)
                sp.dma_start(T["mod_rows"], rows[:]).then_inc(rows_out, 16)
                sp.wait_ge(rows_out, 16)

            @block.scalar
            def _(act):
                act.wait_ge(cond_in, 32)
                act.activation(csilu[:], cond[:], ACT.Silu).then_inc(silu_done, 1)

            @block.tensor
            def _(pe):
                pe.wait_ge(silu_done, 1)
                with pe.Fori(0, n // 2) as i:
                    for j in range(2):
                        pe.wait_ge(w_loaded[j], 16 * i + 16)
                        pe.wait_ge(slot_free, 2 * i + j + 1)
                        for k in range(KT):
                            last = nc.tensor.matmul(psum[j][0:2, :], csilu[:, k, :], ring[j][:, k, :],
                                                    start=k == 0, stop=k == KT - 1)
                        last.then_inc(tile_done, 1)

            @block.vector
            def _(dve):
                dve.sem_inc(slot_free, 2)
                dve.wait_ge(cond_in, 32)
                with dve.Fori(0, n // 2) as i:
                    for j in range(2):
                        cols = bass.ds((2 * i + j) * CHUNK, CHUNK)
                        dve.wait_ge(tile_done, 2 * i + j + 1)
                        nc.vector.tensor_tensor(rows[:, cols], psum[j][0:2, :], bias[:, cols], ALU.add).then_inc(slot_free, 1)


def mod_row(T, cond, part):
    return T["mod_rows"][cond:cond + 1, part * D:(part + 1) * D].to_broadcast([P, D])


def modulate_and_transpose(nc, T, x_src, h_split, ident, first_part):
    high, low = h_split
    with ExitStack() as ctx:
        xb = [ctx.enter_context(nc.sbuf_tensor(f"mt_x{i}", [P, D], F32)) for i in range(NB)]
        vec = ctx.enter_context(nc.sbuf_tensor("mt_vec", [P, 2, 2, D], F32))
        psum = [ctx.enter_context(nc.psum_tensor(f"mt_ps{i}", [P, D], F32)) for i in range(2)]
        with stage(nc, "mt_x", "mt_vec_in", "mt_dve", "mt_tp", "mt_high", "mt_low") as (
                block, (x_in, vec_in, dve_steps, transposed, high_done, low_done)):

            @block.sync
            def _(sp):
                for cond in range(2):
                    for j in range(2):
                        sp.dma_start(vec[:, cond, j, :], mod_row(T, cond, first_part + j)).then_inc(vec_in, 16)
                for b in range(NB):
                    sp.dma_start(xb[b][:], x_src(b)).then_inc(x_in, 16)

            @block.vector
            def _(dve):
                step = Steps(dve, dve_steps)
                dve.wait_ge(vec_in, 64)
                dve.wait_ge(x_in, 16 * NB)
                step(nc.vector.tensor_scalar(vec[:, :, 1, :], vec[:, :, 1, :], 1.0, None, ALU.add))
                for b in range(NB + 1):
                    if b < NB:
                        cond = b // (NB - 1)
                        step(nc.vector.tensor_tensor(xb[b][:], xb[b][:], vec[:, cond, 1, :], ALU.mult))
                        step(nc.vector.tensor_tensor(xb[b][:], xb[b][:], vec[:, cond, 0, :], ALU.add))
                    if b > 0:
                        dve.wait_ge(high_done, b)
                        cols = slice((b - 1) * P, b * P)
                        low_part(nc, low[:, :, cols], psum[(b - 1) % 2][:].rearrange("p (k t) -> p k t", k=KT), high[:, :, cols]).then_inc(low_done, 1)

            @block.tensor
            def _(pe):
                for b in range(NB):
                    pe.wait_ge(dve_steps, 3 + 2 * b)
                    if b >= 2:
                        pe.wait_ge(low_done, b - 1)
                    for k in range(KT):
                        last = nc.tensor.transpose(psum[b % 2][:, k * P:(k + 1) * P], xb[b][:, k * P:(k + 1) * P], ident[:])
                    last.then_inc(transposed, 1)

            @block.scalar
            def _(act):
                for b in range(NB):
                    act.wait_ge(transposed, b + 1)
                    act.activation(high[:, :, b * P:(b + 1) * P],
                                   psum[b % 2][:].rearrange("p (k t) -> p k t", k=KT), ACT.Copy).then_inc(high_done, 1)


def merge_branch(nc, l, T, name, branch, first, h_split, branch_split, merged_t, ring):
    with ExitStack() as ctx:
        sig = ctx.enter_context(nc.sbuf_tensor(f"{name}_sig", [P, D // P, TOK], F32))

        def gate(c):
            def evac(eng, ps, m, step):
                return nc.scalar.activation(token_pair(sig[:, 4 * c + m, :]), bank_pair(ps), ACT.Sigmoid)
            return evac

        def product(c):
            def evac(eng, ps, m, step):
                t = 4 * c + m
                if first:
                    return nc.vector.tensor_tensor(token_pair(merged_t[:, t, :]), bank_pair(ps), token_pair(sig[:, t, :]), ALU.mult)
                step(nc.vector.tensor_tensor(token_pair(sig[:, t, :]), bank_pair(ps), token_pair(sig[:, t, :]), ALU.mult))
                return nc.vector.tensor_tensor(merged_t[:, t, :], merged_t[:, t, :], sig[:, t, :], ALU.add)
            return evac

        jobs = [Job(w_in(T, l, ZG + 2 * branch + c), h_split, True, "scalar", gate(c)) for c in range(2)]
        jobs += [Job(T["w_branch"][bass.ds(l, 1), branch, c].rearrange("a p k n -> (a p) k n"), branch_split, True,
                     "vector", product(c)) for c in range(2)]
        projections(nc, name, jobs, ring)


def half_cols(c, half):
    return slice(c * CHUNK + half * HALF, c * CHUNK + (half + 1) * HALF)


def w_in(T, l, c):
    return T["w_in"][bass.ds(l, 1), c].rearrange("a p k n -> (a p) k n")


def conv_branch(nc, l, T, h_split, out_split, ring):
    PAD = TOK + 4
    with ExitStack() as ctx:
        u = ctx.enter_context(nc.sbuf_tensor("conv_u", [P, KT, PAD], F32))
        y = ctx.enter_context(nc.sbuf_tensor("conv_y", [P, KT, PAD], F32))
        cw = ctx.enter_context(nc.sbuf_tensor("conv_w_sb", [P, KT, 4], F32))
        parts = [(0, 0, TOK // 2, 1), (512, TOK // 2, LAT, 1 + TOK // 2), (512 + LAT - TOK // 2, LAT, TOK, LAT + 3)]

        def keep_c(c):
            def evac(eng, ps, m, step):
                return nc.scalar.activation(token_pair(y[:, 4 * c + m, 0:TOK]), bank_pair(ps), ACT.Copy)
            return evac

        def times_c(c):
            def evac(eng, ps, m, step):
                for at, t0, t1, p0 in parts:
                    last = nc.vector.tensor_tensor(u[:, 4 * c + m, p0:p0 + t1 - t0], ps[:, at:at + t1 - t0], y[:, 4 * c + m, t0:t1], ALU.mult)
                return last
            return evac

        def times_b(c):
            def evac(eng, ps, m, step):
                t = 4 * c + m
                for at, t0, t1, p0 in parts:
                    last = nc.vector.tensor_tensor(y[:, t, p0:p0 + t1 - t0], ps[:, at:at + t1 - t0], y[:, t, p0:p0 + t1 - t0], ALU.mult)
                step(last)
                pads = ((0, LAT, 1), (LAT, TOK, LAT + 3))
                for t0, t1, p0 in pads:
                    last = nc.vector.tensor_copy(out_split[0][:, t, t0:t1], y[:, t, p0:p0 + t1 - t0])
                step(last)
                for t0, t1, p0 in pads:
                    last = low_part(nc, out_split[1][:, t, t0:t1], y[:, t, p0:p0 + t1 - t0], out_split[0][:, t, t0:t1])
                return last
            return evac

        projections(nc, "convu", [Job(w_in(T, l, ZC + c), h_split, True, "scalar", keep_c(c)) for c in range(2)]
                    + [Job(w_in(T, l, ZX + c), h_split, True, "vector", times_c(c)) for c in range(2)], ring)
        with stage(nc, "conv_in", "conv_pad", "conv_dve") as (block, (w_loaded, pads, dve_steps)):
            @block.sync
            def _(sp):
                sp.dma_start(cw[:], T["conv"][bass.ds(l, 1)].rearrange("a p k n -> (a p) k n")).then_inc(w_loaded, 16)

            @block.gpsimd
            def _(pool):
                nc.gpsimd.memset(u[:, :, 0:1], 0.0).then_inc(pads, 1)
                nc.gpsimd.memset(u[:, :, LAT + 1:LAT + 3], 0.0).then_inc(pads, 1)
                nc.gpsimd.memset(u[:, :, PAD - 1:PAD], 0.0).then_inc(pads, 1)

            @block.vector
            def _(dve):
                step = Steps(dve, dve_steps)
                dve.wait_ge(w_loaded, 16)
                dve.wait_ge(pads, 3)
                n = PAD - 2
                for k in range(KT):
                    step(nc.vector.tensor_scalar(y[:, k, 1:1 + n], u[:, k, 0:n], cw[:, k, 0:1], cw[:, k, 3:4], ALU.mult, ALU.add))
                    step(nc.vector.scalar_tensor_tensor(y[:, k, 1:1 + n], u[:, k, 1:1 + n], cw[:, k, 1:2], y[:, k, 1:1 + n], ALU.mult, ALU.add))
                    step(nc.vector.scalar_tensor_tensor(y[:, k, 1:1 + n], u[:, k, 2:2 + n], cw[:, k, 2:3], y[:, k, 1:1 + n], ALU.mult, ALU.add))
        projections(nc, "convb", [Job(w_in(T, l, ZB + c), h_split, True, "vector", times_b(c)) for c in range(2)], ring)


def attention(nc, l, T, h_split, o_tok, ring, ident):
    with ExitStack() as ctx:
        def sb(name, shape):
            return ctx.enter_context(nc.sbuf_tensor(name, shape, F32))
        q_t, k_t = sb("att_q", [P, HEADS, TOK]), sb("att_k", [P, HEADS, TOK])
        v_tok = sb("att_v", [P, NB, D])

        def channel(dst, c):
            def evac(eng, ps, m, step):
                return nc.scalar.activation(token_pair(dst[:, 4 * c + m, :]), bank_pair(ps), ACT.Copy)
            return evac

        def token(dst, c):
            def evac(eng, ps, m, step, half):
                return nc.vector.tensor_copy(dst[:, m, half_cols(c, half)], ps[:, 0:HALF])
            return evac

        projections(nc, "qkv",
                    [Job(w_in(T, l, ZQ + c), h_split, True, "scalar", channel(q_t, c)) for c in range(2)]
                    + [Job(w_in(T, l, ZK + c), h_split, True, "scalar", channel(k_t, c)) for c in range(2)]
                    + [Job(w_in(T, l, ZV + c), h_split, False, "vector", token(v_tok, c)) for c in range(2)], ring)
        attention_core(nc, l, T, q_t, k_t, v_tok, o_tok, ring, ident)


def attention_core(nc, l, T, q_t, k_t, v_tok, o_tok, ring, ident):
    UNITS = NB
    KEYS = LAT + CTX
    with ExitStack() as ctx:
        def sb(name, shape):
            return ctx.enter_context(nc.sbuf_tensor(name, shape, F32))
        room = ring[0][:].rearrange("p k n -> p (k n)")
        k_new, v_old, old = room[:, 0:D], room[:, D:2 * D], room[:, 2 * D:3 * D]
        cos, sin = room[:, 3 * D:3 * D + LAT], room[:, 3 * D + LAT:3 * D + 2 * LAT]
        kc = old.rearrange("p (h j) -> p h j", h=HEADS)
        rot = sb("att_rot", [P, P])
        lam_in, lam_pr = sb("att_lam_in", [P, 4, QK]), sb("att_lam_pr", [P, 2, QK])
        lam = sb("att_lam", [P, 4])
        neg_lam, lam0 = sb("att_neg_lam", [P, 1]), sb("att_lam0", [P, DEPTH])
        qs, ks = [sb(f"att_qs{j}", [P, TOK]) for j in range(2)], [sb(f"att_ks{j}", [P, KEYS + CTX]) for j in range(2)]
        rotated = [sb(f"att_rotated{n}", [P, LAT]) for n in range(2)]
        prob = [sb(f"att_p{i}", [P, 2, KEYS]) for i in range(2)]
        prob_t = sb("att_pt", [P, KEYS])
        mx, rs, ri = sb("att_mx", [P, 2, 2]), sb("att_rs", [P, 2, 2]), sb("att_ri", [P, 2, 2])
        ps_rot = ctx.enter_context(nc.psum_tensor("att_ps_rot", [P, LAT], F32))
        ps_s = ctx.enter_context(nc.psum_tensor("att_ps_s", [P, 2, 1024], F32))
        ps_t = ctx.enter_context(nc.psum_tensor("att_ps_t", [P, 1024], F32))
        ps_o = ctx.enter_context(nc.psum_tensor("att_ps_o", [P, 512], F32))
        with stage(nc, "ac_in", "ac_lam", "ac_lexp", "ac_rot", "ac_rotused", "ac_rope", "ac_staged", "ac_score", "ac_nmax",
                   "ac_exp", "ac_mixed", "ac_tp", "ac_ptc", "ac_pv", "ac_out", "ac_dve", "ac_knt", "ac_kout") as (block, sems):
            (loaded, lam_sum, lam_exp, rot_done, rot_used, rope_steps, staged, scored, maxed, exped, mixed, transposed,
             pt_ready, pv_done, o_out, dve_steps, kn_done, k_out) = sems

            @block.sync
            def _(sp):
                one = bass.ds(l, 1)
                for dst, src in ((kc, T["kc"][one].rearrange("a p h j -> (a p) h j")), (v_old, T["vc"][one].rearrange("a p n -> (a p) n")),
                                 (cos, T["cos"]), (sin, T["sin"]), (rot[:], T["rot"]), (lam0[:], T["lam0"]),
                                 (lam_in[:], T["lam"][one].rearrange("a x d -> a (x d)").to_broadcast([P, 4 * QK]).rearrange("p (x d) -> p x d", x=4))):
                    sp.dma_start(dst, src).then_inc(loaded, 16)
                sp.dma_start(T["new_v"][one].rearrange("a p n -> (a p) n"), v_tok[:, NB - 1, :]).then_inc(k_out, 16)
                sp.wait_ge(kn_done, HEADS)
                sp.dma_start(T["new_k"][one].rearrange("a p n -> (a p) n"), k_new).then_inc(k_out, 16)
                sp.wait_ge(k_out, 32)

            def keys_of(u):
                return (0, KEYS) if u < UNITS - 1 else (KEYS, KEYS + CTX)

            def following(i, j, u):
                return (i, j, u + 1) if u + 1 < UNITS else (i + j, 1 - j, 0)

            def over_heads(eng, body):
                with eng.Fori(0, HEADS // 2 - 1) as i:
                    body(i, 0, True)
                    body(i, 1, True)
                body(HEADS // 2 - 1, 0, True)
                body(HEADS // 2 - 1, 1, False)

            @block.tensor
            def _(pe):
                def rotate(g, n):
                    pe.wait_ge(rot_used, 2 * g + n + 1)
                    nc.tensor.matmul(ps_rot[:], rot[:], (q_t, k_t)[n][:, bass.ds(g, 1), 0:LAT].rearrange("p a t -> p (a t)"),
                                     start=True, stop=True).then_inc(rot_done, 1)

                def scores(i, j, u):
                    h = 2 * i + j
                    n = UNITS * h + u
                    k0, k1 = keys_of(u)
                    if u == 0:
                        pe.wait_ge(staged, h + 1)
                    for m in range(2):
                        pe.wait_ge(exped, 2 * n + m + 1)
                        rows = slice(QK * m, QK * m + QK)
                        for c0 in range(k0, k1, LAT):
                            c1 = min(c0 + LAT, k1)
                            last = nc.tensor.matmul(ps_s[:, m, c0 - k0:c1 - k0], qs[j][rows, u * P:(u + 1) * P],
                                                    ks[j][rows, c0:c1], start=True, stop=True)
                        last.then_inc(scored, 1)

                def body(i, j, more):
                    h = 2 * i + j
                    for u in range(UNITS):
                        n = UNITS * h + u
                        k0, k1 = keys_of(u)
                        if more or u + 1 < UNITS:
                            scores(*following(i, j, u))
                        if more and u < 2:
                            rotate(h + 1, u)
                        pe.wait_ge(mixed, n + 1)
                        pe.wait_ge(pt_ready, n + 1)
                        for kb in range((k1 - k0) // P):
                            last = nc.tensor.transpose(ps_t[:, kb * P:(kb + 1) * P], prob[(j + u) % 2][:, 0, kb * P:(kb + 1) * P], ident[:])
                        last.then_inc(transposed, 1)
                        pe.wait_ge(pt_ready, n + 2)
                        pe.wait_ge(o_out, n + 1)
                        if u == 0:
                            nc.tensor.transpose(ps_o[:, P:2 * P], ks[j][:, KEYS:KEYS + CTX], ident[:])
                        blocks = [0, 1, 2, 3, NB] if u < UNITS - 1 else [NB - 1]
                        for b, vb in enumerate(blocks):
                            values = v_old[:, bass.ds(h * P, P)] if vb == NB else v_tok[:, vb, bass.ds(h * P, P)]
                            last = nc.tensor.matmul(ps_o[:, 0:P], prob_t[:, b * P:(b + 1) * P], values,
                                                    start=b == 0, stop=b == len(blocks) - 1)
                        last.then_inc(pv_done, 1)

                pe.sem_inc(pv_done, 2 * UNITS)
                pe.wait_ge(loaded, 16 * 7)
                rotate(0, 0)
                rotate(0, 1)
                scores(0, 0, 0)
                over_heads(pe, body)

            @block.gpsimd
            def _(pool):
                pool.wait_ge(loaded, 16 * 7)
                with pool.Fori(0, HEADS // 2) as i:
                    for j in range(2):
                        g = 2 * i + j
                        head = bass.ds(g, 1)

                        def flat(ap):
                            return ap.rearrange("p a t -> p (a t)")
                        step = Steps(pool, rope_steps, 6 * g)
                        pool.wait_ge(pv_done, UNITS * g + UNITS)
                        for n, (src, dst) in enumerate(((q_t, qs[j]), (k_t, ks[j]))):
                            step(nc.gpsimd.tensor_tensor(dst[:, 0:LAT], flat(src[:, head, 0:LAT]), cos, ALU.mult))
                            pool.wait_ge(rot_used, 2 * g + n + 2)
                            step(nc.gpsimd.tensor_tensor(dst[:, 0:LAT], dst[:, 0:LAT], rotated[n][:], ALU.add))
                        step(nc.gpsimd.tensor_copy(qs[j][:, LAT:TOK], flat(q_t[:, head, LAT:TOK])))
                        step(nc.gpsimd.tensor_copy(ks[j][:, KEYS:KEYS + CTX], flat(k_t[:, head, LAT:TOK])))
                        nc.gpsimd.tensor_copy(ks[j][:, LAT:KEYS], flat(kc[:, head, :])).then_inc(staged, 1)
                        assert step.n == 6, step.n

            @block.scalar
            def _(act):
                def exps(i, j, u):
                    n = UNITS * (2 * i + j) + u
                    k0, k1 = keys_of(u)
                    slot = (j + u) % 2
                    for m in range(2):
                        act.wait_ge(maxed, 2 * n + m + 1)
                        act.activation(prob[slot][:, m, 0:k1 - k0], ps_s[:, m, 0:k1 - k0], ACT.Exp,
                                       bias=mx[:, slot, m:m + 1], scale=SCALE,
                                       accum_out=rs[:, slot, m:m + 1]).then_inc(exped, 1)

                def body(i, j, more):
                    for u in range(UNITS):
                        k0, k1 = keys_of(u)
                        act.wait_ge(transposed, UNITS * (2 * i + j) + u + 1)
                        act.activation(prob_t[:, 0:k1 - k0], ps_t[:, 0:k1 - k0], ACT.Copy).then_inc(pt_ready, 1)
                        if more or u + 1 < UNITS:
                            exps(*following(i, j, u))

                act.sem_inc(exped, 2)
                act.sem_inc(pt_ready, 1)
                act.wait_ge(lam_sum, 1)
                act.activation(lam[:, 2:4], lam[:, 0:2], ACT.Exp).then_inc(lam_exp, 1)
                exps(0, 0, 0)
                over_heads(act, body)

            @block.vector
            def _(dve):
                dve.sem_inc(o_out, 1)
                dve.sem_inc(rot_used, 1)
                dve.wait_ge(loaded, 16 * 7)
                first = Steps(dve, dve_steps)
                first(nc.vector.tensor_tensor(lam_pr[:], lam_in[:, 0:4:2, :], lam_in[:, 1:4:2, :], ALU.mult))
                nc.vector.tensor_reduce(lam[:, 0:2], lam_pr[:], AX.X, ALU.add).then_inc(lam_sum, 1)
                dve.wait_ge(lam_exp, 1)
                first(nc.vector.tensor_tensor(neg_lam[:], lam[:, 3:4], lam[:, 2:3], ALU.subtract))
                first(nc.vector.tensor_tensor(neg_lam[:], neg_lam[:], lam0[:, bass.ds(l, 1)], ALU.subtract))

                def times_sine(g, n):
                    dve.wait_ge(rot_done, 2 * g + n + 1)
                    nc.vector.tensor_tensor(rotated[n][:], ps_rot[:], sin, ALU.mult).then_inc(rot_used, 1)

                def maxima(step, i, j, u):
                    k0, k1 = keys_of(u)
                    for m in range(2):
                        top = mx[:, (j + u) % 2, m:m + 1]
                        dve.wait_ge(scored, 2 * (UNITS * (2 * i + j) + u) + m + 1)
                        step(nc.vector.tensor_reduce(top, ps_s[:, m, 0:k1 - k0], AX.X, ALU.max))
                        nc.vector.tensor_scalar(top, top, -SCALE, None, ALU.mult).then_inc(maxed, 1)

                def body(i, j, more):
                    h = 2 * i + j
                    step = Steps(dve, dve_steps, STEPS_OF_HEAD * h + first.n)
                    for u in range(UNITS):
                        n = UNITS * h + u
                        k0, k1 = keys_of(u)
                        w, slot = k1 - k0, (j + u) % 2
                        pr, inv = prob[slot], ri[:, slot, :]
                        dve.wait_ge(exped, 2 * n + 4)
                        step(nc.vector.reciprocal(inv, rs[:, slot, :]))
                        step(nc.vector.tensor_scalar(inv[:, 1:2], inv[:, 1:2], neg_lam[:], None, ALU.mult))
                        step(nc.vector.tensor_scalar(pr[:, 1, 0:w], pr[:, 1, 0:w], inv[:, 1:2], None, ALU.mult))
                        nc.vector.scalar_tensor_tensor(pr[:, 0, 0:w], pr[:, 0, 0:w], inv[:, 0:1], pr[:, 1, 0:w], ALU.mult, ALU.add).then_inc(mixed, 1)
                        if more or u + 1 < UNITS:
                            maxima(step, *following(i, j, u))
                        if more and u < 2:
                            times_sine(h + 1, u)
                        dve.wait_ge(pv_done, n + 1 + 2 * UNITS)
                        if u == 0:
                            nc.vector.tensor_copy(k_new[:, bass.ds(h * P, P)], ps_o[:, P:2 * P]).then_inc(kn_done, 1)
                        nc.vector.tensor_copy(o_tok[:, u, bass.ds(h * P, P)], ps_o[:, 0:P]).then_inc(o_out, 1)
                    assert not more or step.n == STEPS_OF_HEAD, step.n

                STEPS_OF_HEAD = 5 * UNITS
                times_sine(0, 0)
                times_sine(0, 1)
                maxima(first, 0, 0, 0)
                over_heads(dve, body)


def normalise(nc, name, o_tok, weight, factor):
    with ExitStack() as ctx:
        def sb(n, shape):
            return ctx.enter_context(nc.sbuf_tensor(f"{name}_{n}", shape, F32))
        sq, w, fac = sb("sq", [P, D]), sb("w", [P, P]), sb("fac", [P, 1])
        ms, rstd = sb("ms", [P, NB * HEADS]), sb("rstd", [P, NB * HEADS])
        with stage(nc, f"{name}_in", f"{name}_dve", f"{name}_ms", f"{name}_rt") as (block, (loaded, dve_steps, ms_done, root_done)):
            @block.sync
            def _(sp):
                sp.dma_start(w[:], weight.to_broadcast([P, P])).then_inc(loaded, 16)
                if factor is not None:
                    sp.dma_start(fac[:], factor).then_inc(loaded, 16)

            @block.scalar
            def _(act):
                act.wait_ge(ms_done, 1)
                act.activation(rstd[:], ms[:], ACT.Sqrt).then_inc(root_done, 1)

            @block.vector
            def _(dve):
                step = Steps(dve, dve_steps)
                for b in range(NB):
                    step(nc.vector.tensor_tensor(sq[:], o_tok[:, b, :], o_tok[:, b, :], ALU.mult))
                    step(nc.vector.tensor_reduce(ms[:, b * HEADS:(b + 1) * HEADS], sq[:].rearrange("p (h v) -> p h v", h=HEADS), AX.X, ALU.add))
                nc.vector.tensor_scalar(ms[:], ms[:], 1.0 / P, EPS, ALU.mult, ALU.add).then_inc(ms_done, 1)
                dve.wait_ge(root_done, 1)
                step(nc.vector.reciprocal(rstd[:], rstd[:]))
                dve.wait_ge(loaded, 16 if factor is None else 32)
                if factor is not None:
                    step(nc.vector.tensor_scalar(w[:], w[:], fac[:], None, ALU.mult))
                for b in range(NB):
                    o = o_tok[:, b, :].rearrange("p (h v) -> p h v", h=HEADS)
                    step(nc.vector.tensor_tensor(o, o, rstd[:, b * HEADS:(b + 1) * HEADS].unsqueeze(2).to_broadcast([P, HEADS, P]), ALU.mult))
                    step(nc.vector.tensor_tensor(o, o, w[:].unsqueeze(1).to_broadcast([P, HEADS, P]), ALU.mult))


def to_channel_major(nc, name, src_tok, dst_split, ident):
    high, low = dst_split
    with ExitStack() as ctx:
        psum = [ctx.enter_context(nc.psum_tensor(f"{name}_ps{i}", [P, D], F32)) for i in range(2)]
        with stage(nc, f"{name}_tp", f"{name}_high", f"{name}_low") as (block, (transposed, high_done, low_done)):
            @block.tensor
            def _(pe):
                for b in range(NB):
                    if b >= 2:
                        pe.wait_ge(low_done, b - 1)
                    for k in range(KT):
                        last = nc.tensor.transpose(psum[b % 2][:, k * P:(k + 1) * P], src_tok[:, b, k * P:(k + 1) * P], ident[:])
                    last.then_inc(transposed, 1)

            @block.scalar
            def _(act):
                for b in range(NB):
                    act.wait_ge(transposed, b + 1)
                    act.activation(high[:, :, b * P:(b + 1) * P], psum[b % 2][:].rearrange("p (k t) -> p k t", k=KT),
                                   ACT.Copy).then_inc(high_done, 1)

            @block.vector
            def _(dve):
                for b in range(NB):
                    cols = slice(b * P, (b + 1) * P)
                    dve.wait_ge(high_done, b + 1)
                    low_part(nc, low[:, :, cols], psum[b % 2][:].rearrange("p (k t) -> p k t", k=KT), high[:, :, cols]).then_inc(low_done, 1)


def split_activation(nc, name, src_t, dst_split):
    high, low = dst_split
    with stage(nc, f"{name}_high", f"{name}_low") as (block, (high_done, low_done)):
        @block.scalar
        def _(act):
            for k in range(KT):
                act.activation(high[:, k, :], src_t[:, k, :], ACT.Copy).then_inc(high_done, 1)

        @block.vector
        def _(dve):
            for k in range(KT):
                dve.wait_ge(high_done, k + 1)
                low_part(nc, low[:, k, :], src_t[:, k, :], high[:, k, :]).then_inc(low_done, 1)


def recurrent_branch(nc, l, T, h_split, q_t, o_tok, ring, ident):
    with ExitStack() as ctx:
        i_tok = ctx.enter_context(nc.sbuf_tensor("rec_i", [P, NB, D], F32))

        def channel(c):
            def evac(eng, ps, m, step):
                return nc.scalar.activation(token_pair(q_t[:, 4 * c + m, :]), bank_pair(ps), ACT.Silu)
            return evac

        def token(c):
            def evac(eng, ps, m, step, half):
                return nc.vector.tensor_copy(i_tok[:, m, half_cols(c, half)], ps[:, 0:HALF])
            return evac

        projections(nc, "rqi", [Job(w_in(T, l, RQ + c), h_split, True, "scalar", channel(c)) for c in range(2)]
                    + [Job(w_in(T, l, RI + c), h_split, False, "vector", token(c)) for c in range(2)], ring)
        with ExitStack() as inner:
            kk = inner.enter_context(nc.sbuf_tensor("rec_k", [P, NB, D], F32))
            for d, first in enumerate((RFF, RFB)):
                def sig(c):
                    def evac(eng, ps, m, step, half):
                        return nc.scalar.activation(kk[:, m, half_cols(c, half)], ps[:, 0:HALF], ACT.Sigmoid)
                    return evac
                projections(nc, f"rf{d}", [Job(w_in(T, l, first + c), h_split, False, "scalar", sig(c)) for c in range(2)], ring)
                with nc.sbuf_tensor(f"rec_lf{d}", [P, NB, D], F32) as lf:
                    forget_gates(nc, l, T, d, kk, lf, ring)
                    scan(nc, l, T, d, q_t, i_tok, kk, lf, o_tok, ring, ident)
        normalise(nc, f"recn", o_tok, T["rec_norm"][bass.ds(l, 1), :], None)
        gate = i_tok

        def gated(c):
            def evac(eng, ps, m, step, half):
                return nc.scalar.activation(gate[:, m, half_cols(c, half)], ps[:, 0:HALF], ACT.Silu)
            return evac
        projections(nc, "rg", [Job(w_in(T, l, RG + c), h_split, False, "scalar", gated(c)) for c in range(2)], ring)
        with stage(nc, "rg_mul") as (block, (multiplied,)):
            @block.vector
            def _(dve):
                for b in range(NB):
                    nc.vector.tensor_tensor(o_tok[:, b, :], o_tok[:, b, :], gate[:, b, :], ALU.mult).then_inc(multiplied, 1)


def forget_gates(nc, l, T, d, kk, lf, ring):
    r = ring[0][:].rearrange("p k n -> p (k n)").rearrange("p (a n) -> p a n", a=4)
    with ExitStack() as ctx:
        sel = ctx.enter_context(nc.sbuf_tensor(f"fg{d}_sel", [P, DEPTH], F32))
        with stage(nc, "fg_in", "fg_dve", "fg_cent", "fg_exp", "fg_f", "fg_ln") as (block, (loaded, dve_steps, centred, exped, f_ready, ln_done)):
            @block.sync
            def _(sp):
                sp.dma_start(sel[:], T["sel"]).then_inc(loaded, 16)
                for j in range(DEPTH):
                    sp.dma_start(r[:, j, :], T["rec_lb"][j, d:d + 1, :].to_broadcast([P, D])).then_inc(loaded, 16)

            @block.scalar
            def _(act):
                act.wait_ge(centred, 1)
                act.activation(r[:, 0:2, :], r[:, 0:2, :], ACT.Exp).then_inc(exped, 1)
                for b in range(NB):
                    act.wait_ge(f_ready, b + 1)
                    act.activation(lf[:, b, :], lf[:, b, :], ACT.Ln).then_inc(ln_done, 1)

            @block.vector
            def _(dve):
                step = Steps(dve, dve_steps)
                dve.wait_ge(loaded, 16 * 3)
                step(nc.vector.tensor_tensor(r[:, 2, :], r[:, 0, :], r[:, 1, :], ALU.max))
                nc.vector.tensor_tensor(r[:, 0:2, :], r[:, 0:2, :], r[:, 2:3, :].to_broadcast([P, 2, D]), ALU.subtract).then_inc(centred, 1)
                dve.wait_ge(exped, 1)
                step(nc.vector.tensor_tensor(r[:, 2, :], r[:, 0, :], r[:, 1, :], ALU.add))
                step(nc.vector.reciprocal(r[:, 2, :], r[:, 2, :]))
                step(nc.vector.tensor_tensor(r[:, 1, :], r[:, 1, :], r[:, 2, :], ALU.mult))
                step(nc.vector.tensor_scalar(r[:, 1, :], r[:, 1, :], sel[:, bass.ds(l, 1)], None, ALU.mult))
                step(nc.vector.tensor_scalar(r[:, 0, :], r[:, 1, :], -1.0, 1.0, ALU.mult, ALU.add))
                for b in range(NB):
                    step(nc.vector.tensor_tensor(lf[:, b, :], kk[:, b, :], r[:, 0, :], ALU.mult))
                    step(nc.vector.tensor_tensor(lf[:, b, :], lf[:, b, :], r[:, 1, :], ALU.add))
                    step(nc.vector.tensor_scalar(kk[:, b, :], lf[:, b, :], -1.0, 1.0, ALU.mult, ALU.add))
                    nc.vector.tensor_scalar(lf[:, b, :], lf[:, b, :], TINY, None, ALU.max).then_inc(f_ready, 1)


def scan(nc, l, T, d, q_t, i_tok, kk, lf, o_tok, ring, ident):
    units = NB * HEADS
    edge = P - 1 if d == 0 else 0
    with ExitStack() as ctx:
        def sb(name, shape):
            return ctx.enter_context(nc.sbuf_tensor(f"scan{d}_{name}", shape, F32))
        levels, suffix, mask = sb("levels", [P, LEVELS + 1, P]), sb("suffix", [P, P]), sb("mask", [P, LEVELS + 1, P])
        state = sb("state", [P, 2, D])
        room = [r[:].rearrange("p k n -> p (k n)") for r in ring]

        def carve(j, at, n):
            return room[j][:, at * P:(at + n) * P]
        expd = [carve(j, 0, 8) for j in range(2)]
        xq = [carve(j, 8, 8) for j in range(2)]
        xk = [carve(j, 16, 7) for j in range(2)]
        k_tr = [carve(j, 23, 1) for j in range(2)]
        masked_w = [carve(j, 24, 8) for j in range(2)]
        lfs = [sb(f"lfs{j}", [P, P]) for j in range(2)]
        ks = [sb(f"ks{j}", [P, P]) for j in range(2)]
        rest = [sb(f"rest{j}", [P, P]) for j in range(2)]
        k_dec = [sb(f"kdec{j}", [P, P]) for j in range(2)]
        weights = [sb(f"w{j}", [P, P]) for j in range(2)]
        ps_d = ctx.enter_context(nc.psum_tensor(f"scan{d}_ps_d", [P, 1024], F32))
        ps_r = ctx.enter_context(nc.psum_tensor(f"scan{d}_ps_r", [P, 512], F32))
        ps_a = ctx.enter_context(nc.psum_tensor(f"scan{d}_ps_a", [P, 1024], F32))
        ps_o = ctx.enter_context(nc.psum_tensor(f"scan{d}_ps_o", [P, 512], F32))
        ps_s = ctx.enter_context(nc.psum_tensor(f"scan{d}_ps_s", [P, 512], F32))

        def where(i, j):
            b = i // 4 if d == 0 else NB - 1 - i // 4
            return b, b // (NB - 1), (i % 4) * 2 + j

        def blk(t, b, h):
            return t[:, bass.ds(b, 1), bass.ds(h * P, P)].rearrange("p a n -> p (a n)")

        def over_units(eng, body):
            with eng.Fori(0, units // 2 - 1) as i:
                body(i, 0, True)
                body(i, 1, True)
            body(units // 2 - 1, 0, False)
            body(units // 2 - 1, 1, False)

        with stage(nc, "sc_in", "sc_copied", "sc_s1", "sc_exped", "sc_xk", "sc_xq", "sc_a", "sc_masked",
                   "sc_as", "sc_o", "sc_unit", "sc_out") as (block, sems):
            loaded, staged, spans, exped, xk_done, xq_done, a_done, masked, w_done, o_done, unit_done, s_out = sems

            @block.sync
            def _(sp):
                one = bass.ds(l, 1)
                sp.dma_start(levels[:], T["levels"][d]).then_inc(loaded, 16)
                sp.dma_start(suffix[:], T["suffix"][d]).then_inc(loaded, 16)
                sp.dma_start(mask[:], T["mask"][d]).then_inc(loaded, 16)
                sp.dma_start(state[:, 0, :], T["state"][one, d].rearrange("a p n -> (a p) n")).then_inc(loaded, 16)
                sp.wait_ge(unit_done, 2 + units)
                sp.dma_start(T["new_state"][one, d].rearrange("a p n -> (a p) n"), state[:, 1, :]).then_inc(s_out, 16)
                sp.wait_ge(s_out, 16)

            @block.gpsimd
            def _(pool):
                nc.gpsimd.memset(state[:, 1, :], 0.0).then_inc(staged, 1)

                def stage_in(i, j):
                    b, _, h = where(i, j)
                    pool.wait_ge(spans, 2 * i + j + 1)
                    nc.gpsimd.tensor_copy(lfs[j][:], blk(lf, b, h)).then_inc(staged, 1)
                    nc.gpsimd.tensor_copy(ks[j][:], blk(kk, b, h)).then_inc(staged, 1)

                def body(i, j, more):
                    b, _, h = where(i, j)
                    pool.wait_ge(exped, 6 * i + 3 * j + 4)
                    pool.wait_ge(unit_done, 2 * i + j + 1)
                    q = q_t[:, bass.ds(h, 1), bass.ds(b * P, P)].to_broadcast([P, LEVELS + 1, P])
                    nc.gpsimd.tensor_tensor(xq[j].rearrange("p (a t) -> p a t", t=P), expd[j].rearrange("p (a t) -> p a t", t=P),
                                            q, ALU.mult).then_inc(xq_done, 1)
                    if more:
                        stage_in(i + 1, j)
                stage_in(0, 0)
                stage_in(0, 1)
                over_units(pool, body)

            @block.tensor
            def _(pe):
                def span_sums(i, j):
                    pe.wait_ge(staged, 4 * i + 2 * j + 3)
                    pe.wait_ge(exped, 6 * i + 3 * j + 1)
                    for c in range(2):
                        nc.tensor.matmul(ps_d[:, c * 512:(c + 1) * 512], lfs[j][:],
                                         levels[:, 4 * c:4 * c + 4, :].rearrange("p a t -> p (a t)"), start=True, stop=True)
                    nc.tensor.matmul(ps_r[:, 0:P], suffix[:], lfs[j][:], start=True, stop=True)
                    nc.tensor.transpose(ps_r[:, P:2 * P], ks[j][:], ident[:]).then_inc(spans, 1)

                def body(i, j, more):
                    b, req, h = where(i, j)
                    pe.wait_ge(xk_done, 4 * i + 2 * j + 1)
                    pe.wait_ge(xq_done, 2 * i + j + 1)
                    pe.wait_ge(w_done, 2 * i + j + 1)
                    for a in range(LEVELS):
                        nc.tensor.matmul(ps_a[:, a * P:(a + 1) * P], xk[j][:, a * P:(a + 1) * P], xq[j][:, a * P:(a + 1) * P],
                                         start=True, stop=True)
                    nc.tensor.matmul(ps_a[:, LEVELS * P:], k_tr[j],
                                     q_t[:, bass.ds(h, 1), bass.ds(b * P, P)].rearrange("p a t -> p (a t)"),
                                     start=True, stop=True).then_inc(a_done, 1)
                    if more:
                        span_sums(i + 1, j)
                    pe.wait_ge(w_done, 2 * i + j + 2)
                    pe.wait_ge(xk_done, 4 * i + 2 * j + 2)
                    pe.wait_ge(unit_done, 2 * i + j + 2)
                    nc.tensor.matmul(ps_o[:, 0:P], weights[j][:], blk(i_tok, b, h), start=True, stop=False)
                    nc.tensor.matmul(ps_o[:, 0:P], xq[j][:, LEVELS * P:], blk(state, req, h), start=False, stop=True)
                    nc.tensor.matmul(ps_s[:, 0:P], k_dec[j][:], blk(i_tok, b, h), start=True, stop=True).then_inc(o_done, 1)

                pe.sem_inc(spans, 2)
                pe.wait_ge(loaded, 64)
                span_sums(0, 0)
                span_sums(0, 1)
                over_units(pe, body)

            @block.scalar
            def _(act):
                act.sem_inc(exped, 1)

                def body(i, j, more):
                    act.wait_ge(spans, 2 * i + j + 3)
                    act.wait_ge(unit_done, 2 * i + j + 1)
                    act.activation(expd[j], ps_d[:], ACT.Exp).then_inc(exped, 1)
                    act.activation(rest[j][:], ps_r[:, 0:P], ACT.Exp).then_inc(exped, 1)
                    act.activation(k_tr[j], ps_r[:, P:2 * P], ACT.Copy).then_inc(exped, 1)
                over_units(act, body)

            @block.vector
            def _(dve):
                def keys(i, j):
                    b, _, h = where(i, j)
                    dve.wait_ge(exped, 6 * i + 3 * j + 4)
                    nc.vector.tensor_tensor(xk[j].rearrange("p (a t) -> p a t", t=P), expd[j][:, 0:LEVELS * P].rearrange("p (a t) -> p a t", t=P),
                                            k_tr[j].unsqueeze(1).to_broadcast([P, LEVELS, P]), ALU.mult).then_inc(xk_done, 1)
                    nc.vector.tensor_tensor(k_dec[j][:], blk(kk, b, h), rest[j][:], ALU.mult).then_inc(xk_done, 1)

                def body(i, j, more):
                    b, req, h = where(i, j)
                    dve.wait_ge(a_done, 2 * i + j + 1)
                    nc.vector.tensor_tensor(masked_w[j], ps_a[:], mask[:].rearrange("p a t -> p (a t)"), ALU.mult).then_inc(masked, 1)
                    dve.wait_ge(masked, 2 * i + j + 1)
                    nc.vector.tensor_reduce(weights[j][:], masked_w[j].rearrange("p (a t) -> p t a", t=P), AX.X, ALU.add).then_inc(w_done, 1)
                    if more or j == 0:
                        keys(i + j, 1 - j)
                    dve.wait_ge(o_done, 2 * i + j + 1)
                    if d == 0:
                        nc.vector.tensor_copy(blk(o_tok, b, h), ps_o[:, 0:P])
                    else:
                        nc.vector.tensor_tensor(blk(o_tok, b, h), blk(o_tok, b, h), ps_o[:, 0:P], ALU.add)
                    nc.vector.scalar_tensor_tensor(blk(state, req, h), blk(state, req, h), expd[j][:, LEVELS * P + edge:LEVELS * P + edge + 1],
                                                   ps_s[:, 0:P], ALU.mult, ALU.add).then_inc(unit_done, 1)

                dve.sem_inc(unit_done, 2)
                dve.sem_inc(w_done, 1)
                dve.wait_ge(loaded, 64)
                dve.wait_ge(staged, 1)
                keys(0, 0)
                over_units(dve, body)


def output_projection(nc, l, T, merged_split, y_tok, ring):
    with ExitStack() as ctx:
        gate = ctx.enter_context(nc.sbuf_tensor("op_gate", [P, 2, D], F32))
        with stage(nc, "op_in") as (block, (loaded,)):
            @block.sync
            def _(sp):
                for cond in range(2):
                    sp.dma_start(gate[:, cond, :], mod_row(T, cond, 2)).then_inc(loaded, 16)
                sp.wait_ge(loaded, 32)

        def evac(c):
            def f(eng, ps, m, step, half):
                cols = half_cols(c, half)
                return nc.vector.tensor_tensor(y_tok[:, m, cols], ps[:, 0:HALF], gate[:, m // (NB - 1), cols], ALU.mult)
            return f
        projections(nc, "op", [Job(T["w_out"][bass.ds(l, 1), c].rearrange("a p k n -> (a p) k n"), merged_split, False, "vector", evac(c))
                               for c in range(2)], ring)


def residual_norm(nc, l, T, name, which, y_tok, x_tok, x_from, h_tok, gate_part, x_to):
    with ExitStack() as ctx:
        def sb(n, shape):
            return ctx.enter_context(nc.sbuf_tensor(f"{name}_{n}", shape, F32))
        gb = sb("gb", [P, 2, D])
        vec = sb("vec", [P, 2, 2, D]) if h_tok is not None else None
        scale = sb("ysc", [P, 2, D]) if gate_part is not None else None
        stats, mv, root, nbias = sb("stats", [P, NB, 12]), sb("mv", [P, NB, 2]), sb("root", [P, NB]), sb("nb", [P, NB])
        with stage(nc, f"{name}_in", f"{name}_dve", f"{name}_var", f"{name}_root", f"{name}_xd", f"{name}_out") as (
                block, (loaded, dve_steps, var_done, root_done, x_done, stored)):
            n_in = 2 + (NB if x_from is not None else 0) + (4 if h_tok is not None else 0) + (2 if gate_part is not None else 0)

            @block.sync
            def _(sp):
                one = bass.ds(l, 1)
                sp.dma_start(gb[:, 0, :], T["ln_g"][one, which, :].to_broadcast([P, D])).then_inc(loaded, 16)
                sp.dma_start(gb[:, 1, :], T["ln_b"][one, which, :].to_broadcast([P, D])).then_inc(loaded, 16)
                if x_from is not None:
                    for b in range(NB):
                        sp.dma_start(x_tok[:, b, :], x_from(b)).then_inc(loaded, 16)
                if h_tok is not None:
                    for cond in range(2):
                        for j in range(2):
                            sp.dma_start(vec[:, cond, j, :], mod_row(T, cond, 3 + j)).then_inc(loaded, 16)
                if scale is not None:
                    for cond in range(2):
                        sp.dma_start(scale[:, cond, :], mod_row(T, cond, gate_part)).then_inc(loaded, 16)
                if x_to is not None:
                    for b in range(NB):
                        sp.wait_ge(x_done, b + 1)
                        sp.dma_start(x_to(b), x_tok[:, b, :]).then_inc(stored, 16)
                    sp.wait_ge(stored, 16 * NB)

            @block.scalar
            def _(act):
                act.wait_ge(var_done, 1)
                act.activation(root[:], mv[:, :, 1], ACT.Sqrt).then_inc(root_done, 1)

            @block.vector
            def _(dve):
                step = Steps(dve, dve_steps)
                dve.wait_ge(loaded, 16 * n_in)
                if vec is not None:
                    step(nc.vector.tensor_scalar(vec[:, :, 1, :], vec[:, :, 1, :], 1.0, None, ALU.add))
                for b in range(NB):
                    if scale is not None:
                        step(nc.vector.tensor_tensor(y_tok[:, b, :], y_tok[:, b, :], scale[:, b // (NB - 1), :], ALU.mult))
                    step(nc.vector.scalar_tensor_tensor(x_tok[:, b, :], x_tok[:, b, :], ALPHA, y_tok[:, b, :], ALU.mult, ALU.add))
                    for half in range(2):
                        step(nc.vector.bn_stats(stats[:, b, 6 * half:6 * half + 6], x_tok[:, b, half * 512:(half + 1) * 512]))
                    step(nc.vector.bn_aggr(mv[:, b, :], stats[:, b, :]))
                nc.vector.tensor_scalar(mv[:, :, 1], mv[:, :, 1], EPS, None, ALU.add).then_inc(var_done, 1)
                dve.wait_ge(root_done, 1)
                step(nc.vector.reciprocal(root[:], root[:]))
                for b in range(NB):
                    x = x_tok[:, b, :]
                    step(nc.vector.tensor_scalar(x, x, mv[:, b, 0:1], root[:, b:b + 1], ALU.subtract, ALU.mult))
                    step(nc.vector.tensor_tensor(x, x, gb[:, 0, :], ALU.mult))
                    nc.vector.tensor_tensor(x, x, gb[:, 1, :], ALU.add).then_inc(x_done, 1)
                    if h_tok is not None:
                        cond = b // (NB - 1)
                        dve.wait_ge(x_done, b + 1)
                        step(nc.vector.tensor_tensor(h_tok[:, b, :], x, vec[:, cond, 1, :], ALU.mult))
                        step(nc.vector.tensor_tensor(h_tok[:, b, :], h_tok[:, b, :], vec[:, cond, 0, :], ALU.add))


def peer_queries(nc, l, T, h_split, q_t, ring):
    def evac(c):
        def f(eng, ps, m, step):
            return nc.scalar.activation(token_pair(q_t[:, 4 * c + m, :]), bank_pair(ps), ACT.Copy)
        return f
    projections(nc, "pq", [Job(T["peer_wq"][bass.ds(l, 1), c].rearrange("a p k n -> (a p) k n"), h_split, True, "scalar", evac(c))
                           for c in range(4)], ring)


def expert_scores(nc, l, T, q_t, scores):
    S = 2 * PH
    with ExitStack() as ctx:
        keys = ctx.enter_context(nc.sbuf_tensor("es_keys", [P, S, P], F32))
        psum = [ctx.enter_context(nc.psum_tensor(f"es_ps{i}", [P, S * P], F32)) for i in range(2)]
        with stage(nc, "es_in", "es_mm", "es_cp") as (block, (loaded, scored, copied)):
            @block.sync
            def _(sp):
                sp.dma_start(keys[:], T["peer_keys"][bass.ds(l, 1)].rearrange("a p s n -> (a p) s n")).then_inc(loaded, 16)

            @block.tensor
            def _(pe):
                pe.wait_ge(loaded, 16)
                for b in range(NB):
                    if b >= 2:
                        pe.wait_ge(copied, b - 1)
                    for s in range(S):
                        last = nc.tensor.matmul(psum[b % 2][:, s * P:(s + 1) * P], q_t[:, s, b * P:(b + 1) * P], keys[:, s, :],
                                                start=True, stop=True)
                    last.then_inc(scored, 1)

            @block.scalar
            def _(act):
                for b in range(NB):
                    act.wait_ge(scored, b + 1)
                    act.activation(scores[:, b, :], psum[b % 2][:], ACT.Copy).then_inc(copied, 1)


def experts(nc, l, T, h_tok, y_tok, scores, ident, u_in, v_in, ring):
    units, pairs = NB * PH, PH // 2
    with ExitStack() as ctx:
        def sb(name, shape, dt=F32):
            return ctx.enter_context(nc.sbuf_tensor(name, shape, dt))
        U_SLOTS, V_SLOTS, DIAGS = 8, TOPK, 4
        rooms = [r[:].rearrange("p k n -> p (k n)") for r in ring]
        u_row = [rooms[s // 4][:, (s % 4) * D:(s % 4 + 1) * D] for s in range(U_SLOTS)]
        v_row = [sb(f"ex_v{s}", [P, D])[:] for s in range(V_SLOTS)]
        h_now, zero = sb("ex_h", [P, D]), sb("ex_zero", [P, 512])
        idx_now = [sb(f"ex_i{j}", [P, TOPK], U32) for j in range(2)]
        dot = [sb(f"ex_dot{j}", [P, TOPK]) for j in range(2)]
        act_v = [sb(f"ex_act{j}", [P, TOPK]) for j in range(2)]
        soft = [sb(f"ex_soft{j}", [P, TOPK]) for j in range(2)]
        total = [sb(f"ex_total{j}", [P, 1]) for j in range(2)]
        wgt = [sb(f"ex_w{j}", [P, TOPK]) for j in range(2)]
        diag = [sb(f"ex_diag{i}", [P, P]) for i in range(DIAGS)]
        index, centred = sb("ex_index", [P, units * TOPK], U32), sb("ex_centred", [P, units * TOPK])
        lists, top, top_i = sb("ex_lists", [P, 2, P]), sb("ex_top", [P, 2, TOPK]), sb("ex_topi", [P, 2, TOPK], U32)
        top_f, cand = sb("ex_topf", [P, 2, TOPK]), sb("ex_cand", [P, TOPK * TOPK])
        best, pos = sb("ex_best", [P, TOPK]), sb("ex_pos", [P, TOPK], U32)
        part_u, part_f = sb("ex_partu", [P, 2, TOPK], U32), sb("ex_partf", [P, 2, TOPK])
        hit, num = sb("ex_hit", [P, 2, TOPK, TOPK]), sb("ex_num", [P, 2, TOPK])
        iota, base = sb("ex_iota", [P, TOPK]), sb("ex_base", [P, DEPTH])
        ps_y = ctx.enter_context(nc.psum_tensor("ex_ps_y", [P, D], F32))
        by_list = scores[:].rearrange("p b (s n) -> p (b s) n", n=P)
        with stage(nc, "ex_in", "ex_hnow", "ex_idx", "ex_udone", "ex_vdone", "ex_gelu", "ex_wgt", "ex_diagd", "ex_ydone", "ex_yout",
                   "ex_zeroed", "ex_going", "ex_dve", "ex_routed", "ex_recip", "ex_picking") as (block, sems):
            (loaded, h_ready, idx_ready, u_used, v_used, gelu_done, w_ready, diag_ready, y_done, y_out, zeroed, going,
             dve_steps, routed, recip_done, picking) = sems

            @block.sync
            def _(sp):
                sp.dma_start(iota[:], T["iota"]).then_inc(loaded, 16)
                sp.dma_start(base[:], T["base"]).then_inc(loaded, 16)

            @block.gpsimd
            def _(pool):
                with pool.Fori(0, NB * pairs) as i:
                    for j in range(2):
                        n = 2 * i + j
                        pool.wait_ge(routed, n + 1)
                        nc.gpsimd.tensor_copy(idx_now[j][:], index[:, bass.ds(TOPK * n, TOPK)]).then_inc(idx_ready, 1)
                        for rows, arrived, used, table, go in ((u_row, u_in, u_used, T["peer_u"], 2), (v_row, v_in, v_used, T["peer_v"], 4)):
                            for s in range(TOPK):
                                slot = s % len(rows)
                                if s % go == 0:
                                    pool.wait_ge(used, TOPK * n + s + go)
                                    if s == 0 and rows is u_row:
                                        pool.wait_ge(idx_ready, n + 1)
                                    pool.sem_inc(going, 1)
                                nc.gpsimd.indirect_dma_start(rows[slot], None, table, bass.IndirectOffsetOnAxis(
                                    ap=idx_now[j][:, s:s + 1], axis=0)).then_inc(arrived[slot], 16)

            @block.vector
            def _(dve):
                V = nc.vector

                def choose(count, unit):
                    step = Steps(dve, dve_steps, count * CHOICE_STEPS)
                    cols = bass.ds(unit * TOPK, TOPK)
                    step(V.tensor_copy(lists[:], by_list[:, bass.ds(2 * unit, 2), :]))
                    for lo in (0, 8):
                        dve.sem_inc(picking, 1)
                        for a in range(2):
                            last = V.max(top[:, a, lo:lo + 8], lists[:, a, :])
                        step(last)
                        dve.sem_inc(picking, 1)
                        for a in range(2):
                            last = V.max_index(top_i[:, a, lo:lo + 8], top[:, a, lo:lo + 8], lists[:, a, :])
                            if lo == 0:
                                last = V.match_replace(lists[:, a, :], top[:, a, 0:8], lists[:, a, :], LOWEST)
                        step(last)
                    V.tensor_copy(top_f[:], top_i[:])
                    step(V.tensor_tensor(cand[:].rearrange("p (i j) -> p i j", i=TOPK), top[:, 0, :].unsqueeze(2).to_broadcast([P, TOPK, TOPK]),
                                         top[:, 1, :].unsqueeze(1).to_broadcast([P, TOPK, TOPK]), ALU.add))
                    dve.sem_inc(picking, 1)
                    step(V.max(best[:, 0:8], cand[:]))
                    dve.sem_inc(picking, 1)
                    V.max_index(pos[:, 0:8], best[:, 0:8], cand[:])
                    step(V.match_replace(cand[:], best[:, 0:8], cand[:], LOWEST))
                    dve.sem_inc(picking, 1)
                    step(V.max(best[:, 8:16], cand[:]))
                    dve.sem_inc(picking, 1)
                    step(V.max_index(pos[:, 8:16], best[:, 8:16], cand[:]))
                    V.tensor_scalar(centred[:, cols], best[:], best[:, 0:1], None, ALU.subtract)
                    V.tensor_scalar(part_u[:, 0], pos[:], 4, None, ALU.logical_shift_right)
                    step(V.tensor_scalar(part_u[:, 1], pos[:], 15, None, ALU.bitwise_and))
                    step(V.tensor_copy(part_f[:], part_u[:]))
                    full = [P, 2, TOPK, TOPK]
                    step(V.tensor_tensor(hit[:], part_f[:].unsqueeze(3).to_broadcast(full),
                                         iota[:].unsqueeze(1).unsqueeze(1).to_broadcast(full), ALU.is_equal))
                    step(V.tensor_tensor(hit[:], hit[:], top_f[:].unsqueeze(2).to_broadcast(full), ALU.mult))
                    step(V.tensor_reduce(num[:], hit[:], AX.X, ALU.add))
                    step(V.scalar_tensor_tensor(num[:, 0], num[:, 0], float(P), num[:, 1], ALU.mult, ALU.add))
                    V.tensor_scalar(index[:, cols], num[:, 0], base[:, bass.ds(l, 1)], None, ALU.add).then_inc(routed, 1)
                    assert step.n == CHOICE_STEPS, step.n

                V.memset(zero[:], 0.0).then_inc(zeroed, 1)
                dve.sem_inc(u_used, U_SLOTS)
                dve.wait_ge(loaded, 32)
                choose(0, 0)
                choose(1, 1)
                with dve.Fori(0, NB) as b:
                    V.tensor_copy(h_now[:], h_tok[:, bass.ds(b, 1), :].rearrange("p a n -> p (a n)")).then_inc(h_ready, 1)
                    with dve.Fori(0, pairs) as i:
                        for j in range(2):
                            n = PH * b + 2 * i + j
                            dve.wait_ge(h_ready, b + 1)
                            for s in range(TOPK):
                                dve.wait_ge(u_in[s % U_SLOTS], (l * units + n) * 32 + 16 * (s // U_SLOTS + 1))
                                row = u_row[s % U_SLOTS]
                                V.tensor_tensor_reduce(out=row, in0=row, in1=h_now[:], scale=1.0, scalar=0.0, op0=ALU.mult,
                                                       op1=ALU.add, accum_out=dot[j][:, s:s + 1]).then_inc(u_used, 1)
                            dve.wait_ge(gelu_done, n + 1)
                            V.reciprocal(total[j][:], total[j][:]).then_inc(recip_done, 1)
                            dve.wait_ge(recip_done, n + 1)
                            V.scalar_tensor_tensor(wgt[j][:], act_v[j][:], total[j][:], soft[j][:], ALU.mult, ALU.mult).then_inc(w_ready, 1)
                            choose(n + 2, (n + 2) % units)

            @block.scalar
            def _(act):
                with act.Fori(0, NB) as b:
                    with act.Fori(0, pairs) as i:
                        for j in range(2):
                            n = PH * b + 2 * i + j
                            act.wait_ge(routed, n + 1)
                            act.activation(soft[j][:], centred[:, bass.ds(TOPK * n, TOPK)], ACT.Exp, accum_out=total[j][:])
                            act.wait_ge(u_used, TOPK * n + TOPK + U_SLOTS)
                            act.activation(act_v[j][:], dot[j][:], ACT.Gelu).then_inc(gelu_done, 1)
                            act.wait_ge(w_ready, n + 1)
                            for s in range(TOPK):
                                act.wait_ge(v_used, TOPK * n + s + 1 + V_SLOTS - DIAGS)
                                act.activation(diag[s % DIAGS][:], ident[:], ACT.Copy, scale=wgt[j][:, s:s + 1]).then_inc(diag_ready, 1)
                    act.wait_ge(y_done, b + 1)
                    act.activation(y_tok[:, bass.ds(b, 1), :].rearrange("p a n -> p (a n)"), ps_y[:], ACT.Copy).then_inc(y_out, 1)

            @block.tensor
            def _(pe):
                pe.sem_inc(v_used, V_SLOTS)
                pe.sem_inc(y_out, 1)
                pe.wait_ge(zeroed, 1)
                with pe.Fori(0, NB) as b:
                    pe.wait_ge(y_out, b + 1)
                    for c in (0, 512):
                        nc.tensor.matmul(ps_y[:, c:c + 512], zero[:, 0:P], zero[:], start=True, stop=False)
                    with pe.Fori(0, pairs) as i:
                        for j in range(2):
                            n = PH * b + 2 * i + j
                            for s in range(TOPK):
                                pe.wait_ge(v_in[s], (l * units + n) * 16 + 16)
                                pe.wait_ge(diag_ready, TOPK * n + s + 1)
                                for c in (0, 512):
                                    last = nc.tensor.matmul(ps_y[:, c:c + 512], diag[s % DIAGS][:], v_row[s][:, c:c + 512], start=False, stop=False)
                                last.then_inc(v_used, 1)
                    for c in (0, 512):
                        last = nc.tensor.matmul(ps_y[:, c:c + 512], zero[:, 0:P], zero[:], start=False, stop=True)
                    last.then_inc(y_done, 1)


CHOICE_STEPS = 16


def token_rows(x_rows):
    return lambda b: x_rows[b * P:(b + 1) * P, :]


def copy_rows(nc, name, pairs):
    with stage(nc, f"{name}_done") as (block, (done,)):
        @block.sync
        def _(sp):
            for dst, src in pairs:
                sp.dma_start(dst, src).then_inc(done, 16)
            sp.wait_ge(done, 16 * len(pairs))


def trunk(nc, T, depth=DEPTH, stop=None):
    with ExitStack() as ctx:
        def sb(name, shape, dt=F32):
            return ctx.enter_context(nc.sbuf_tensor(name, shape, dt))

        def split_tensor(scope, name):
            return [scope.enter_context(nc.sbuf_tensor(f"{name}_{part}", [P, KT, TOK], F32R)) for part in ("high", "low")]
        ident = sb("ident", [P, P])
        main = sb("main", [P, KT, TOK])
        y_tok = main[:].rearrange("p k t -> p (k t)").rearrange("p (b n) -> p b n", b=NB)
        ring = [sb(f"ring{i}", [P, KT, CHUNK]) for i in range(2)]
        u_in = [ctx.enter_context(nc.semaphore(f"u_in{s}")) for s in range(TOPK // 2)]
        v_in = [ctx.enter_context(nc.semaphore(f"v_in{s}")) for s in range(TOPK)]
        rows = token_rows(T["x_rows"])
        copy_rows(nc, "start", [(T["x_rows"][0:LAT, :], T["x_sample"]), (T["x_rows"][LAT:TOK, :], T["x_prompt"]), (ident[:], T["ident"])])
        with nc.Fori(0, depth) as l:
            modulation(nc, l, T, ring)
            with ExitStack() as mixer:
                h_split = split_tensor(mixer, "mixer_h")
                modulate_and_transpose(nc, T, rows, h_split, ident, 0)
                if stop == "mod": return
                with ExitStack() as branch:
                    o_tok = branch.enter_context(nc.sbuf_tensor("rec_o", [P, NB, D], F32))
                    recurrent_branch(nc, l, T, h_split, main, o_tok, ring, ident)
                    if stop == "rec": return
                    branch_split = split_tensor(branch, "rec_out")
                    to_channel_major(nc, "rect", o_tok, branch_split, ident)
                    merge_branch(nc, l, T, "mg2", 2, True, h_split, branch_split, main, ring)
                with ExitStack() as branch:
                    branch_split = split_tensor(branch, "conv_out")
                    conv_branch(nc, l, T, h_split, branch_split, ring)
                    merge_branch(nc, l, T, "mg1", 1, False, h_split, branch_split, main, ring)
                with ExitStack() as branch:
                    o_tok = branch.enter_context(nc.sbuf_tensor("att_o", [P, NB, D], F32))
                    attention(nc, l, T, h_split, o_tok, ring, ident)
                    if stop == "attcore": return
                    normalise(nc, "attn", o_tok, T["subln"][bass.ds(l, 1), :], T["lam_keep"][bass.ds(l, 1)].rearrange("a p n -> (a p) n"))
                    if stop == "att": return
                    branch_split = split_tensor(branch, "att_out")
                    to_channel_major(nc, "attt", o_tok, branch_split, ident)
                    merge_branch(nc, l, T, "mg0", 0, False, h_split, branch_split, main, ring)
            with ExitStack() as inner:
                merged_split = split_tensor(inner, "merged")
                split_activation(nc, "ms", main, merged_split)
                output_projection(nc, l, T, merged_split, y_tok, ring)
            if stop == "mix": return
            with ExitStack() as peer:
                scores = peer.enter_context(nc.sbuf_tensor("scores", [P, NB, 2 * PH * P], F32))
                with ExitStack() as inner:
                    h_split = split_tensor(inner, "peer_h")
                    with ExitStack() as norm:
                        x_tok = norm.enter_context(nc.sbuf_tensor("x_tok1", [P, NB, D], F32))
                        h_tok = norm.enter_context(nc.sbuf_tensor("h_tok1", [P, NB, D], F32))
                        residual_norm(nc, l, T, "ln1", 0, y_tok, x_tok, rows, h_tok, None, rows)
                        to_channel_major(nc, "ht", h_tok, h_split, ident)
                        copy_rows(nc, "h_out", [(T["h_rows"].rearrange("(b p) n -> p b n", p=P), h_tok[:])])
                    q_t = inner.enter_context(nc.sbuf_tensor("peer_q", [P, 2 * PH, TOK], F32))
                    peer_queries(nc, l, T, h_split, q_t, ring)
                    expert_scores(nc, l, T, q_t, scores)
                with ExitStack() as inner:
                    h_tok = inner.enter_context(nc.sbuf_tensor("h_tok2", [P, NB, D], F32))
                    copy_rows(nc, "h_in", [(h_tok[:], T["h_rows"].rearrange("(b p) n -> p b n", p=P))])
                    experts(nc, l, T, h_tok, y_tok, scores, ident, u_in, v_in, ring)
            if stop == "experts": return
            with ExitStack() as norm:
                x_tok = norm.enter_context(nc.sbuf_tensor("x_tok2", [P, NB, D], F32))
                residual_norm(nc, l, T, "ln2", 1, y_tok, x_tok, rows, None, 5, rows)
        copy_rows(nc, "end", [(T["y_sample"], T["x_rows"][0:LAT, :]), (T["y_prompt"], T["x_rows"][LAT:TOK, :])])


def constants():
    eye = np.eye(P, dtype=np.float32)
    levels = np.zeros((2, P, LEVELS + 1, P), np.float32)
    mask = np.zeros((2, P, LEVELS + 1, P), np.float32)
    s, t = np.meshgrid(np.arange(P), np.arange(P), indexing="ij")
    for a in range(LEVELS):
        half = 1 << a
        mid = (t // (2 * half)) * (2 * half) + half
        levels[0, :, a, :] = np.where(t >= mid, (s >= mid) & (s <= t), (s > t) & (s < mid))
        mask[0, :, a, :] = (s // (2 * half) == t // (2 * half)) & (s < mid) & (t >= mid)
    levels[0, :, LEVELS, :] = s <= t
    mask[0, :, LEVELS, :] = s == t
    suffix = np.stack([s > t, s < t]).astype(np.float32)
    levels[1], mask[1] = levels[0, ::-1, :, ::-1], mask[0, ::-1, :, ::-1]
    half, quarter = QK // 2, QK // 4
    freqs = (10000.0 ** (-np.arange(0, half, 2, dtype=np.float32) / np.float32(half))).astype(np.float32)
    tok = np.arange(LAT)
    cos, sin = np.zeros((P, LAT), np.float32), np.zeros((P, LAT), np.float32)
    rot = np.zeros((P, P), np.float32)
    for c in range(P):
        axis, place = (c % QK) // half, c % half
        ang = (tok // GRID_W if axis == 0 else tok % GRID_W).astype(np.float32) * freqs[place % quarter]
        cos[c], sin[c] = np.cos(ang), np.sin(ang)
        if place < quarter:
            rot[c + quarter, c] = -1.0
        else:
            rot[c - quarter, c] = 1.0
    ones = np.ones((P, 1), np.float32)
    return {
        "ident": eye, "levels": levels, "suffix": suffix, "mask": mask, "cos": cos, "sin": sin, "rot": rot,
        "lam0": ones * np.array(LAM_INIT, np.float32), "sel": ones * np.arange(DEPTH, dtype=np.float32),
        "lam_keep": np.stack([ones * np.float32(1.0 - x) for x in LAM_INIT]),
        "iota": ones * np.arange(TOPK, dtype=np.float32), "base": ones * (EXPERTS * np.arange(DEPTH, dtype=np.float32)),
    }


def layouts(a):
    def chunks(w):
        *lead, d, n = w.shape
        w = w.reshape(*lead, KT, P, n // CHUNK, CHUNK)
        r = len(lead)
        return w.transpose(*range(r), r + 2, r + 1, r, r + 3)

    conv = np.concatenate([a["conv_w"], a["conv_b"][:, None, :]], axis=1)
    return {
        "x_sample": a["x_sample"].reshape(LAT, D), "x_prompt": a["x_prompt"].reshape(CTX, D),
        "cond": np.stack([a["c"].reshape(KT, P), a["c_ctx"].reshape(KT, P)]).transpose(2, 1, 0),
        "kc": a["cache_attn_k"][0].transpose(0, 3, 2, 1), "vc": a["cache_attn_v"][0].reshape(DEPTH, CTX, D),
        "state": a["state_hgrn"][0].transpose(0, 1, 3, 2, 4).reshape(DEPTH, 2, P, D),
        "mod_w": chunks(a["mod_w"]), "mod_b": a["mod_b"], "w_in": chunks(a["w_in"]), "lam": a["attn_lambda"],
        "subln": a["attn_subln"], "conv": conv.reshape(DEPTH, 4, KT, P).transpose(0, 3, 2, 1), "rec_lb": a["rec_lb"],
        "rec_norm": a["rec_norm"], "w_branch": chunks(a["w_branch"]), "w_out": chunks(a["w_out"]), "ln_g": a["ln_g"],
        "ln_b": a["ln_b"], "peer_wq": chunks(a["peer_wq"]),
        "peer_keys": a["peer_keys"].reshape(DEPTH, 2 * PH, P, P).transpose(0, 3, 1, 2),
        "peer_u": a["peer_u"].reshape(DEPTH * EXPERTS, D), "peer_v": a["peer_v"].reshape(DEPTH * EXPERTS, D),
    }


OUTPUTS = {"y_prompt": (CTX, D), "y_sample": (LAT, D), "new_k": (DEPTH, CTX, D), "new_v": (DEPTH, CTX, D),
           "new_state": (DEPTH, 2, P, D)}
SCRATCH = {"x_rows": (TOK, D), "h_rows": (TOK, D), "mod_rows": (2, 6 * D)}


def build(nc, arrays, depth=DEPTH, stop=None):
    tensors = {n: nc.dram_tensor(f"in_{n}", a.shape, F32, kind="ExternalInput").ap() for n, a in arrays.items()}
    tensors.update({n: nc.dram_tensor(f"out_{n}", s, F32, kind="ExternalOutput").ap() for n, s in OUTPUTS.items()})
    tensors.update({n: nc.dram_tensor(n, s, F32, kind="Internal").ap() for n, s in SCRATCH.items()})
    trunk(nc, tensors, depth, stop)


def kernel(**inputs):
    import concourse.bacc as bacc
    from concourse.bass_utils import run_bass_kernel_spmd

    arrays = layouts({k: np.asarray(v) for k, v in inputs.items()})
    arrays.update(constants())
    arrays = {k: np.ascontiguousarray(v) for k, v in arrays.items()}
    nc = bacc.Bacc("TRN2", target_bir_lowering=False, num_devices=1)
    build(nc, arrays)
    got = run_bass_kernel_spmd(nc, [{f"in_{k}": a for k, a in arrays.items()}], core_ids=[0]).results[0]
    out = {n: got[f"out_{n}"] for n in OUTPUTS}
    state = out["new_state"].reshape(DEPTH, 2, P, HEADS, P).transpose(0, 1, 3, 2, 4)
    return (out["y_prompt"].reshape(1, CTX, D), out["y_sample"].reshape(1, LAT, D),
            out["new_k"].reshape(1, DEPTH, CTX, HEADS, P), out["new_v"].reshape(1, DEPTH, CTX, HEADS, P),
            np.ascontiguousarray(state)[None])
```
